# Optimizing a Trainium2 kernel written in Bass

```python
import math
import jax, jax.numpy as jnp
from jax import lax
import numpy as np

D_MODEL = 2048
BATCH = 1
SEQ = 256
DEPTH = 1

D_MIX = D_MODEL
MLSTM_WIDTH = D_MIX // 2
MLSTM_HEADS = 4
MLSTM_HEAD_DIM = MLSTM_WIDTH // MLSTM_HEADS
MLSTM_CHUNK = 128
CONV_WIDTH = 4
S5_WIDTH = D_MIX - MLSTM_WIDTH
S5_GROUP = 16
S5_GROUPS = S5_WIDTH // S5_GROUP
S5_STATE = 64
S5_DT_MIN = 1e-3
S5_DT_MAX = 1e-1
PEER_HEADS = 8
PEER_NKEYS = 128
PEER_EXPERTS = PEER_NKEYS * PEER_NKEYS
PEER_TOPK = 16
PEER_QDIM = 256
PEER_BLOCK = 128
RMS_EPS = 1e-6
N_IN = 4 * MLSTM_WIDTH + 2 * MLSTM_HEADS + S5_WIDTH


def rmsnorm(x, g):
    xf = x.astype(jnp.float32)
    y = xf * lax.rsqrt(jnp.mean(xf * xf, axis=-1, keepdims=True) + RMS_EPS)
    return (y * g.astype(jnp.float32)).astype(x.dtype)

def causal_dwconv(x, w):
    K, C = w.shape
    return lax.conv_general_dilated(
        x, w[:, None, :].astype(x.dtype), window_strides=(1,), padding=((K - 1, 0),),
        dimension_numbers=('NWC', 'WIO', 'NWC'), feature_group_count=C)

def mlstm_chunkwise(q, k, v, li, lf):
    B, H, S, Dh = q.shape
    L = MLSTM_CHUNK
    NC = S // L
    q = q.reshape(B, H, NC, L, Dh) * (Dh ** -0.5)
    k = k.reshape(B, H, NC, L, Dh)
    v = v.reshape(B, H, NC, L, Dh)
    li = li.reshape(B, H, NC, L)
    lf = lf.reshape(B, H, NC, L)
    a = jnp.cumsum(lf, axis=-1)
    A = a[..., -1]
    g = A[..., None] - a + li
    m_loc = jnp.max(g, axis=-1)
    w = jnp.exp(g - m_loc[..., None])
    dC = jnp.einsum('bhcl,bhcld,bhcle->bhcde', w, k, v)
    dn = jnp.einsum('bhcl,bhcld->bhcd', w, k)

    def step(carry, inp):
        C, n, m = carry
        dC_c, dn_c, m_c, A_c = inp
        m_new = jnp.maximum(A_c + m, m_c)
        s_old = jnp.exp(A_c + m - m_new)
        s_new = jnp.exp(m_c - m_new)
        C_new = s_old[..., None, None] * C + s_new[..., None, None] * dC_c
        n_new = s_old[..., None] * n + s_new[..., None] * dn_c
        return (C_new, n_new, m_new), (C, n, m)

    init = (jnp.zeros((B, H, Dh, Dh), jnp.float32), jnp.zeros((B, H, Dh), jnp.float32),
            jnp.zeros((B, H), jnp.float32))
    xs = (jnp.moveaxis(dC, 2, 0), jnp.moveaxis(dn, 2, 0), jnp.moveaxis(m_loc, 2, 0), jnp.moveaxis(A, 2, 0))
    _, (C0, n0, m0) = lax.scan(step, init, xs)
    C0 = jnp.moveaxis(C0, 0, 2)
    n0 = jnp.moveaxis(n0, 0, 2)
    m0 = jnp.moveaxis(m0, 0, 2)

    Dmat = a[..., :, None] - a[..., None, :] + li[..., None, :]
    causal = jnp.tril(jnp.ones((L, L), dtype=bool))
    Dmat = jnp.where(causal, Dmat, -jnp.inf)
    m_inter = a + m0[..., None]
    m_t = jnp.maximum(m_inter, jnp.max(Dmat, axis=-1))
    Wm = jnp.exp(Dmat - m_t[..., None])
    s_inter = jnp.exp(m_inter - m_t)
    qk = jnp.einsum('bhcjd,bhcsd->bhcjs', q, k) * Wm
    num = jnp.einsum('bhcjs,bhcse->bhcje', qk, v) + s_inter[..., None] * jnp.einsum('bhcjd,bhcde->bhcje', q, C0)
    den = jnp.sum(qk, axis=-1) + s_inter * jnp.einsum('bhcjd,bhcd->bhcj', q, n0)
    h = num / jnp.maximum(jnp.abs(den), jnp.exp(-m_t))[..., None]
    return h.reshape(B, H, S, Dh)

def s5_groups(u, lam_re, lam_im, log_dt, b_re, b_im, c_re, c_im, d, glu_w):
    S = u.shape[1]
    f32 = jnp.float32
    lam_re = lam_re.astype(f32); lam_im = lam_im.astype(f32)
    dt = jnp.exp(log_dt.astype(f32))[:, None]
    mag = jnp.exp(lam_re * dt)
    ar = mag * jnp.cos(lam_im * dt)
    ai = mag * jnp.sin(lam_im * dt)
    den = lam_re * lam_re + lam_im * lam_im
    fr = ((ar - 1.0) * lam_re + ai * lam_im) / den
    fi = (ai * lam_re - (ar - 1.0) * lam_im) / den
    b_re = b_re.astype(f32); b_im = b_im.astype(f32)
    bbr = fr[..., None] * b_re - fi[..., None] * b_im
    bbi = fr[..., None] * b_im + fi[..., None] * b_re
    xr = jnp.einsum('bsgh,gph->bsgp', u, bbr)
    xi = jnp.einsum('bsgh,gph->bsgp', u, bbi)
    G, P = ar.shape
    a_r = jnp.broadcast_to(ar[None, None], (1, S, G, P))
    a_i = jnp.broadcast_to(ai[None, None], (1, S, G, P))

    def combine(e1, e2):
        a1r, a1i, b1r, b1i = e1
        a2r, a2i, b2r, b2i = e2
        return (a1r * a2r - a1i * a2i, a1r * a2i + a1i * a2r,
                a2r * b1r - a2i * b1i + b2r, a2r * b1i + a2i * b1r + b2i)

    _, _, sr, si = lax.associative_scan(combine, (a_r, a_i, xr, xi), axis=1)
    y = (jnp.einsum('bsgp,ghp->bsgh', sr, c_re.astype(f32))
         - jnp.einsum('bsgp,ghp->bsgh', si, c_im.astype(f32))
         + d.astype(f32) * u)
    ab = jnp.einsum('bsgh,ghk->bsgk', jax.nn.gelu(y, approximate=False), glu_w.astype(f32))
    return ab[..., :S5_GROUP] * jax.nn.sigmoid(ab[..., S5_GROUP:])

def peer(x, wq, subkeys, u_tab, v_tab):
    B, S, D = x.shape
    f32 = jnp.float32
    half = PEER_QDIM // 2
    q = (x @ wq).astype(f32).reshape(B, S, PEER_HEADS, 2, half)
    s = jnp.einsum('bshpd,pkd->bshpk', q, subkeys.astype(f32))
    s1, i1 = lax.top_k(s[..., 0, :], PEER_TOPK)
    s2, i2 = lax.top_k(s[..., 1, :], PEER_TOPK)
    cand_s = (s1[..., :, None] + s2[..., None, :]).reshape(B, S, PEER_HEADS, PEER_TOPK * PEER_TOPK)
    cand_i = (i1[..., :, None] * PEER_NKEYS + i2[..., None, :]).reshape(B, S, PEER_HEADS, PEER_TOPK * PEER_TOPK)
    top_s, pos = lax.top_k(cand_s, PEER_TOPK)
    idx = jnp.take_along_axis(cand_i, pos, axis=-1)
    gate = jax.nn.softmax(top_s, axis=-1)
    T = B * S
    HK = PEER_HEADS * PEER_TOPK
    xb = x.reshape(T // PEER_BLOCK, PEER_BLOCK, D)
    ib = idx.reshape(T // PEER_BLOCK, PEER_BLOCK, HK)
    gb = gate.reshape(T // PEER_BLOCK, PEER_BLOCK, HK)

    def block(args):
        xt, it, gt = args
        ue = jnp.take(u_tab, it, axis=0)
        ve = jnp.take(v_tab, it, axis=0)
        act = jax.nn.gelu(jnp.einsum('td,ted->te', xt, ue).astype(f32), approximate=False)
        return jnp.einsum('te,ted->td', (gt * act).astype(ve.dtype), ve)

    out = lax.map(block, (xb, ib, gb))
    return out.reshape(B, S, D)

def first_inputs(seed: int = 0) -> dict:
    key = jax.random.key(seed)
    ks = jax.random.split(key, 24)
    f32 = jnp.float32
    nrm = lambda k, shape, s: jax.random.normal(k, shape, f32) * s
    L = DEPTH
    G, P, Hg = S5_GROUPS, S5_STATE, S5_GROUP
    f_bias = jnp.broadcast_to(jnp.linspace(3.0, 6.0, MLSTM_HEADS, dtype=f32), (L, MLSTM_HEADS))
    b_gates = jnp.concatenate([nrm(ks[3], (L, MLSTM_HEADS), 0.1),
                               f_bias + nrm(ks[4], (L, MLSTM_HEADS), 0.1)], axis=-1)
    lam_im0 = jnp.pi * jnp.arange(P, dtype=f32)
    log_dt = jax.random.uniform(ks[8], (L, G), f32, math.log(S5_DT_MIN), math.log(S5_DT_MAX))
    return dict(
        x=nrm(ks[0], (BATCH, SEQ, D_MODEL), 1.0),
        norm1_g=1.0 + nrm(ks[1], (L, D_MODEL), 0.1),
        w_in=nrm(ks[2], (L, D_MODEL, N_IN), D_MODEL ** -0.5),
        b_gates=b_gates,
        conv_qk_w=nrm(ks[5], (L, CONV_WIDTH, 2 * MLSTM_WIDTH), CONV_WIDTH ** -0.5),
        mlstm_norm_g=1.0 + nrm(ks[6], (L, MLSTM_WIDTH), 0.1),
        s5_lambda_re=-0.5 + nrm(ks[7], (L, G, P), 0.01),
        s5_lambda_im=lam_im0 + nrm(ks[9], (L, G, P), 0.01),
        s5_log_dt=log_dt,
        s5_b_re=nrm(ks[10], (L, G, P, Hg), (2 * Hg) ** -0.5),
        s5_b_im=nrm(ks[11], (L, G, P, Hg), (2 * Hg) ** -0.5),
        s5_c_re=nrm(ks[12], (L, G, Hg, P), P ** -0.5),
        s5_c_im=nrm(ks[13], (L, G, Hg, P), P ** -0.5),
        s5_d=nrm(ks[14], (L, G, Hg), 0.5),
        s5_glu_w=nrm(ks[15], (L, G, Hg, 2 * Hg), Hg ** -0.5),
        w_out=nrm(ks[16], (L, D_MIX, D_MODEL), D_MIX ** -0.5),
        norm2_g=1.0 + nrm(ks[17], (L, D_MODEL), 0.1),
        peer_wq=nrm(ks[18], (L, D_MODEL, PEER_HEADS * PEER_QDIM), D_MODEL ** -0.5),
        peer_subkeys=nrm(ks[19], (L, 2, PEER_NKEYS, PEER_QDIM // 2), (PEER_QDIM // 2) ** -0.5),
        peer_u=nrm(ks[20], (L, PEER_EXPERTS, D_MODEL), D_MODEL ** -0.5),
        peer_v=nrm(ks[21], (L, PEER_EXPERTS, D_MODEL), PEER_HEADS ** -0.5),
        final_g=1.0 + nrm(ks[22], (D_MODEL,), 0.1),
    )

def first_block(x, norm1_g, w_in, b_gates, conv_qk_w, mlstm_norm_g, s5_lambda_re, s5_lambda_im,
              s5_log_dt, s5_b_re, s5_b_im, s5_c_re, s5_c_im, s5_d, s5_glu_w, w_out, norm2_g,
              peer_wq, peer_subkeys, peer_u, peer_v, final_g):
    B, S, _ = x.shape
    f32 = jnp.float32
    W, H, Dh = MLSTM_WIDTH, MLSTM_HEADS, MLSTM_HEAD_DIM
    h = x
    for l in range(DEPTH):
        xn = rmsnorm(h, norm1_g[l])
        z = xn @ w_in[l]
        q, k, v, o, gates, u = jnp.split(z, [W, 2 * W, 3 * W, 4 * W, 4 * W + 2 * H], axis=-1)
        qk = jax.nn.silu(causal_dwconv(jnp.concatenate([q, k], axis=-1), conv_qk_w[l]))
        q, k = qk[..., :W], qk[..., W:]
        to_heads = lambda t: t.astype(f32).reshape(B, S, H, Dh).transpose(0, 2, 1, 3)
        gates = gates.astype(f32) + b_gates[l].astype(f32)
        li = gates[..., :H].transpose(0, 2, 1)
        lf = jax.nn.log_sigmoid(gates[..., H:]).transpose(0, 2, 1)
        hm = mlstm_chunkwise(to_heads(q), to_heads(k), to_heads(v), li, lf)
        hm = hm.transpose(0, 2, 1, 3)
        hm = hm * lax.rsqrt(jnp.mean(hm * hm, axis=-1, keepdims=True) + RMS_EPS)
        hm = hm.reshape(B, S, W) * mlstm_norm_g[l].astype(f32) * jax.nn.sigmoid(o.astype(f32))
        ys = s5_groups(u.astype(f32).reshape(B, S, S5_GROUPS, S5_GROUP),
                       s5_lambda_re[l], s5_lambda_im[l], s5_log_dt[l], s5_b_re[l], s5_b_im[l],
                       s5_c_re[l], s5_c_im[l], s5_d[l], s5_glu_w[l]).reshape(B, S, S5_WIDTH)
        mix = jnp.concatenate([hm, ys], axis=-1).astype(h.dtype) @ w_out[l]
        h = h + mix.astype(h.dtype)
        h = h + peer(rmsnorm(h, norm2_g[l]), peer_wq[l], peer_subkeys[l], peer_u[l], peer_v[l]).astype(h.dtype)
    return rmsnorm(h, final_g)


HEAD_DIM = 128
SB_HEADS = 6
SB_BLOCK = 128
DIL_GROUPS = ((128, 1), (512, 4), (2048, 16))
DIL_HEADS_PER_GROUP = 2
DIL_HEADS = DIL_HEADS_PER_GROUP * len(DIL_GROUPS)
GLA_HEADS = 4
GLA_DK = 128
GLA_DV = 256
GLA_GATE_RANK = 16
GLA_GATE_TAU = 16.0
GLA_CHUNK = 64
N_BRANCH = 3
D_FF = -(-8 * D_MODEL // (3 * 256)) * 256
N_MOD = 6
EPS = 1e-6

SB_W = SB_HEADS * HEAD_DIM
DIL_W = DIL_HEADS * HEAD_DIM
DIL_OUT_W = DIL_HEADS_PER_GROUP * HEAD_DIM
GLA_QK_W = GLA_HEADS * GLA_DK
GLA_V_W = GLA_HEADS * GLA_DV
IN_SPLITS = (SB_W, SB_W, SB_W, DIL_W, DIL_W, DIL_W, GLA_QK_W, GLA_QK_W, GLA_V_W, GLA_V_W, GLA_GATE_RANK, N_BRANCH * D_MODEL)
IN_WIDTH = sum(IN_SPLITS)


def rms_norm(x, gain):
    xf = x.astype(jnp.float32)
    y = xf * lax.rsqrt(jnp.mean(jnp.square(xf), axis=-1, keepdims=True) + EPS)
    return (y * gain.astype(jnp.float32)).astype(x.dtype)

def split_heads(x, n):
    b, t, w = x.shape
    return x.reshape(b, t, n, w // n).transpose(0, 2, 1, 3)

def merge_heads(x):
    b, h, t, d = x.shape
    return x.transpose(0, 2, 1, 3).reshape(b, t, h * d)

def alibi_slopes(n):
    return 2.0 ** (-8.0 * jnp.arange(1, n + 1, dtype=jnp.float32) / n)

def stick_breaking_attention(q, k, v):
    b, h, t, d = q.shape
    scale = d ** -0.5
    outs = []
    for blk in range(t // SB_BLOCK):
        start = blk * SB_BLOCK
        end = start + SB_BLOCK
        qb = q[:, :, start:end]
        kb = k[:, :, :end]
        vb = v[:, :, :end]
        z = jnp.einsum('bhqd,bhkd->bhqk', qb, kb).astype(jnp.float32) * scale
        t_pos = start + jnp.arange(SB_BLOCK)[:, None]
        s_pos = jnp.arange(end)[None, :]
        causal = s_pos < t_pos
        log_beta = jax.nn.log_sigmoid(z)
        log_rest = jnp.where(causal, jax.nn.log_sigmoid(-z), 0.0)
        after = lax.cumsum(log_rest, axis=3, reverse=True) - log_rest
        w = jnp.where(causal, jnp.exp(log_beta + after), 0.0)
        outs.append(jnp.einsum('bhqk,bhkd->bhqd', w.astype(v.dtype), vb))
    return jnp.concatenate(outs, axis=2)

def dilated_group_attention(q, k, v, window, dilation, slopes):
    b, h, t, d = q.shape
    blk = window // dilation
    u_len = t // dilation
    nb = -(-u_len // blk)
    u_pad = nb * blk

    def strided(x):
        x = x.reshape(b, h, u_len, dilation, d).transpose(0, 1, 3, 2, 4)
        x = jnp.pad(x, ((0, 0), (0, 0), (0, 0), (0, u_pad - u_len), (0, 0)))
        return x.reshape(b, h, dilation, nb, blk, d)

    def with_prev(x):
        prev = jnp.pad(x[:, :, :, :-1], ((0, 0), (0, 0), (0, 0), (1, 0), (0, 0), (0, 0)))
        return jnp.concatenate([prev, x], axis=4)

    qs = strided(q)
    kk = with_prev(strided(k))
    vv = with_prev(strided(v))
    s = jnp.einsum('bhrnqd,bhrnkd->bhrnqk', qs, kk).astype(jnp.float32) * (d ** -0.5)
    i = jnp.arange(blk)[:, None]
    j = jnp.arange(2 * blk)[None, :]
    delta = blk + i - j
    n = jnp.arange(nb)[:, None, None]
    valid = (delta >= 0) & (delta <= blk) & (n * blk - blk + j >= 0)
    bias = -(slopes.astype(jnp.float32)[:, None, None] * (dilation * delta).astype(jnp.float32))
    logits = jnp.where(valid, s + bias[None, :, None, None], -jnp.inf)
    lse = jax.nn.logsumexp(logits, axis=-1)
    p = jnp.exp(logits - lse[..., None])
    o = jnp.einsum('bhrnqk,bhrnkd->bhrnqd', p.astype(v.dtype), vv)
    o = o.reshape(b, h, dilation, u_pad, d)[:, :, :, :u_len].transpose(0, 1, 3, 2, 4).reshape(b, h, t, d)
    lse = lse.reshape(b, h, dilation, u_pad)[..., :u_len].transpose(0, 1, 3, 2).reshape(b, h, t)
    return o, lse

def dilated_mixture(q, k, v, slopes):
    outs, lses = [], []
    for g, (window, dilation) in enumerate(DIL_GROUPS):
        sl = slice(g * DIL_HEADS_PER_GROUP, (g + 1) * DIL_HEADS_PER_GROUP)
        o, l = dilated_group_attention(q[:, sl], k[:, sl], v[:, sl], window, dilation, slopes[sl])
        outs.append(o)
        lses.append(l)
    weights = jax.nn.softmax(jnp.stack(lses, axis=0), axis=0)
    mixed = jnp.sum(weights[..., None] * jnp.stack(outs, axis=0).astype(jnp.float32), axis=0)
    return mixed.astype(q.dtype)

def gla_chunked(q, k, v, log_a):
    b, h, t, dk = q.shape
    dv = v.shape[-1]
    c = GLA_CHUNK
    n = t // c

    def chunks(x):
        return x.reshape(b, h, n, c, x.shape[-1]).transpose(2, 0, 1, 3, 4)

    qc = chunks((q.astype(jnp.float32) * (dk ** -0.5)))
    kc = chunks(k.astype(jnp.float32))
    vc = chunks(v.astype(jnp.float32))
    ac = chunks(log_a.astype(jnp.float32))
    mask = jnp.tril(jnp.ones((c, c), dtype=bool))

    def step(state, inp):
        qi, ki, vi, ai = inp
        cum = jnp.cumsum(ai, axis=2)
        inter = jnp.einsum('bhcd,bhde->bhce', qi * jnp.exp(cum), state)
        diff = cum[:, :, :, None, :] - cum[:, :, None, :, :]
        decay = jnp.exp(jnp.where(mask[:, :, None], diff, -jnp.inf))
        scores = jnp.einsum('bhid,bhjd,bhijd->bhij', qi, ki, decay)
        intra = jnp.einsum('bhij,bhje->bhie', scores, vi)
        last = cum[:, :, -1:, :]
        new_state = jnp.exp(last[:, :, 0, :])[..., None] * state + jnp.einsum('bhcd,bhce->bhde', ki * jnp.exp(last - cum), vi)
        return new_state, inter + intra

    s0 = jnp.zeros((b, h, dk, dv), jnp.float32)
    _, o = lax.scan(step, s0, (qc, kc, vc, ac))
    return o.transpose(1, 2, 0, 3, 4).reshape(b, h, t, dv).astype(v.dtype)

def mixing_sublayer(h, w_in, sb_q_gain, sb_k_gain, dil_q_gain, dil_k_gain, w_gla_a, b_gla_a, gla_out_gain,
                    w_br_sb, w_br_dil, w_br_gla, w_out):
    b, t, d = h.shape
    proj = h @ w_in
    idx = [int(i) for i in np.cumsum(IN_SPLITS)[:-1]]
    (q_sb, k_sb, v_sb, q_dil, k_dil, v_dil, q_gla, k_gla, v_gla, r_gla, a_gla, gate_cols) = jnp.split(proj, idx, axis=-1)

    qa = rms_norm(split_heads(q_sb, SB_HEADS), sb_q_gain)
    ka = rms_norm(split_heads(k_sb, SB_HEADS), sb_k_gain)
    o_sb = merge_heads(stick_breaking_attention(qa, ka, split_heads(v_sb, SB_HEADS)))

    qb = rms_norm(split_heads(q_dil, DIL_HEADS), dil_q_gain)
    kb = rms_norm(split_heads(k_dil, DIL_HEADS), dil_k_gain)
    o_dil = merge_heads(dilated_mixture(qb, kb, split_heads(v_dil, DIL_HEADS), alibi_slopes(DIL_HEADS)))

    a = (a_gla @ w_gla_a + b_gla_a).astype(jnp.float32)
    log_a = jax.nn.log_sigmoid(a) / GLA_GATE_TAU
    o_g = gla_chunked(split_heads(q_gla, GLA_HEADS), split_heads(k_gla, GLA_HEADS),
                      split_heads(v_gla, GLA_HEADS), split_heads(log_a, GLA_HEADS))
    o_gla = merge_heads(rms_norm(o_g, gla_out_gain)) * jax.nn.silu(r_gla)

    g = jax.nn.sigmoid(gate_cols.reshape(b, t, N_BRANCH, d))
    y = (g[:, :, 0] * (o_sb @ w_br_sb)
         + g[:, :, 1] * (o_dil @ w_br_dil)
         + g[:, :, 2] * (o_gla @ w_br_gla))
    return y @ w_out

def swiglu(h, w_ffn_in, w_ffn_out):
    gate, up = jnp.split(h @ w_ffn_in, 2, axis=-1)
    return (jax.nn.silu(gate) * up) @ w_ffn_out

def second_inputs(seed: int = 0) -> dict:
    key = jax.random.key(seed)
    ks = jax.random.split(key, 20)
    L, D = DEPTH, D_MODEL

    def normal(k, shape, scale):
        return jax.random.normal(k, shape, jnp.float32) * scale

    return {
        "x": normal(ks[0], (BATCH, SEQ, D), 1.0),
        "c": normal(ks[1], (BATCH, D), 1.0),
        "w_ada": normal(ks[2], (L, D, N_MOD * D), 0.5 * D ** -0.5),
        "b_ada": normal(ks[3], (L, N_MOD * D), 0.02),
        "norm1_gain": 1.0 + normal(ks[4], (L, D), 0.02),
        "norm2_gain": 1.0 + normal(ks[5], (L, D), 0.02),
        "w_in": normal(ks[6], (L, D, IN_WIDTH), D ** -0.5),
        "sb_q_gain": 1.0 + normal(ks[7], (L, HEAD_DIM), 0.02),
        "sb_k_gain": 1.0 + normal(ks[8], (L, HEAD_DIM), 0.02),
        "dil_q_gain": 1.0 + normal(ks[9], (L, HEAD_DIM), 0.02),
        "dil_k_gain": 1.0 + normal(ks[10], (L, HEAD_DIM), 0.02),
        "w_gla_a": normal(ks[11], (L, GLA_GATE_RANK, GLA_QK_W), GLA_GATE_RANK ** -0.5),
        "b_gla_a": normal(ks[12], (L, GLA_QK_W), 0.02),
        "gla_out_gain": 1.0 + normal(ks[13], (L, GLA_DV), 0.02),
        "w_br_sb": normal(ks[14], (L, SB_W, D), SB_W ** -0.5),
        "w_br_dil": normal(ks[15], (L, DIL_OUT_W, D), DIL_OUT_W ** -0.5),
        "w_br_gla": normal(ks[16], (L, GLA_V_W, D), GLA_V_W ** -0.5),
        "w_out": normal(ks[17], (L, D, D), D ** -0.5),
        "w_ffn_in": normal(ks[18], (L, D, 2 * D_FF), D ** -0.5),
        "w_ffn_out": normal(ks[19], (L, D_FF, D), D_FF ** -0.5),
    }

def second_block(x, c, w_ada, b_ada, norm1_gain, norm2_gain, w_in, sb_q_gain, sb_k_gain, dil_q_gain, dil_k_gain,
              w_gla_a, b_gla_a, gla_out_gain, w_br_sb, w_br_dil, w_br_gla, w_out, w_ffn_in, w_ffn_out):
    for l in range(DEPTH):
        mod = jax.nn.silu(c) @ w_ada[l] + b_ada[l]
        shift1, scale1, gate1, shift2, scale2, gate2 = jnp.split(mod[:, None, :], N_MOD, axis=-1)
        h = rms_norm(x, norm1_gain[l]) * (1 + scale1) + shift1
        x = x + gate1 * mixing_sublayer(h, w_in[l], sb_q_gain[l], sb_k_gain[l], dil_q_gain[l], dil_k_gain[l],
                                        w_gla_a[l], b_gla_a[l], gla_out_gain[l],
                                        w_br_sb[l], w_br_dil[l], w_br_gla[l], w_out[l])
        h = rms_norm(x, norm2_gain[l]) * (1 + scale2) + shift2
        x = x + gate2 * swiglu(h, w_ffn_in[l], w_ffn_out[l])
    return x


def setup_inputs(seed=0):
    out = dict(first_inputs(seed))
    for name, value in second_inputs(seed + 1).items():
        if name != "x":
            out[name + "_2"] = value
    return out


def reference(
    x, norm1_g, w_in, b_gates, conv_qk_w, mlstm_norm_g, s5_lambda_re, s5_lambda_im, s5_log_dt,
    s5_b_re, s5_b_im, s5_c_re, s5_c_im, s5_d, s5_glu_w, w_out, norm2_g, peer_wq, peer_subkeys,
    peer_u, peer_v, final_g, c_2, w_ada_2, b_ada_2, norm1_gain_2, norm2_gain_2, w_in_2,
    sb_q_gain_2, sb_k_gain_2, dil_q_gain_2, dil_k_gain_2, w_gla_a_2, b_gla_a_2, gla_out_gain_2,
    w_br_sb_2, w_br_dil_2, w_br_gla_2, w_out_2, w_ffn_in_2, w_ffn_out_2,
):
    x = first_block(
        x, norm1_g, w_in, b_gates, conv_qk_w, mlstm_norm_g, s5_lambda_re, s5_lambda_im,
        s5_log_dt, s5_b_re, s5_b_im, s5_c_re, s5_c_im, s5_d, s5_glu_w, w_out, norm2_g, peer_wq,
        peer_subkeys, peer_u, peer_v, final_g,
    )
    return second_block(
        x, c_2, w_ada_2, b_ada_2, norm1_gain_2, norm2_gain_2, w_in_2, sb_q_gain_2, sb_k_gain_2,
        dil_q_gain_2, dil_k_gain_2, w_gla_a_2, b_gla_a_2, gla_out_gain_2, w_br_sb_2, w_br_dil_2,
        w_br_gla_2, w_out_2, w_ffn_in_2, w_ffn_out_2,
    )


_drawn_inputs = setup_inputs


def setup_inputs(seed=0):
    import zlib

    import numpy as np

    out = dict(_drawn_inputs(seed))
    spreads = {}
    factors = {'s5_lambda_re': 47.088,
     'norm1_gain_2': 8.0,
     'norm2_gain_2': 8.0,
     'sb_q_gain_2': 34.215,
     'sb_k_gain_2': 30.419,
     'dil_q_gain_2': 8.0,
     'dil_k_gain_2': 8.0,
     'b_gla_a_2': 8.0,
     'gla_out_gain_2': 8.0}
    for name, (base, spread) in spreads.items():
        noise = np.random.default_rng([zlib.crc32(name.encode()), seed]).standard_normal(out[name].shape)
        drawn = base * np.exp(spread * noise) if base else spread * noise
        out[name] = __import__('jax').numpy.asarray(drawn.astype(out[name].dtype))
    for name, factor in factors.items():
        out[name] = (out[name] * factor).astype(out[name].dtype)
    return out
```

```python
import math
from contextlib import ExitStack

import numpy as np

import concourse.bass as bass
from concourse import mybir
from concourse.alu_op_type import AluOpType as ALU

F32 = mybir.dt.float32
U32 = mybir.dt.uint32
ACT = mybir.ActivationFunctionType
AX = mybir.AxisListType.X

P = 128
NB = 512
KS = 4
SLOTS = 8
NEG = -1.0e30
MAGIC = 1.5 * 2.0 ** 23


def bc(ap, axis, shape):
    return ap.unsqueeze(axis).to_broadcast(shape)


def build(nc, a, out, stop=99):
    T, D = a["x"].shape[1:]
    TT = T // P
    KD = D // P
    EPS = 1e-6
    W = a["mlstm_norm_g"].shape[1]
    H = a["b_gates"].shape[1] // 2
    DH = W // H
    DC = DH // P
    G, PS, HG = a["s5_b_re"].shape[1:]
    SC = G * HG // P
    GP = P // HG
    TILES = G * PS // P
    TC = TILES // SC
    CW = a["conv_qk_w"].shape[1]
    QC = 2 * W // P
    KEYS, HALF = a["peer_subkeys"].shape[2:]
    PH = a["peer_wq"].shape[2] // (2 * HALF)
    TOPK = 16
    HK = PH * TOPK
    HD = a["sb_q_gain_2"].shape[1]
    SBW = a["w_br_sb_2"].shape[1]
    SBH = SBW // HD
    DILG = ((128, 1), (512, 4), (2048, 16))
    DHG = a["w_br_dil_2"].shape[1] // HD
    DLH = DHG * len(DILG)
    DLW = DLH * HD
    GV = a["w_br_gla_2"].shape[1]
    GK = a["w_gla_a_2"].shape[2]
    GR = a["w_gla_a_2"].shape[1]
    GH = GK // P
    GDV = GV // GH
    TAU = 16.0
    FF = a["w_ffn_out_2"].shape[1]
    NMOD = 6
    assert TT == 2 and HD == P and TC * SC == TILES and PS * 2 == P

    ctx = ExitStack()
    with ctx:
        def sb(name, shape, dt=F32):
            return ctx.enter_context(nc.sbuf_tensor(name, shape, dt))

        phase_sems = []

        def sem(name):
            phase_sems.append(nc.alloc_semaphore(name=name))
            return phase_sems[-1]

        def recycle():
            nc.clear_and_free_semaphores(phase_sems)
            nc.all_engine_barrier()
            phase_sems.clear()

        ps = [ctx.enter_context(nc.psum_tensor(f"bank{i}", [P, NB], F32)) for i in range(8)]
        ring = sb("ring", [P, SLOTS, KS, NB])
        res = sb("res", [P, TT, D])
        nat = sb("nat", [P, TT, D])
        aT = sb("aT", [P, KD, T])
        ident = sb("ident", [P, P])
        ones = sb("ones", [P, P])
        upto = sb("upto", [P, P])
        causal = sb("causal", [P, P])
        small = sb("small", [P, 256])
        POOL = 22700
        pool = sb("pool", [P, POOL])

        def view(ap, shape):
            names = "abcd"[:len(shape)]
            return ap.rearrange(f"p ({' '.join(names)}) -> p {' '.join(names)}", **dict(zip(names, shape)))

        class Places:

            def __init__(self, tensor, at=0):
                self.tensor, self.at = tensor, at

            def take(self, *shape):
                n = int(np.prod(shape))
                ap = self.tensor[:, self.at:self.at + n]
                self.at += n
                assert self.at <= self.tensor.shape[1], self.at
                return view(ap, shape) if len(shape) > 1 else ap

        landed = [ctx.enter_context(nc.semaphore(f"slab_landed{i}")) for i in range(SLOTS)]
        slabs_used = ctx.enter_context(nc.semaphore("slabs_used"))

        def cols(w, k0, c0, n=NB, ks=KS):
            return w[k0 * P:(k0 + ks) * P, c0:c0 + n].rearrange("(k p) n -> p k n", p=P) if isinstance(c0, int) \
                else w[k0 * P:(k0 + ks) * P, bass.ds(c0, n)].rearrange("(k p) n -> p k n", p=P)

        class Section:

            def __init__(self, blocks, per, source):
                self.blocks, self.per, self.source = blocks, per, source
                self.n = blocks * per

        w_in, w_in2 = a["w_in"][0], a["w_in_2"][0]
        C_GATES, C_U = 4 * W, 4 * W + 2 * H
        C_A = 3 * SBW + 3 * DLW + 2 * GK + 2 * GV
        C_G = C_A + GR
        OB = D // NB

        def plain(w, c0=0):
            return lambda b, s: [(0, KS, cols(w, KS * s, c0 + b * NB))]

        br = [a["w_br_sb_2"][0], a["w_br_dil_2"][0], a["w_br_gla_2"][0]]
        br_rows = [w.shape[0] // P for w in br]
        br_chunks = [(i, k) for i in range(3) for k in range(br_rows[i])]

        def gated(b, s):
            n, part = divmod(b, 4)
            if part < 3:
                return [(0, KS, cols(w_in2, KS * s, C_G + part * D + n * NB))]
            parts, todo = [], br_chunks[KS * s:KS * s + KS]
            for i in range(3):
                ks = [k for j, k in todo if j == i]
                if ks:
                    parts.append((todo.index((i, ks[0])), len(ks), cols(br[i], ks[0], n * NB, ks=len(ks))))
            return parts

        def ffn_pairs(b, s):
            return [(0, KS, cols(a["w_ffn_in_2"][0], KS * s, (b % 2) * FF + (b // 2) * NB))]

        SECTIONS = [
            Section(2, 4, plain(w_in, C_U)),
            Section(4 * W // NB, 4, plain(w_in)),
            Section(OB, 4, plain(a["w_out"][0])),
            Section(PH * 2 * HALF // NB, 4, plain(a["peer_wq"][0])),
            Section(NMOD * OB, 4, plain(a["w_ada_2"][0])),
            Section(C_A // NB, 4, plain(w_in2)),
            Section(4 * OB, 4, gated),
            Section(OB, 4, plain(a["w_out_2"][0])),
            Section(2 * FF // NB, 4, ffn_pairs),
            Section(OB, FF // P // KS, plain(a["w_ffn_out_2"][0])),
        ]
        first_slab = [0]
        for s in SECTIONS:
            first_slab.append(first_slab[-1] + s.n)

        def issue(sp, sec, n, g):
            s = SECTIONS[sec]
            if g >= SLOTS:
                sp.wait_ge(slabs_used, g - SLOTS + 1)
            for k0, ks, src in s.source(n // s.per, n % s.per):
                sp.dma_start(ring[:, g % SLOTS, k0:k0 + ks, :], src).then_inc(landed[g % SLOTS], 16)

        transfers, reach = [0] * SLOTS, []
        for s in SECTIONS:
            for n in range(s.n):
                g = len(reach)
                count = len(gated(n // 4, n % 4)) if s.source is gated else 1
                transfers[g % SLOTS] += 16 * count
                reach.append(transfers[g % SLOTS])

        def stream(sp, sec):
            s, g0 = SECTIONS[sec], first_slab[sec]
            n = SLOTS
            if s.source not in (gated, ffn_pairs) and s.per == 4 and s.n // 8 > 1:
                with sp.Fori(1, s.n // 8) as i:
                    for j in range(8):
                        sp.wait_ge(slabs_used, i * 8 + (g0 + j - SLOTS + 1))
                        (k0, ks, src), = s.source(i * 2 + j // 4, j % 4)
                        slot = (g0 + j) % SLOTS
                        sp.dma_start(ring[:, slot, :, :], src).then_inc(landed[slot], 16)
                n = s.n // 8 * 8
            for m in range(n, s.n):
                issue(sp, sec, m, g0 + m)
            if sec + 1 < len(SECTIONS):
                for m in range(min(SLOTS, SECTIONS[sec + 1].n)):
                    issue(sp, sec + 1, m, first_slab[sec + 1] + m)

        def slab(pe, g, outs, lhs, k0, start, stop):
            pe.wait_ge(landed[g % SLOTS], reach[g])
            for k in range(KS):
                for o, t in outs:
                    last = nc.tensor.matmul(o, lhs(k0 + k, t), ring[:, g % SLOTS, k, :],
                                            start=start and k == 0, stop=stop and k == KS - 1)
            last.then_inc(slabs_used, 1)

        def left(k, t):
            return aT[:, k, t * P:(t + 1) * P]

        def linear(pe, sec, taken, lhs=left, tts=TT, banks=(0, 1, 2, 3)):
            s, g0 = SECTIONS[sec], first_slab[sec]
            def pair(i, first):
                for p in range(2):
                    if not first:
                        for t in taken:
                            each = tts // len(taken)
                            pe.wait_ge(t, i * 2 * each + (p - 1) * each)
                    for j in range(KD // KS):
                        m = p * (KD // KS) + j
                        slot = (g0 + m) % SLOTS
                        pe.wait_ge(landed[slot], i * 16 + reach[g0 + m])
                        for k in range(KS):
                            for t in range(tts):
                                last = nc.tensor.matmul(ps[banks[p * tts + t]][0:lhs(0, t).shape[1], :],
                                                        lhs(j * KS + k, t), ring[:, slot, k, :],
                                                        start=j + k == 0, stop=j * KS + k == KD - 1)
                        last.then_inc(slabs_used, 1)
            pair(0, True)
            with pe.Fori(1, s.blocks // 2) as i:
                pair(i, False)

        def halt(sec):
            last = first_slab[sec] + min(SLOTS, SECTIONS[sec].n)
            with nc.Block() as block:
                @block.sync
                def _(sp):
                    for g in range(max(0, last - SLOTS), last):
                        sp.wait_ge(landed[g % SLOTS], reach[g])

        maskG = small[:, 0:GP]
        maskB = view(small[:, 8:8 + TC * GP], [TC, GP])
        gate_b = small[:, 40:40 + 2 * H]
        mlstm = Places(small, 64)
        stat = small[:, 48:64]

        s_const = sem("constants")
        s_x = sem("x_landed")
        with nc.Block() as block:
            @block.gpsimd
            def _(g):
                n = [0]

                def then(ins):
                    ins.then_inc(s_const, 1)
                    n[0] += 1
                    g.wait_ge(s_const, n[0])
                g.memset(ident[:, :], 0.0)
                g.memset(ones[:, :], 1.0)
                g.memset(upto[:, :], 1.0)
                g.memset(maskG, 1.0)
                g.memset(maskB, 1.0)
                then(g.memset(causal[:, :], 0.0))
                g.affine_select(out=ident[:, :], in_=ident[:, :], compare_op=ALU.not_equal, fill=1.0, base=0,
                                pattern=[[-1, P]], channel_multiplier=1)
                g.affine_select(out=upto[:, :], in_=upto[:, :], compare_op=ALU.is_ge, fill=0.0, base=0,
                                pattern=[[1, P]], channel_multiplier=-1)
                g.affine_select(out=causal[:, :], in_=causal[:, :], compare_op=ALU.is_ge, fill=NEG, base=0,
                                pattern=[[-1, P]], channel_multiplier=1)
                then(g.affine_select(out=maskG, in_=maskG, compare_op=ALU.is_ge, fill=0.0, base=0,
                                     pattern=[[-HG, GP]], channel_multiplier=1))
                then(g.affine_select(out=maskG, in_=maskG, compare_op=ALU.is_ge, fill=0.0, base=HG - 1,
                                     pattern=[[HG, GP]], channel_multiplier=-1))
                for h in range(2):
                    m = maskB[h * PS:(h + 1) * PS]
                    then(g.affine_select(out=m, in_=m, compare_op=ALU.is_equal, fill=0.0, base=-h,
                                         pattern=[[-2, TC], [1, GP]], channel_multiplier=0))

            @block.sync
            def _(sp):
                sp.dma_start(res[:, :, :], a["x"][0].rearrange("(t p) d -> p t d", p=P)).then_inc(s_x, 16)
                for m in range(SLOTS):
                    issue(sp, 0, m, m)
                sp.wait_ge(s_x, 16)

        def norm_phase(name, gain, scale=None, shift=None, dst=None, transposed=True):
            if stop < 0:
                return
            dst = nat if dst is None else dst
            rows = Places(pool)
            gain_row, scale_row, shift_row = rows.take(D), rows.take(D), rows.take(D)
            s_rows, s_sq, s_rt = sem(name + "_rows"), sem(name + "_squares"), sem(name + "_root")
            s_step, s_nat, s_tr = sem(name + "_vector_step"), sem(name + "_normed"), sem(name + "_transposed")
            s_ev = [sem(name + "_copied_act"), sem(name + "_copied_dve")]
            with nc.Block() as block:
                @block.sync
                def _(sp):
                    for row, src in ((gain_row, gain), (scale_row, scale), (shift_row, shift)):
                        if src is not None:
                            sp.dma_start(row, src.partition_broadcast(P)).then_inc(s_rows, 16)

                @block.scalar
                def _(act):
                    for t in range(TT):
                        nc.scalar.activation(aT[:, 8 * t:8 * t + 8, :].rearrange("p k t -> p (k t)"), res[:, t, :],
                                             ACT.Square, accum_out=stat[:, t:t + 1]).then_inc(s_sq, 1)
                    act.wait_ge(s_step, 1)
                    nc.scalar.activation(stat[:, 4:4 + TT], stat[:, 2:2 + TT], ACT.Sqrt).then_inc(s_rt, 1)
                    if transposed:
                        act.wait_ge(s_sq, TT)
                        for n in range(0, 8, 2):
                            act.wait_ge(s_tr, n + 1)
                            nc.scalar.copy(aT[:, 2 * n:2 * n + 2, :].rearrange("p k t -> p (k t)"),
                                           ps[n % 4][:, :]).then_inc(s_ev[0], 1)

                @block.vector
                def _(dve):
                    c = [0]

                    def then(ins):
                        ins.then_inc(s_step, 1)
                        c[0] += 1
                        dve.wait_ge(s_step, c[0])
                    dve.wait_ge(s_sq, TT)
                    then(nc.vector.tensor_scalar(stat[:, 2:2 + TT], stat[:, 0:TT], 1.0 / D, EPS, ALU.mult, ALU.add))
                    dve.wait_ge(s_rt, 1)
                    then(nc.vector.reciprocal(stat[:, 6:6 + TT], stat[:, 4:4 + TT]))
                    dve.wait_ge(s_rows, 16 * (1 + (scale is not None) + (shift is not None)))
                    if scale is not None:
                        then(nc.vector.tensor_scalar(scale_row, scale_row, 1.0, None, ALU.add))
                        then(nc.vector.tensor_tensor(gain_row, gain_row, scale_row, ALU.mult))
                    for t in range(TT):
                        ins = nc.vector.scalar_tensor_tensor(dst[:, t, :], res[:, t, :], stat[:, 6 + t:7 + t], gain_row,
                                                             ALU.mult, ALU.mult)
                        if shift is not None:
                            then(ins)
                            ins = nc.vector.tensor_tensor(dst[:, t, :], dst[:, t, :], shift_row, ALU.add)
                        ins.then_inc(s_nat, 1)
                    if transposed:
                        for n in range(1, 8, 2):
                            dve.wait_ge(s_tr, n + 1)
                            nc.vector.tensor_copy(aT[:, 2 * n:2 * n + 2, :].rearrange("p k t -> p (k t)"),
                                                  ps[n % 4][:, :]).then_inc(s_ev[1], 1)

                if transposed:
                    @block.tensor
                    def _(pe):
                        pe.wait_ge(s_nat, TT)
                        pe.wait_ge(s_sq, TT)
                        for n in range(8):
                            if n >= 4:
                                pe.wait_ge(s_ev[n % 2], (n - 4) // 2 + 1)
                            for j in range(4):
                                k, t = 2 * n + j // 2, j % 2
                                last = nc.tensor.transpose(ps[n % 4][:, j * P:(j + 1) * P],
                                                           dst[:, t, k * P:(k + 1) * P], ident[:, :])
                            last.then_inc(s_tr, 1)

        norm_phase("norm1", a["norm1_g"][0])
        if stop <= 1:
            return halt(0)

        place = Places(pool)
        mixT = place.take(KD, T)
        uT = mixT[:, KD - SC:KD, :]
        v_aug = place.take(TT, H, DH + 1)
        o_nat = place.take(TT, W)
        zg = place.take(TT, 2 * H)
        bb = [place.take(TILES, HG) for _ in range(2)]
        c_nat = [place.take(SC, PS) for _ in range(2)]
        glu_nat = place.take(SC, 2 * HG)
        d_col = place.take(SC)
        prm = place.take(5, TILES)
        NPOW = int(math.log2(T))
        powc, pows = place.take(NPOW, TILES), place.take(NPOW, TILES)
        s5_at = place.at
        blk_b = [place.take(TC, P) for _ in range(2)]
        blk_c = [place.take(TC, P) for _ in range(2)]
        BT = [place.take(TC, P) for _ in range(2)]
        CT = [place.take(TC, P) for _ in range(2)]
        tab_c, tab_s = place.take(TC, T), place.take(TC, T)
        w_re, w_im = place.take(TC, T), place.take(TC, T)
        r_re, r_im = place.take(TC, T), place.take(TC, T)
        tmp = place.take(TC, T)
        scratch = Places(pool, s5_at)
        u_nat = scratch.take(TT, SC * P)
        b_raw = [scratch.take(TILES, HG) for _ in range(2)]
        wg = scratch.take(KD, 2 * H)
        row = scratch.take(24, P)
        prod = [scratch.take(TILES, HG) for _ in range(2)]

        s_par, s_wg = sem("s5_parameters"), sem("gate_columns_landed")
        s_ua, s_ud, s_upe = sem("u_taken"), sem("u_transposed_copied"), sem("u_transposed")
        s_gpe = sem("gate_products")
        s_lin = sem("s5_row_step")
        s_act = sem("s5_row_functions")
        s_prt, s_prc = sem("s5_rows_transposed"), sem("s5_columns_copied")
        g0 = first_slab[0]
        with nc.Block() as block:
            @block.sync
            def _(sp):
                R = row[0:TILES]
                sp.dma_start(R[:, 0, :], a["s5_lambda_re"][0].rearrange("(j g) p -> j (g p)", g=2)).then_inc(s_par, 16)
                sp.dma_start(R[:, 1, :], a["s5_lambda_im"][0].rearrange("(j g) p -> j (g p)", g=2)).then_inc(s_par, 16)
                sp.dma_start(R[:, 23, 0:2], a["s5_log_dt"][0].rearrange("(j g) -> j g", g=2)).then_inc(s_par, 16)
                for i, n in enumerate(("s5_b_re", "s5_b_im")):
                    src = a[n][0].rearrange("(j g) p h -> (g p) j h", g=2)
                    sp.dma_start(b_raw[i], src).then_inc(s_par, 16)
                for i, n in enumerate(("s5_c_re", "s5_c_im")):
                    sp.dma_start(c_nat[i], a[n][0].rearrange("g h p -> (g h) p").rearrange("(c q) p -> q c p", q=P))\
                      .then_inc(s_par, 16)
                sp.dma_start(glu_nat, a["s5_glu_w"][0].rearrange("g h k -> (g h) k").rearrange("(c q) k -> q c k", q=P))\
                  .then_inc(s_par, 16)
                sp.dma_start(d_col, a["s5_d"][0].rearrange("g h -> (g h)").rearrange("(c q) -> q c", q=P),
                             allow_slow_non_contiguous=True).then_inc(s_par, 16)
                sp.dma_start(gate_b, a["b_gates"][0].partition_broadcast(P)).then_inc(s_par, 16)
                sp.dma_start(wg, w_in[:, C_GATES:C_U].rearrange("(k p) n -> p k n", p=P)).then_inc(s_wg, 16)
                stream(sp, 0)

            @block.tensor
            def _(pe):
                for b in range(2):
                    for j in range(4):
                        slab(pe, g0 + 4 * b + j, [(ps[2 * b + t][:, :], t) for t in range(TT)], left, 4 * j,
                             j == 0, j == 3)
                pe.wait_ge(s_wg, 16)
                for t in range(TT):
                    for k in range(KD):
                        last = nc.tensor.matmul(ps[4][:, t * 8:t * 8 + 2 * H], left(k, t), wg[:, k, :],
                                                start=k == 0, stop=k == KD - 1)
                last.then_inc(s_gpe, 1)
                pe.wait_ge(s_ua, 4)
                for n in range(4):
                    for j in range(4):
                        c, t = 2 * n + j // 2, j % 2
                        last = nc.tensor.transpose(ps[n][:, j * P:(j + 1) * P], u_nat[:, t, c * P:(c + 1) * P],
                                                   ident[:, :])
                    last.then_inc(s_upe, 1)
                pe.wait_ge(s_act, 4)
                for j in range(5):
                    last = nc.tensor.transpose(ps[5][:, j * TILES:(j + 1) * TILES], row[0:TILES, 16 + j, :],
                                               ident[0:TILES, 0:TILES])
                last.then_inc(s_prt, 1)

            @block.scalar
            def _(act):
                R = row[0:TILES]
                act.wait_ge(s_par, 160)
                nc.scalar.activation(R[:, 23, 2:4], R[:, 23, 0:2], ACT.Exp).then_inc(s_act, 1)
                act.wait_ge(s_lin, 2)
                nc.scalar.activation(R[:, 18, :], R[:, 3, :], ACT.Exp).then_inc(s_act, 1)
                act.wait_ge(s_lin, 10)
                nc.scalar.activation(R[:, 20, :], R[:, 5, :], ACT.Sin)
                nc.scalar.activation(R[:, 19, :], R[:, 6, :], ACT.Sin).then_inc(s_act, 1)
                for b in range(2):
                    act.wait_ge(slabs_used, g0 + 4 * b + 4)
                    for t in range(TT):
                        nc.scalar.copy(u_nat[:, t, b * NB:(b + 1) * NB], ps[2 * b + t][:, :]).then_inc(s_ua, 1)

            @block.vector
            def _(dve):
                R = row[0:TILES]
                v = nc.vector
                c = [0]

                def then(ins):
                    ins.then_inc(s_lin, 1)
                    c[0] += 1
                    dve.wait_ge(s_lin, c[0])
                dve.wait_ge(s_par, 160)
                dve.wait_ge(s_act, 1)
                dt = bc(R[:, 23, 2:4], 2, [TILES, 2, PS])
                for i in range(2):
                    then(v.tensor_tensor(R[:, 3 + i, :].rearrange("j (g p) -> j g p", g=2),
                                         R[:, i, :].rearrange("j (g p) -> j g p", g=2), dt, ALU.mult))
                two_pi = 2 * math.pi
                h1 = 6.28125
                h2 = float(np.float32(np.round((two_pi - h1) * 2 ** 21) / 2 ** 21))
                h3 = two_pi - h1 - h2
                then(v.tensor_scalar(R[:, 7, :], R[:, 4, :], 1.0 / two_pi, MAGIC, ALU.mult, ALU.add))
                then(v.tensor_scalar(R[:, 7, :], R[:, 7, :], MAGIC, None, ALU.subtract))
                then(v.scalar_tensor_tensor(R[:, 5, :], R[:, 7, :], -h1, R[:, 4, :], ALU.mult, ALU.add))
                then(v.scalar_tensor_tensor(R[:, 5, :], R[:, 7, :], -h2, R[:, 5, :], ALU.mult, ALU.add))
                then(v.scalar_tensor_tensor(R[:, 5, :], R[:, 7, :], -h3, R[:, 5, :], ALU.mult, ALU.add))
                then(v.tensor_scalar(R[:, 5, :], R[:, 5, :], math.pi - 1e-6, -(math.pi - 1e-6), ALU.min, ALU.max))
                then(v.scalar_tensor_tensor(R[:, 6, :], R[:, 5, :], -1.0, R[:, 5, :], ALU.mult, ALU.max))
                then(v.tensor_scalar(R[:, 6, :], R[:, 6, :], -1.0, math.pi / 2, ALU.mult, ALU.add))
                dve.wait_ge(s_act, 3)
                re, im = R[:, 0, :], R[:, 1, :]
                then(v.tensor_tensor(R[:, 8, :], R[:, 18, :], R[:, 19, :], ALU.mult))
                then(v.tensor_tensor(R[:, 9, :], R[:, 18, :], R[:, 20, :], ALU.mult))
                then(v.tensor_scalar(R[:, 8, :], R[:, 8, :], 1.0, None, ALU.subtract))
                then(v.tensor_tensor(R[:, 10, :], re, re, ALU.mult))
                then(v.tensor_tensor(R[:, 11, :], im, im, ALU.mult))
                then(v.tensor_tensor(R[:, 10, :], R[:, 10, :], R[:, 11, :], ALU.add))
                then(v.reciprocal(R[:, 10, :], R[:, 10, :]))
                for dst, (x0, y0, x1, y1, op) in ((16, (8, re, 9, im, ALU.add)), (17, (9, re, 8, im, ALU.subtract))):
                    then(v.tensor_tensor(R[:, 12, :], R[:, x0, :], y0, ALU.mult))
                    then(v.tensor_tensor(R[:, 13, :], R[:, x1, :], y1, ALU.mult))
                    then(v.tensor_tensor(R[:, 12, :], R[:, 12, :], R[:, 13, :], op))
                    ins = v.tensor_tensor(R[:, dst, :], R[:, 12, :], R[:, 10, :], ALU.mult)
                    if dst == 16:
                        then(ins)
                    else:
                        ins.then_inc(s_act, 1)
                dve.wait_ge(s_prt, 1)
                then(v.tensor_copy(prm, view(ps[5][:, 0:5 * TILES], [5, TILES])))
                f = [bc(prm[:, i, :], 2, [P, TILES, HG]) for i in range(2)]
                for i, op in ((0, ALU.subtract), (1, ALU.add)):
                    then(v.tensor_tensor(prod[0], b_raw[i], f[0], ALU.mult))
                    then(v.tensor_tensor(prod[1], b_raw[1 - i], f[1], ALU.mult))
                    then(v.tensor_tensor(bb[i], prod[0], prod[1], op))
                then(v.tensor_copy(powc[:, 0, :], prm[:, 3, :]))
                then(v.tensor_copy(pows[:, 0, :], prm[:, 4, :]))
                q0, q1 = prod[0][:, 0:2, :].rearrange("p a b -> p (a b)"), prod[1][:, 0:2, :].rearrange("p a b -> p (a b)")
                for n in range(1, NPOW):
                    then(v.tensor_tensor(q0, powc[:, n - 1, :], powc[:, n - 1, :], ALU.mult))
                    then(v.tensor_tensor(q1, pows[:, n - 1, :], pows[:, n - 1, :], ALU.mult))
                    then(v.tensor_tensor(powc[:, n, :], q0, q1, ALU.subtract))
                    then(v.scalar_tensor_tensor(pows[:, n, :], powc[:, n - 1, :], 2.0, pows[:, n - 1, :],
                                                ALU.mult, ALU.mult))
                dve.wait_ge(s_gpe, 1)
                for t in range(TT):
                    v.tensor_tensor(zg[:, t, :], ps[4][:, t * 8:t * 8 + 2 * H], gate_b, ALU.add)
                for n in range(4):
                    dve.wait_ge(s_upe, n + 1)
                    v.tensor_copy(uT[:, 2 * n:2 * n + 2, :].rearrange("p k t -> p (k t)"), ps[n][:, :])
        if stop <= 2:
            return halt(1)

        s_blk, s_bT, s_bTc = sem("s5_blocks"), sem("s5_b_transposed"), sem("s5_b_copied")
        s_blkc = sem("s5_c_blocks")
        s_cT, s_cTc = sem("s5_c_transposed"), sem("s5_c_copied")
        s_xp, s_rot, s_st, s_yp, s_yd = (sem("s5_inputs"), sem("s5_rotated"), sem("s5_states"), sem("s5_outputs"),
                                         sem("s5_outputs_taken"))
        s_proj, s_v5 = sem("qkvo_taken"), sem("s5_vector_step")
        g0 = first_slab[1]
        with nc.Block() as block:
            @block.sync
            def _(sp):
                stream(sp, 1)

            @block.tensor
            def _(pe):
                def b_transposes(c):
                    pe.wait_ge(s_blk, c + 1)
                    if c:
                        pe.wait_ge(s_bTc, 2 * c)
                    for i in range(2):
                        for b in range(TC):
                            last = nc.tensor.transpose(ps[4 + i][:, b * P:(b + 1) * P], blk_b[i][:, b, :], ident[:, :])
                    last.then_inc(s_bT, 1)

                b_transposes(0)
                for c in range(SC):
                    pe.wait_ge(s_bTc, 2 * c + 2)
                    if c:
                        pe.wait_ge(s_yd, c)
                        pe.wait_ge(s_cTc, 2 * c)
                    for i in range(2):
                        for b in range(TC):
                            last = nc.tensor.matmul(ps[2 * i + b // 2][:, (b % 2) * T:(b % 2 + 1) * T],
                                                    BT[i][:, b, :], uT[:, c, :], start=True, stop=True)
                    last.then_inc(s_xp, 1)
                    if c + 1 < SC:
                        b_transposes(c + 1)
                    if c:
                        pe.wait_ge(s_proj, 2 * c)
                    for j in range(4):
                        slab(pe, g0 + 4 * c + j, [(ps[6 + t][:, :], t) for t in range(TT)], left, 4 * j,
                             j == 0, j == 3)
                    pe.wait_ge(s_rot, c + 1)
                    pe.wait_ge(s_blkc, c + 1)
                    for i in range(2):
                        for b in range(TC):
                            last = nc.tensor.transpose(ps[1 + i][:, b * P:(b + 1) * P], blk_c[i][:, b, :], ident[:, :])
                    last.then_inc(s_cT, 1)
                    pe.wait_ge(s_cTc, 2 * c + 2)
                    pe.wait_ge(s_st, c + 1)
                    n = 0
                    for i, s in enumerate((w_re, w_im)):
                        for b in range(TC):
                            last = nc.tensor.matmul(ps[0][:, 0:T], CT[i][:, b, :], s[:, b, :],
                                                    start=n == 0, stop=n == 2 * TC - 1)
                            n += 1
                    last.then_inc(s_yp, 1)

            @block.scalar
            def _(act):
                def copy_b(c):
                    act.wait_ge(s_bT, c + 1)
                    if c:
                        act.wait_ge(s_xp, c)
                    for i in range(2):
                        nc.scalar.copy(BT[i].rearrange("p b q -> p (b q)"), ps[4 + i][:, :]).then_inc(s_bTc, 1)

                copy_b(0)
                for c in range(SC):
                    if c + 1 < SC:
                        copy_b(c + 1)
                    act.wait_ge(slabs_used, g0 + 4 * c + 4)
                    for t in range(TT):
                        if c < 4:
                            dst = nat[:, t, c * NB:(c + 1) * NB]
                        elif c < 6:
                            hs = NB // DH
                            dst = v_aug[:, t, (c - 4) * hs:(c - 3) * hs, 0:DH]
                        else:
                            dst = o_nat[:, t, (c - 6) * NB:(c - 5) * NB]
                        src = ps[6 + t][:, :]
                        if 4 <= c < 6:
                            src = view(src, [NB // DH, DH])
                        nc.scalar.copy(dst, src).then_inc(s_proj, 1)
                    act.wait_ge(s_cT, c + 1)
                    if c:
                        act.wait_ge(s_yp, c)
                    for i in range(2):
                        nc.scalar.copy(CT[i].rearrange("p b q -> p (b q)"), ps[1 + i][:, :]).then_inc(s_cTc, 1)

            @block.vector
            def _(dve):
                v = nc.vector
                n = [0]

                def then(ins):
                    ins.then_inc(s_v5, 1)
                    n[0] += 1
                    dve.wait_ge(s_v5, n[0])

                def blocks_b(c):
                    if c:
                        dve.wait_ge(s_bT, c)
                    for i in range(2):
                        dst = blk_b[i].rearrange("p b (g h) -> p b g h", g=GP)
                        last = v.tensor_tensor(dst, bc(bb[i][:, TC * c:TC * c + TC, :], 2, [P, TC, GP, HG]),
                                               bc(maskB, 3, [P, TC, GP, HG]), ALU.mult)
                    last.then_inc(s_blk, 1)

                def blocks_c(c):
                    if c:
                        dve.wait_ge(s_cT, c)
                    for i in range(2):
                        dst = blk_c[i].rearrange("p b (g q) -> p (b g) q", g=2)
                        last = v.scalar_tensor_tensor(dst, bc(c_nat[i][:, c, :], 1, [P, GP, PS]), 1.0 - 2.0 * i,
                                                      bc(maskG, 2, [P, GP, PS]), ALU.mult, ALU.mult)
                    last.then_inc(s_blkc, 1)

                def tables(c):
                    v.memset(tab_c[:, :, 0:1], 1.0)
                    then(v.memset(tab_s[:, :, 0:1], 0.0))
                    for m in range(NPOW):
                        k = 1 << m
                        cn = bc(powc[:, m, TC * c:TC * c + TC], 2, [P, TC, k])
                        sn = bc(pows[:, m, TC * c:TC * c + TC], 2, [P, TC, k])
                        lo, hi = (lambda x: x[:, :, 0:k]), (lambda x: x[:, :, k:2 * k])
                        v.tensor_tensor(hi(tab_c), lo(tab_c), cn, ALU.mult)
                        v.tensor_tensor(lo(tmp), lo(tab_s), sn, ALU.mult)
                        v.tensor_tensor(hi(tab_s), lo(tab_s), cn, ALU.mult)
                        then(v.tensor_tensor(hi(tmp), lo(tab_c), sn, ALU.mult))
                        v.tensor_tensor(hi(tab_c), hi(tab_c), lo(tmp), ALU.subtract)
                        then(v.tensor_tensor(hi(tab_s), hi(tab_s), hi(tmp), ALU.add))

                blocks_b(0)
                tables(0)
                then(v.memset(v_aug[:, :, :, DH:DH + 1], 1.0))
                for c in range(SC):
                    blocks_c(c)
                    if c + 1 < SC:
                        blocks_b(c + 1)
                    dve.wait_ge(s_xp, c + 1)
                    if c:
                        dve.wait_ge(s_yp, c)
                    x = [[view(ps[2 * i + q][:, :], [2, T]) for q in range(2)] for i in range(2)]
                    half = [slice(0, 2), slice(2, 4)]
                    for q in range(2):
                        v.tensor_tensor(w_re[:, half[q], :], x[0][q], tab_c[:, half[q], :], ALU.mult)
                        v.tensor_tensor(r_re[:, half[q], :], x[1][q], tab_s[:, half[q], :], ALU.mult)
                        v.tensor_tensor(w_im[:, half[q], :], x[1][q], tab_c[:, half[q], :], ALU.mult)
                        last = v.tensor_tensor(r_im[:, half[q], :], x[0][q], tab_s[:, half[q], :], ALU.mult)
                    then(last)
                    v.tensor_tensor(w_re, w_re, r_re, ALU.add).then_inc(s_rot, 1)
                    then(v.tensor_tensor(w_im, w_im, r_im, ALU.subtract))
                    for b in range(TC):
                        mag = prm[:, 2, TC * c + b:TC * c + b + 1].to_broadcast([P, T])
                        v.tensor_tensor_scan(r_re[:, b, :], mag, w_re[:, b, :], 0.0, ALU.mult, ALU.add)
                        last = v.tensor_tensor_scan(r_im[:, b, :], mag, w_im[:, b, :], 0.0, ALU.mult, ALU.add)
                    then(last)
                    v.tensor_tensor(w_re, r_re, tab_c, ALU.mult)
                    then(v.tensor_tensor(tmp, r_im, tab_s, ALU.mult))
                    then(v.tensor_tensor(w_re, w_re, tmp, ALU.subtract))
                    v.tensor_tensor(w_im, r_re, tab_s, ALU.mult)
                    then(v.tensor_tensor(tmp, r_im, tab_c, ALU.mult))
                    v.tensor_tensor(w_im, w_im, tmp, ALU.add).then_inc(s_st, 1)
                    if c + 1 < SC:
                        dve.wait_ge(s_st, c + 1)
                        tables(c + 1)
                    dve.wait_ge(s_yp, c + 1)
                    v.scalar_tensor_tensor(uT[:, c, :], uT[:, c, :], d_col[:, c:c + 1], ps[0][:, 0:T],
                                           ALU.mult, ALU.add).then_inc(s_yd, 1)
        if stop <= 3:
            return halt(2)

        scratch = Places(pool, s5_at)
        qkT = scratch.take(QC, T)
        raw = scratch.take(QC, CW - 1 + T)
        glu_blk = scratch.take(2, SC, P)
        cw_row = scratch.take(P)
        cw = scratch.take(CW, QC)
        gated_b = view(aT[:, 0:8, :].rearrange("p k t -> p (k t)"), [SC, T])
        s_cwl, s_gelu, s_glub = sem("conv_weights_landed"), sem("s5_gelu"), sem("glu_blocks")
        s_glu, s_sig, s_ys = sem("glu_products"), sem("glu_sigmoid"), sem("s5_done")
        s_cwT, s_cwc, s_halo = sem("conv_weights_transposed"), sem("conv_weights_copied"), sem("conv_halo")
        s_qkT, s_qkc, s_cstep, s_silu = sem("qk_transposed"), sem("qk_copied"), sem("conv_step"), sem("qk_done")
        s_og = sem("o_gate")
        with nc.Block() as block:
            @block.sync
            def _(sp):
                sp.dma_start(cw_row[0:CW * QC, :], a["conv_qk_w"][0].rearrange("i (c p) -> (i c) p", p=P))\
                  .then_inc(s_cwl, 16)

            @block.tensor
            def _(pe):
                pe.wait_ge(s_cwl, 16)
                nc.tensor.transpose(ps[6][:, 0:CW * QC], cw_row[0:CW * QC, :], ident[0:CW * QC, 0:CW * QC])\
                  .then_inc(s_cwT, 1)
                for n in range(8):
                    if n >= 4:
                        pe.wait_ge(s_qkc, n - 3)
                    for j in range(4):
                        c, t = 2 * n + j // 2, j % 2
                        last = nc.tensor.transpose(ps[n % 4][:, j * P:(j + 1) * P], nat[:, t, c * P:(c + 1) * P],
                                                   ident[:, :])
                    last.then_inc(s_qkT, 1)
                pe.wait_ge(s_gelu, 1)
                pe.wait_ge(s_glub, 1)
                for c in range(SC):
                    if c >= 2:
                        pe.wait_ge(s_ys, c - 1)
                    for i in range(2):
                        last = nc.tensor.matmul(ps[4 + c % 2][:, i * T:(i + 1) * T], glu_blk[:, i, c, :], uT[:, c, :],
                                                start=True, stop=True)
                    last.then_inc(s_glu, 1)

            @block.scalar
            def _(act):
                nc.scalar.activation(uT, uT, ACT.Gelu).then_inc(s_gelu, 1)
                for n in range(8):
                    act.wait_ge(s_qkT, n + 1)
                    nc.scalar.copy(raw[:, 2 * n:2 * n + 2, CW - 1:], view(ps[n % 4][:, :], [2, T])).then_inc(s_qkc, 1)
                for c in range(SC):
                    act.wait_ge(s_glu, c + 1)
                    nc.scalar.activation(gated_b[:, c, :], ps[4 + c % 2][:, T:2 * T], ACT.Sigmoid).then_inc(s_sig, 1)
                nc.scalar.activation(o_nat, o_nat, ACT.Sigmoid).then_inc(s_og, 1)
                for n in range(4):
                    act.wait_ge(s_cstep, 64 // 4 * (n + 1))
                    nc.scalar.activation(qkT[:, 4 * n:4 * n + 4, :], qkT[:, 4 * n:4 * n + 4, :], ACT.Silu)\
                      .then_inc(s_silu, 1)

            @block.vector
            def _(dve):
                v = nc.vector
                for i in range(2):
                    for c in range(SC):
                        last = v.tensor_tensor(view(glu_blk[:, i, c, :], [GP, HG]),
                                               bc(glu_nat[:, c, i * HG:(i + 1) * HG], 1, [P, GP, HG]),
                                               bc(maskG, 2, [P, GP, HG]), ALU.mult)
                last.then_inc(s_glub, 1)
                v.memset(raw[:, :, 0:CW - 1], 0.0).then_inc(s_halo, 1)
                dve.wait_ge(s_cwT, 1)
                v.tensor_copy(cw, view(ps[6][:, 0:CW * QC], [CW, QC])).then_inc(s_cwc, 1)
                dve.wait_ge(s_halo, 1)
                dve.wait_ge(s_cwc, 1)
                for n in range(QC // 4):
                    dve.wait_ge(s_qkc, 2 * n + 2)
                    for i in range(CW):
                        if n or i:
                            dve.wait_ge(s_cstep, 16 * n + 4 * i)
                        for c in range(4 * n, 4 * n + 4):
                            if i == 0:
                                ins = v.tensor_scalar(qkT[:, c, :], raw[:, c, 0:T], cw[:, 0, c:c + 1], None, ALU.mult)
                            else:
                                ins = v.scalar_tensor_tensor(qkT[:, c, :], raw[:, c, i:i + T], cw[:, i, c:c + 1],
                                                             qkT[:, c, :], ALU.mult, ALU.add)
                            ins.then_inc(s_cstep, 1)
                for c in range(SC):
                    dve.wait_ge(s_sig, c + 1)
                    v.tensor_tensor(uT[:, c, :], ps[4 + c % 2][:, 0:T], gated_b[:, c, :], ALU.mult).then_inc(s_ys, 1)
        if stop <= 4:
            return halt(2)

        R2 = TT * H
        kit = Places(aT[:, :, :].rearrange("p k t -> p (k t)"))
        bm = kit.take(R2, P)
        dg = kit.take(R2, P)
        kw = kit.take(H, DH)
        c0_at = Places(nat[:, :, :].rearrange("p t d -> p (t d)"))
        c0 = c0_at.take(H, DC, DH + 1)
        ng_row = c0_at.take(W)
        rawp = Places(pool, s5_at + QC * T)
        nd = rawp.take(R2, DH + 1)
        hm = rawp.take(TT, H, DH)
        cols_ = Places(small, 64)
        (lf, acum, atot, bcol, bmax, mt, minter, shift_, sint, eneg, t0, t1, ss, rr) = [cols_.take(R2) for _ in range(14)]
        bmax0, mloc, m0, wcol, snew = [cols_.take(H) for _ in range(5)]
        s_m, s_mf = sem("mlstm_vector_step"), sem("mlstm_functions")
        s_mp, s_mc, s_ngl = sem("mlstm_products"), sem("mlstm_copies"), sem("mlstm_gain_landed")
        s_nd, s_ndt, s_hmt = sem("mlstm_heads"), sem("mlstm_heads_taken"), sem("mlstm_transposed")
        with nc.Block() as block:
            @block.sync
            def _(sp):
                sp.dma_start(ng_row, a["mlstm_norm_g"][0].partition_broadcast(P)).then_inc(s_ngl, 16)

            m = {}

            @block.vector
            def _(dve):
                v = nc.vector
                n = [0]

                def then(ins, mark=None):
                    ins.then_inc(s_m, 1)
                    n[0] += 1
                    m[mark] = n[0]
                    dve.wait_ge(s_m, n[0])
                gi = zg[:, :, 0:H]
                gf = zg[:, :, H:2 * H]
                by = (lambda x: view(x, [TT, H]))
                then(v.scalar_tensor_tensor(by(t0), gf, -1.0, gf, ALU.mult, ALU.max), "abs")
                dve.wait_ge(s_mf, 2)
                then(v.scalar_tensor_tensor(by(lf), gf, 0.0, by(t1), ALU.min, ALU.subtract), "lf")
                dve.wait_ge(s_mp, 1)
                v.tensor_copy(acum, ps[6][:, 0:R2])
                then(v.tensor_copy(atot, ps[6][:, R2:2 * R2]))
                then(v.tensor_tensor(by(bcol), gi, by(acum), ALU.subtract))
                then(v.tensor_tensor(dg, bc(ident[:, :], 1, [P, R2, P]), bc(bcol, 2, [P, R2, P]), ALU.mult), "dg")
                dve.wait_ge(s_mp, 3)
                for c in range(TT):
                    v.tensor_tensor(bm[:, c * H:(c + 1) * H, :], view(ps[c][:, :], [H, P]),
                                    bc(causal[:, :], 1, [P, H, P]), ALU.add)
                then(v.tensor_reduce(bmax0, view(ps[0][:, :], [H, P]), AX, ALU.max))
                then(v.tensor_reduce(bmax, bm, AX, ALU.max))
                then(v.tensor_tensor(mloc, atot[:, 0:H], bmax0, ALU.add))
                then(v.tensor_tensor(m0, atot[:, 0:H], mloc, ALU.max))
                v.tensor_tensor(snew, mloc, m0, ALU.subtract)
                v.tensor_tensor(wcol, bcol[:, 0:H], bmax0, ALU.subtract)
                v.tensor_copy(minter[:, 0:H], acum[:, 0:H])
                v.tensor_tensor(minter[:, H:], acum[:, H:], m0, ALU.add)
                then(v.tensor_tensor(mt, acum, bmax, ALU.add))
                then(v.tensor_tensor(mt, mt, minter, ALU.max))
                v.tensor_tensor(sint, minter, mt, ALU.subtract)
                then(v.tensor_tensor(shift_, acum, mt, ALU.subtract))
                then(v.tensor_tensor(bm, bm, bc(shift_, 2, [P, R2, P]), ALU.add), "w")
                dve.wait_ge(s_mf, 3)
                then(v.tensor_tensor(wcol, wcol, snew, ALU.mult))
                for j in range(2):
                    src = view(ps[4 + j][:, :], [H // 2, DH])
                    last = v.tensor_tensor(kw[:, j * H // 2:(j + 1) * H // 2, :], src,
                                           bc(wcol[:, j * H // 2:(j + 1) * H // 2], 2, [P, H // 2, DH]), ALU.mult)
                then(last, "kw")
                dve.wait_ge(s_mf, 4)
                for c in range(TT):
                    last = v.scalar_tensor_tensor(bm[:, c * H:(c + 1) * H, :], view(ps[2 + c][:, :], [H, P]),
                                                  DH ** -0.5, bm[:, c * H:(c + 1) * H, :], ALU.mult, ALU.mult)
                then(last, "p")
                for k in range(H * DC):
                    dve.wait_ge(s_nd, k + 1)
                    v.tensor_copy(c0[:, k // DC, k % DC, :], ps[(6, 7, 4, 5)[k % 4]][:, 0:DH + 1]).then_inc(s_ndt, 1)
                dve.wait_ge(s_mp, 4)
                for c in range(TT):
                    last = v.tensor_copy(dg[:, c * H:(c + 1) * H, :], view(ps[c][:, :], [H, P]))
                then(last, "pt")
                v.tensor_scalar(sint, sint, DH ** -0.5, None, ALU.mult)
                for r in range(R2):
                    dve.wait_ge(s_nd, H * DC + r + 1)
                    last = v.tensor_copy(nd[:, r, :], ps[(2, 3)[r % 2]][:, 0:DH + 1])
                    last.then_inc(s_ndt, 1)
                dve.wait_ge(s_ndt, H * DC + R2)
                for h in range(H):
                    dve.wait_ge(s_nd, H * DC + R2 + h + 1)
                    last = v.scalar_tensor_tensor(nd[:, H + h, :], ps[4 + h][:, 0:DH + 1], sint[:, H + h:H + h + 1],
                                                  nd[:, H + h, :], ALU.mult, ALU.add)
                then(last)
                den = nd[:, :, DH:DH + 1].rearrange("p r o -> p (r o)")
                then(v.scalar_tensor_tensor(t0, den, -1.0, den, ALU.mult, ALU.max))
                then(v.tensor_tensor(t0, t0, eneg, ALU.max))
                then(v.reciprocal(t0, t0))
                hr = hm.rearrange("p c h d -> p (c h) d")
                then(v.tensor_tensor(hr, nd[:, :, 0:DH], bc(t0, 2, [P, R2, DH]), ALU.mult))
                sq = nd[:, :, 0:DH]
                then(v.tensor_tensor(sq, hr, hr, ALU.mult))
                then(v.tensor_reduce(ss, sq, AX, ALU.add))
                then(v.tensor_scalar(ss, ss, 1.0 / DH, EPS, ALU.mult, ALU.add), "sq")
                dve.wait_ge(s_mf, 5)
                then(v.reciprocal(rr, ss))
                then(v.tensor_tensor(hr, hr, bc(rr, 2, [P, R2, DH]), ALU.mult))
                dve.wait_ge(s_ngl, 16)
                hf = hm.rearrange("p c h d -> p c (h d)")
                then(v.tensor_tensor(hf, hf, bc(ng_row, 1, [P, TT, W]), ALU.mult))
                then(v.tensor_tensor(hf, hf, o_nat, ALU.mult), "h")

            @block.scalar
            def _(act):
                act.wait_ge(s_m, 1)
                nc.scalar.activation(t1, t0, ACT.Exp, scale=-1.0).then_inc(s_mf, 1)
                act.wait_ge(s_mf, 1)
                nc.scalar.activation(t1, t1, ACT.Ln, bias=1.0).then_inc(s_mf, 1)
                act.wait_ge(s_m, m["w"])
                nc.scalar.activation(wcol, wcol, ACT.Exp)
                nc.scalar.activation(snew, snew, ACT.Exp)
                nc.scalar.activation(sint, sint, ACT.Exp)
                nc.scalar.activation(eneg, mt, ACT.Exp, scale=-1.0).then_inc(s_mf, 1)
                nc.scalar.activation(bm, bm, ACT.Exp).then_inc(s_mf, 1)
                act.wait_ge(s_m, m["sq"])
                nc.scalar.activation(ss, ss, ACT.Sqrt).then_inc(s_mf, 1)
                for n in range(4):
                    act.wait_ge(s_hmt, n + 1)
                    nc.scalar.copy(mixT[:, 2 * n:2 * n + 2, :].rearrange("p k t -> p (k t)"), ps[n][:, :])\
                      .then_inc(s_mc, 1)

            @block.tensor
            def _(pe):
                pe.wait_ge(s_m, m["lf"])
                nc.tensor.matmul(ps[6][:, 0:R2], upto[:, :], lf, start=True, stop=True)
                nc.tensor.matmul(ps[6][:, R2:2 * R2], ones[:, :], lf, start=True, stop=True).then_inc(s_mp, 1)
                for c in range(TT):
                    for h in range(H):
                        for d in range(DC):
                            tok = slice(c * P, (c + 1) * P)
                            last = nc.tensor.matmul(ps[2 + c][:, h * P:(h + 1) * P], qkT[:, h * DC + d, tok],
                                                    qkT[:, QC // 2 + h * DC + d, tok], start=d == 0, stop=d == DC - 1)
                for j in range(QC // 2):
                    last = nc.tensor.transpose(ps[4 + j // 4][:, (j % 4) * P:(j % 4 + 1) * P],
                                               qkT[:, QC // 2 + j, 0:P], ident[:, :])
                last.then_inc(s_mp, 1)
                pe.wait_ge(s_m, m["dg"])
                for c in range(TT):
                    last = nc.tensor.matmul(ps[c][:, :], ones[:, :],
                                            dg[:, c * H:(c + 1) * H, :].rearrange("p a b -> p (a b)"),
                                            start=True, stop=True)
                last.then_inc(s_mp, 1)
                pe.wait_ge(s_m, m["kw"])
                for h in range(H):
                    for d in range(DC):
                        n = h * DC + d
                        b = (6, 7, 4, 5)[n % 4]
                        if n >= 4:
                            pe.wait_ge(s_ndt, n - 3)
                        nc.tensor.matmul(ps[b][:, 0:DH + 1], kw[:, h, d * P:(d + 1) * P], v_aug[:, 0, h, :],
                                         start=True, stop=True).then_inc(s_nd, 1)
                pe.wait_ge(s_m, m["p"])
                for c in range(TT):
                    for h in range(H):
                        last = nc.tensor.transpose(ps[c][:, h * P:(h + 1) * P], bm[:, c * H + h, :], ident[:, :])
                last.then_inc(s_mp, 1)
                pe.wait_ge(s_m, m["pt"])
                for r in range(R2):
                    b = (2, 3)[r % 2]
                    if r >= 2:
                        pe.wait_ge(s_ndt, 8 + r - 1)
                    nc.tensor.matmul(ps[b][:, 0:DH + 1], dg[:, r, :], v_aug[:, r // H, r % H, :],
                                     start=True, stop=True).then_inc(s_nd, 1)
                for h in range(H):
                    b = 4 + h
                    for d in range(DC):
                        last = nc.tensor.matmul(ps[b][:, 0:DH + 1], qkT[:, h * DC + d, P:2 * P], c0[:, h, d, :],
                                                start=d == 0, stop=d == DC - 1)
                    last.then_inc(s_nd, 1)
                pe.wait_ge(s_m, m["h"])
                for n in range(4):
                    for j in range(4):
                        k, t = 2 * n + j // 2, j % 2
                        last = nc.tensor.transpose(ps[n][:, j * P:(j + 1) * P],
                                                   hm[:, t, :, :].rearrange("p h d -> p (h d)")[:, k * P:(k + 1) * P],
                                                   ident[:, :])
                    last.then_inc(s_hmt, 1)
        if stop <= 5:
            return halt(2)

        def into_residual(name, sec, lhs):
            taken = sem(name + "_taken")
            s, g0 = SECTIONS[sec], first_slab[sec]
            with nc.Block() as block:
                @block.sync
                def _(sp):
                    stream(sp, sec)

                @block.tensor
                def _(pe):
                    linear(pe, sec, [taken], lhs)

                @block.vector
                def _(dve):
                    for b in range(s.blocks):
                        dve.wait_ge(slabs_used, g0 + 4 * (b + 1))
                        for t in range(TT):
                            dst = res[:, t, b * NB:(b + 1) * NB]
                            nc.vector.tensor_tensor(dst, ps[(b % 2) * TT + t][:, :], dst, ALU.add).then_inc(taken, 1)

        into_residual("w_out", 2, lambda k, t: mixT[:, k, t * P:(t + 1) * P])
        if stop <= 6:
            return halt(3)

        norm_phase("norm2", a["norm2_g"][0])

        place = Places(pool)
        GB = 8
        rows_ = [place.take(D) for _ in range(GB)]
        place_q = Places(pool)
        q_nat = place_q.take(TT, PH * 2 * HALF)
        cand = place.take(PH, TOPK * TOPK)
        hot = place.take(HK, TOPK)
        idx = place.take(TT, HK).bitcast(U32)
        gate = place.take(TT, HK)
        actv = place.take(TT, HK)
        top = place.take(2 * PH, TOPK)
        topi = place.take(2 * PH, TOPK)
        pos = place.take(2, HK)
        stage = small[:, 0:2 * GB].bitcast(U32)
        iota16 = small[:, 16:16 + TOPK]
        dots = small[:, 32:32 + GB]
        ccol = small[:, 40:40 + KD]
        skT = place.take(2, KEYS)
        modrow = view(aT[0:1, 0:4, :].rearrange("p k t -> p (k t)"), [2, NB])
        scores = view(aT[:, :, :].rearrange("p k t -> p (k t)"), [TT, 2 * PH, KEYS])
        sk_nat = view(rows_[4][:, 0:2 * KEYS], [2, HALF])

        def project_rows(name, sec, dst, more_sp=None):
            taken = [sem(name + "_taken_act"), sem(name + "_taken_dve")]
            s, g0 = SECTIONS[sec], first_slab[sec]
            with nc.Block() as block:
                @block.sync
                def _(sp):
                    if more_sp:
                        more_sp(sp)
                    stream(sp, sec)

                @block.tensor
                def _(pe):
                    linear(pe, sec, taken)

                def evac(eng, copy, t):
                    for b in range(s.blocks):
                        eng.wait_ge(slabs_used, g0 + 4 * (b + 1))
                        copy(dst(t, b), ps[(b % 2) * TT + t][:, :]).then_inc(taken[t], 1)

                @block.scalar
                def _(act):
                    evac(act, nc.scalar.copy, 0)

                @block.vector
                def _(dve):
                    evac(dve, nc.vector.tensor_copy, 1)

        s_cl, s_sk = sem("condition_landed"), sem("subkeys_landed")

        def peer_small(sp):
            sp.dma_start(ccol, a["c_2"][0].rearrange("(k p) -> p k", p=P), allow_slow_non_contiguous=True)\
              .then_inc(s_cl, 16)
            sp.dma_start(sk_nat, a["peer_subkeys"][0].rearrange("h k d -> k h d")).then_inc(s_sk, 16)
        project_rows("peer_q", 3, lambda t, b: q_nat[:, t, b * NB:(b + 1) * NB], peer_small)

        s_qT, s_qTc, s_sc = sem("peer_q_transposed"), sem("peer_q_copied"), sem("peer_scores")
        s_skT, s_skc, s_cs, s_io = sem("subkeys_transposed"), sem("subkeys_copied"), sem("condition_silu"), sem("iota_done")
        with nc.Block() as block:
            @block.gpsimd
            def _(g):
                g.iota(iota16, pattern=[[1, TOPK]], base=0, channel_multiplier=0,
                       allow_small_or_imprecise_dtypes=True).then_inc(s_io, 1)

            @block.tensor
            def _(pe):
                pe.wait_ge(s_sk, 16)
                for i in range(2):
                    last = nc.tensor.transpose(ps[7][:, i * P:(i + 1) * P], sk_nat[:, i, :], ident[:, :])
                last.then_inc(s_skT, 1)
                for n in range(8):
                    if n >= 4:
                        pe.wait_ge(s_qTc, n - 3)
                    for j in range(4):
                        k, t = 2 * n + j // 2, j % 2
                        last = nc.tensor.transpose(ps[n % 4][:, j * P:(j + 1) * P], q_nat[:, t, k * P:(k + 1) * P],
                                                   ident[:, :])
                    last.then_inc(s_qT, 1)
                pe.wait_ge(s_qTc, 8)
                pe.wait_ge(s_skc, 1)
                for t in range(TT):
                    for g in range(2 * PH):
                        last = nc.tensor.matmul(ps[4 * t + g // 4][:, (g % 4) * KEYS:(g % 4 + 1) * KEYS],
                                                left(g, t), skT[:, g % 2, :], start=True, stop=True)
                last.then_inc(s_sc, 1)

            @block.scalar
            def _(act):
                act.wait_ge(s_cl, 16)
                nc.scalar.activation(ccol, ccol, ACT.Silu).then_inc(s_cs, 1)
                for n in range(8):
                    act.wait_ge(s_qT, n + 1)
                    nc.scalar.copy(aT[:, 2 * n:2 * n + 2, :].rearrange("p k t -> p (k t)"), ps[n % 4][:, :])\
                      .then_inc(s_qTc, 1)
                act.wait_ge(s_sc, 1)
                for b in range(4, 8):
                    nc.scalar.copy(aT[:, 2 * b:2 * b + 2, :].rearrange("p k t -> p (k t)"), ps[b][:, :])

            @block.vector
            def _(dve):
                dve.wait_ge(s_skT, 1)
                nc.vector.tensor_copy(skT, view(ps[7][:, 0:2 * P], [2, P])).then_inc(s_skc, 1)
                dve.wait_ge(s_sc, 1)
                for b in range(4):
                    nc.vector.tensor_copy(aT[:, 2 * b:2 * b + 2, :].rearrange("p k t -> p (k t)"), ps[b][:, :])
        if stop <= 7:
            return halt(4)

        gsum = small[:, 64:64 + PH]
        mod = nc.dram_tensor("modulation", (NMOD * D,), F32, kind="Internal").ap()
        s_r, s_idx, s_e, s_g = sem("route_step"), sem("experts_known"), sem("gate_exponentials"), sem("activations")
        s_stage, s_free, s_turn = sem("indices_staged"), sem("rows_used"), sem("gathers_let_go")
        s_row = [sem(f"row_gathered{i}") for i in range(GB)]
        s_dv, s_gl, s_w = sem("dots_step"), sem("gelu_done"), sem("expert_weights")
        s_mtk, s_mout = sem("modulation_taken"), [sem(f"modulation_written{i}") for i in range(2)]
        s_mb, s_mba = sem("modulation_read_back"), sem("modulation_biased")
        g0 = first_slab[4]
        HB = HK // GB
        fsr = place.take(PH, TOPK)
        mod_sum = place.take(2, P)
        with nc.Block() as block:
            DV = {}

            @block.vector
            def _(dve):
                v = nc.vector
                n = [0]

                def then(ins):
                    ins.then_inc(s_r, 1)
                    n[0] += 1
                    dve.wait_ge(s_r, n[0])
                dve.wait_ge(s_io, 1)
                for t in range(TT):
                    for half in range(2):
                        o = slice(8 * half, 8 * half + 8)
                        for g in range(2 * PH):
                            last = v.max(top[:, g, o], scores[:, t, g, :])
                        then(last)
                        for g in range(2 * PH):
                            last = v.max_index(topi[:, g, o].bitcast(U32), top[:, g, o], scores[:, t, g, :])
                        then(last)
                        if half == 0:
                            for g in range(2 * PH):
                                last = v.match_replace(scores[:, t, g, :], top[:, g, o], scores[:, t, g, :], -3.0e38)
                            then(last)
                    pair_ = top.rearrange("p (h q) i -> p h q i", q=2)
                    then(v.tensor_tensor(cand.rearrange("p h (i j) -> p h i j", i=TOPK),
                                         bc(pair_[:, :, 0, :], 3, [P, PH, TOPK, TOPK]),
                                         bc(pair_[:, :, 1, :], 2, [P, PH, TOPK, TOPK]), ALU.add))
                    pu = pos.bitcast(U32)
                    for half in range(2):
                        for h in range(PH):
                            last = v.max(fsr[:, h, 8 * half:8 * half + 8], cand[:, h, :])
                        then(last)
                        for h in range(PH):
                            last = v.max_index(pu[:, 0, h * TOPK + 8 * half:h * TOPK + 8 * half + 8],
                                               fsr[:, h, 8 * half:8 * half + 8], cand[:, h, :])
                        then(last)
                        if half == 0:
                            for h in range(PH):
                                last = v.match_replace(cand[:, h, :], fsr[:, h, 0:8], cand[:, h, :], -3.0e38)
                            then(last)
                    gt = view(gate[:, t, :], [PH, TOPK])
                    v.tensor_tensor(gt, fsr, fsr[:, :, 0:1].to_broadcast([P, PH, TOPK]), ALU.subtract).then_inc(s_g, 1)
                    v.tensor_scalar(pu[:, 1, :], pu[:, 0, :], 15, None, ALU.bitwise_and)
                    then(v.tensor_scalar(pu[:, 0, :], pu[:, 0, :], 4, None, ALU.logical_shift_right))
                    v.tensor_copy(pos, pu)
                    then(v.tensor_copy(topi, topi.bitcast(U32)))
                    ti = topi.rearrange("p (h q) i -> p h q i", q=2)
                    for q in range(2):
                        then(v.tensor_tensor(hot, bc(pos[:, q, :], 2, [P, HK, TOPK]), bc(iota16, 1, [P, HK, TOPK]),
                                             ALU.is_equal))
                        hk = hot.rearrange("p (h k) i -> p h k i", h=PH)
                        then(v.tensor_tensor(hk, hk, bc(ti[:, :, q, :], 2, [P, PH, TOPK, TOPK]), ALU.mult))
                        then(v.tensor_reduce(pos[:, q, :], hot, AX, ALU.add))
                    v.scalar_tensor_tensor(idx[:, t, :], pos[:, 0, :], float(KEYS), pos[:, 1, :], ALU.mult, ALU.add)\
                     .then_inc(s_idx, 1)
                    dve.wait_ge(s_idx, t + 1)
                    dve.wait_ge(s_e, t + 1)
                    then(v.tensor_reduce(gsum, gt, AX, ALU.add))
                    then(v.reciprocal(gsum, gsum))
                    then(v.tensor_tensor(gt, gt, bc(gsum, 2, [P, PH, TOPK]), ALU.mult))
                for q in range(4):
                    t = q % 2
                    if q == 2:
                        dve.wait_ge(s_gl, TT)
                        then(v.tensor_tensor(actv, actv, gate, ALU.mult))
                    with dve.Fori(0, HB) as i:
                        at = bass.ds(i * GB, GB)
                        if q < 2:
                            for r in range(GB):
                                dve.wait_ge(s_row[r], i * 16 + 16 * (q * HB + 1))
                                v.tensor_tensor_reduce(out=rows_[r], in0=rows_[r], in1=nat[:, t, :], scale=1.0,
                                                       scalar=0.0, op0=ALU.mult, op1=ALU.add,
                                                       accum_out=dots[:, r:r + 1]).then_inc(s_free, 1)
                            dve.wait_ge(s_free, i * GB + (q * HK + GB))
                            v.tensor_copy(actv[:, t, at], dots).then_inc(s_dv, 1)
                            dve.wait_ge(s_dv, i + (q * HB + 1))
                        else:
                            for r in range(GB):
                                dve.wait_ge(s_row[r], i * 16 + 16 * (q * HB + 1))
                                dve.wait_ge(s_free, i * GB + (q * HK + r))
                                v.scalar_tensor_tensor(res[:, t, :], rows_[r], actv[:, t, bass.ds(i * GB + r, 1)], res[:, t, :],
                                                       ALU.mult, ALU.add).then_inc(s_free, 1)
                    DV[q] = (q + 1) * HB
                dve.wait_ge(s_mb, 32)
                v.tensor_tensor(mod_sum[0:NMOD * KD, 0, :], mod_sum[0:NMOD * KD, 0, :], mod_sum[0:NMOD * KD, 1, :],
                                ALU.add).then_inc(s_mba, 1)

            @block.gpsimd
            def _(g):
                def half(q, i, p, first):
                    t = q % 2
                    src = (a["peer_u"] if q < 2 else a["peer_v"])[0]
                    st = stage[:, p * GB:(p + 1) * GB]
                    g.tensor_copy(st, idx[:, t, bass.ds(i * (2 * GB) + p * GB, GB)]).then_inc(s_stage, 1)
                    for r in range(GB):
                        if r == 0:
                            g.wait_ge(s_stage, i * 2 + (q * HB + p + 1))
                        if not first:
                            g.wait_ge(s_free, i * (2 * GB) + (q * HK + p * GB + r + 1 - GB))
                        g.sem_inc(s_turn, 1)
                        g.indirect_dma_start(rows_[r], None, src, bass.IndirectOffsetOnAxis(st[:, r:r + 1], 0))\
                         .then_inc(s_row[r], 16)

                g.wait_ge(s_idx, TT)
                for q in range(4):
                    if q == 0:
                        half(0, 0, 0, True)
                        half(0, 0, 1, False)
                    with g.Fori(int(q == 0), HB // 2) as i:
                        half(q, i, 0, False)
                        half(q, i, 1, False)

            @block.sync
            def _(sp):
                stream(sp, 4)
                for p in range(2):
                    sp.wait_ge(s_mout[p], 16 * NMOD * OB // 2)
                sp.dma_start(mod_sum[0:NMOD * KD, 0, :], mod.rearrange("(r c) -> r c", c=P)).then_inc(s_mb, 16)
                sp.dma_start(mod_sum[0:NMOD * KD, 1, :], a["b_ada_2"][0].rearrange("(r c) -> r c", c=P)).then_inc(s_mb, 16)
                sp.wait_ge(s_mba, 1)
                sp.dma_start(mod.rearrange("(r c) -> r c", c=P), mod_sum[0:NMOD * KD, 0, :]).then_inc(s_mb, 16)
                sp.wait_ge(s_mb, 48)

            @block.tensor
            def _(pe):
                linear(pe, 4, [s_mtk], lambda k, t: ccol[:, k:k + 1], 1, (0, 1))

            @block.scalar
            def _(act):
                for t in range(TT):
                    act.wait_ge(s_g, t + 1)
                    nc.scalar.activation(gate[:, t, :], gate[:, t, :], ACT.Exp).then_inc(s_e, 1)
                act.wait_ge(s_idx, TT)

                def pair(i, first):
                    for p in range(2):
                        act.wait_ge(slabs_used, i * 8 + (g0 + 4 * p + 4))
                        if not first:
                            act.wait_ge(s_mout[p], i * 16)
                        nc.scalar.copy(modrow[:, p, :], ps[p][0:1, :]).then_inc(s_mtk, 1)
                        act.wait_ge(s_mtk, i * 2 + (p + 1))
                        act.dma_start(mod[bass.ds(i * (2 * NB) + p * NB, NB)].rearrange("(o n) -> o n", o=1),
                                      modrow[:, p, :]).then_inc(s_mout[p], 16)
                pair(0, True)
                with act.Fori(1, NMOD * OB // 2) as i:
                    pair(i, False)
                for t in range(TT):
                    act.wait_ge(s_dv, DV[t])
                    nc.scalar.activation(actv[:, t, :], actv[:, t, :], ACT.Gelu).then_inc(s_gl, 1)
        if stop <= 8:
            return halt(5)

        recycle()
        norm_phase("final1", a["final_g"], dst=res, transposed=False)
        mods = [mod[i * D:(i + 1) * D] for i in range(NMOD)]
        norm_phase("norm1b", a["norm1_gain_2"][0], mods[1], mods[0])
        if stop <= 9:
            return halt(5)

        DKH = 2 * SBH + 2 * DLH
        place = Places(pool)
        sb_v, dil_v = place.take(TT, SBW), place.take(TT, DLW)
        gla_v, gla_r = place.take(TT, GV), place.take(TT, GV)
        oT_at = place.at
        sb_qk, dil_qk, gla_qk = place.take(TT, 2 * SBW), place.take(TT, 2 * DLW), place.take(TT, 2 * GK)
        oT = view(pool[:, oT_at:oT_at + KD * T], [KD, T])
        work_at = oT_at + KD * T
        spare_at = place.at
        T2_at = POOL - KD * T
        T2 = Places(pool, T2_at)
        T1 = Places(nat[:, :, :].rearrange("p t d -> p (t d)"))
        sbT, gkT = T1.take(2 * SBH, T), T1.take(GH, T)
        dilT, gqT = T2.take(2 * DLH, T), T2.take(GH, T)
        keep = Places(small, 64)
        a_nat = keep.take(TT, GR)
        qk_ss = keep.take(TT, DKH)
        gains = keep.take(4)
        segments = [(sb_qk, 2 * SBW), (sb_v, SBW), (dil_qk, 2 * DLW), (dil_v, DLW), (gla_qk, 2 * GK), (gla_v, GV),
                    (gla_r, GV)]

        def pieces(b, t):
            at, out_, lo, hi = 0, [], b * NB, (b + 1) * NB
            for seg, w in segments:
                x, y = max(lo, at), min(hi, at + w)
                if x < y:
                    out_.append((seg[:, t, x - at:y - at], x - lo, y - x))
                at += w
            return out_

        s5_, g0 = SECTIONS[5], first_slab[5]
        wa = view(pool[:, spare_at:spare_at + KD * GR], [KD, GR])
        s_wa, s_ap, s_ac = sem("rank_columns_landed"), sem("rank_products"), sem("rank_copied")
        s_pt = [sem("mix_taken_act"), sem("mix_taken_dve")]
        with nc.Block() as block:
            @block.sync
            def _(sp):
                sp.dma_start(wa, w_in2[:, C_A:C_G].rearrange("(k p) n -> p k n", p=P)).then_inc(s_wa, 16)
                for i, nme in enumerate(("sb_q_gain_2", "sb_k_gain_2", "dil_q_gain_2", "dil_k_gain_2")):
                    sp.dma_start(gains[:, i:i + 1], a[nme][0].rearrange("(p o) -> p o", o=1)).then_inc(s_wa, 16)
                stream(sp, 5)
                sp.wait_ge(s_wa, 80)

            @block.tensor
            def _(pe):
                linear(pe, 5, s_pt)
                b = s5_.blocks - 1
                for t in range(TT):
                    pe.wait_ge(s_pt[t], b - 1)
                for j in range(4):
                    slab(pe, g0 + 4 * b + j, [(ps[t][:, :], t) for t in range(TT)], left, 4 * j, j == 0, j == 3)
                pe.wait_ge(s_wa, 80)
                for t in range(TT):
                    for k in range(KD):
                        last = nc.tensor.matmul(ps[4][:, t * GR:(t + 1) * GR], left(k, t), wa[:, k, :],
                                                start=k == 0, stop=k == KD - 1)
                last.then_inc(s_ap, 1)

            def evac(eng, copy, t):
                for b in range(s5_.blocks):
                    eng.wait_ge(slabs_used, g0 + 4 * (b + 1))
                    for dst, c0_, w in pieces(b, t):
                        last = copy(dst, ps[(b % 2) * TT + t][:, c0_:c0_ + w])
                    last.then_inc(s_pt[t], 1)

            @block.scalar
            def _(act):
                evac(act, nc.scalar.copy, 0)

            @block.vector
            def _(dve):
                evac(dve, nc.vector.tensor_copy, 1)
                dve.wait_ge(s_ap, 1)
                nc.vector.tensor_copy(a_nat, view(ps[4][:, 0:TT * GR], [TT, GR]))

        s_hs, s_hr, s_hn = sem("head_step"), sem("head_root"), sem("heads_normed")
        s_hT, s_hc = sem("heads_transposed"), [sem("heads_copied_act"), sem("heads_copied_dve")]
        sq = view(pool[:, spare_at:spare_at + 2 * SBW], [2 * SBH, HD])
        hmarks = {}
        heads = [(sb_qk, h, sbT, h, h // SBH) for h in range(2 * SBH)]
        heads += [(dil_qk, h, dilT, h, 2 + h // DLH) for h in range(2 * DLH)]
        heads += [(gla_qk, h, gqT if h < GH else gkT, h % GH, None) for h in range(2 * GH)]
        with nc.Block() as block:
            @block.vector
            def _(dve):
                v = nc.vector
                n = [0]

                def then(ins, mark=None):
                    ins.then_inc(s_hs, 1)
                    n[0] += 1
                    hmarks[mark] = n[0]
                    dve.wait_ge(s_hs, n[0])
                for t in range(TT):
                    for i, qk in enumerate((sb_qk, dil_qk)):
                        hv = view(qk[:, t, :], [2 * SBH, HD])
                        then(v.tensor_tensor(sq, hv, hv, ALU.mult))
                        then(v.tensor_reduce(qk_ss[:, t, i * 2 * SBH:(i + 1) * 2 * SBH], sq, AX, ALU.add))
                then(v.tensor_scalar(qk_ss, qk_ss, 1.0 / HD, EPS, ALU.mult, ALU.add), "ss")
                dve.wait_ge(s_hr, 1)
                then(v.reciprocal(qk_ss, qk_ss))
                for i, qk in enumerate((sb_qk, dil_qk)):
                    for t in range(TT):
                        hv = view(qk[:, t, :], [2 * SBH, HD])
                        last = v.tensor_tensor(hv, hv, bc(qk_ss[:, t, i * 2 * SBH:(i + 1) * 2 * SBH], 2,
                                                          [P, 2 * SBH, HD]), ALU.mult)
                    last.then_inc(s_hn, 1)
                for m in range(1, len(heads) // 2, 2):
                    dve.wait_ge(s_hT, m + 1)
                    for j in range(2):
                        _, _, dst, hh, gcol = heads[2 * m + j]
                        src = ps[m % 4][:, j * T:(j + 1) * T]
                        if gcol is None:
                            last = v.tensor_scalar(dst[:, hh, :], src, P ** -0.5 if dst is gqT else 1.0, None, ALU.mult)
                        else:
                            last = v.tensor_scalar(dst[:, hh, :], src, gains[:, gcol:gcol + 1], None, ALU.mult)
                    last.then_inc(s_hc[1], 1)

            @block.scalar
            def _(act):
                act.wait_ge(s_hs, hmarks["ss"])
                nc.scalar.activation(qk_ss, qk_ss, ACT.Sqrt).then_inc(s_hr, 1)
                for m in range(0, len(heads) // 2, 2):
                    act.wait_ge(s_hT, m + 1)
                    for j in range(2):
                        _, _, dst, hh, gcol = heads[2 * m + j]
                        src = ps[m % 4][:, j * T:(j + 1) * T]
                        if gcol is None:
                            last = nc.scalar.mul(dst[:, hh, :], src, P ** -0.5 if dst is gqT else 1.0)
                        else:
                            last = nc.scalar.mul(dst[:, hh, :], src, gains[:, gcol:gcol + 1])
                    last.then_inc(s_hc[0], 1)

            @block.tensor
            def _(pe):
                for m in range(len(heads) // 2):
                    src = heads[2 * m][0]
                    pe.wait_ge(s_hn, 1 if src is sb_qk else 2)
                    if m >= 4:
                        pe.wait_ge(s_hc[m % 2], (m - 4) // 2 + 1)
                    for j in range(4):
                        src, h, *_ = heads[2 * m + j // 2]
                        t = j % 2
                        last = nc.tensor.transpose(ps[m % 4][:, j * P:(j + 1) * P], src[:, t, h * P:(h + 1) * P],
                                                   ident[:, :])
                    last.then_inc(s_hT, 1)
        if stop <= 10:
            return halt(6)

        TC3 = 3 * P
        diag = [slice(0, P), slice(2 * P, TC3)]
        work = Places(pool, work_at)
        z, lb, lr = work.take(SBH, TC3), work.take(SBH, TC3), work.take(SBH, TC3)
        s_mk, s_sp, s_ss, s_sf, s_so, s_oc = (sem("stick_masks"), sem("stick_products"), sem("stick_step"),
                                              sem("stick_functions"), sem("stick_outputs"), sem("stick_copied"))
        sm = {}
        with nc.Block() as block:
            @block.gpsimd
            def _(g):
                g.memset(causal[:, :], 1.0).then_inc(s_mk, 1)
                g.memset(upto[:, :], 1.0).then_inc(s_mk, 1)
                g.wait_ge(s_mk, 2)
                g.affine_select(out=causal[:, :], in_=causal[:, :], compare_op=ALU.is_gt, fill=0.0, base=0,
                                pattern=[[1, P]], channel_multiplier=-1).then_inc(s_mk, 1)
                g.affine_select(out=upto[:, :], in_=upto[:, :], compare_op=ALU.is_gt, fill=0.0, base=0,
                                pattern=[[-1, P]], channel_multiplier=1).then_inc(s_mk, 1)

            @block.vector
            def _(dve):
                v = nc.vector
                n = [0]

                def then(ins, mark=None):
                    ins.then_inc(s_ss, 1)
                    n[0] += 1
                    sm[mark] = n[0]
                    dve.wait_ge(s_ss, n[0])
                dve.wait_ge(s_mk, 4)
                for h in range(SBH):
                    dve.wait_ge(s_sp, h + 1)
                    last = v.tensor_scalar(z[:, h, :], ps[h][:, 0:TC3], HD ** -0.5, None, ALU.mult)
                then(last)
                then(v.scalar_tensor_tensor(lr, z, -1.0, z, ALU.mult, ALU.max), "abs")
                dve.wait_ge(s_sf, 2)
                then(v.scalar_tensor_tensor(lb, z, 0.0, lr, ALU.min, ALU.subtract))
                then(v.tensor_scalar(z, z, -1.0, 0.0, ALU.mult, ALU.min))
                then(v.tensor_tensor(lr, z, lr, ALU.subtract))
                for d in diag:
                    last = v.tensor_tensor(lr[:, :, d], lr[:, :, d], bc(causal[:, :], 1, [P, SBH, P]), ALU.mult)
                then(last, "rest")
                for h in range(SBH):
                    dve.wait_ge(s_sp, SBH + h + 1)
                    last = v.tensor_tensor(lb[:, h, :], ps[h][:, 0:TC3], lb[:, h, :], ALU.add)
                then(last, "logw")
                dve.wait_ge(s_sf, 3)
                for d in diag:
                    last = v.tensor_tensor(lb[:, :, d], lb[:, :, d], bc(causal[:, :], 1, [P, SBH, P]), ALU.mult)
                then(last, "w")

            @block.scalar
            def _(act):
                act.wait_ge(s_ss, sm["abs"])
                nc.scalar.activation(lr, lr, ACT.Exp, scale=-1.0).then_inc(s_sf, 1)
                act.wait_ge(s_sf, 1)
                nc.scalar.activation(lr, lr, ACT.Ln, bias=1.0).then_inc(s_sf, 1)
                act.wait_ge(s_ss, sm["logw"])
                nc.scalar.activation(lb, lb, ACT.Exp).then_inc(s_sf, 1)
                for h in range(SBH):
                    act.wait_ge(s_so, h + 1)
                    nc.scalar.copy(oT[:, h, :], ps[h][:, 0:T])

            @block.tensor
            def _(pe):
                for h in range(SBH):
                    k = SBH + h
                    nc.tensor.matmul(ps[h][:, 0:T], sbT[:, k, 0:P], sbT[:, h, :], start=True, stop=True)
                    nc.tensor.matmul(ps[h][:, T:TC3], sbT[:, k, P:T], sbT[:, h, P:T], start=True, stop=True)\
                      .then_inc(s_sp, 1)
                pe.wait_ge(s_ss, sm["rest"])
                for h in range(SBH):
                    r = lr[:, h, :]
                    nc.tensor.matmul(ps[h][:, 0:P], upto[:, :], r[:, 0:P], start=True, stop=True)
                    nc.tensor.matmul(ps[h][:, P:T], upto[:, :], r[:, P:T], start=True, stop=False)
                    nc.tensor.matmul(ps[h][:, P:T], ones[:, :], r[:, T:TC3], start=False, stop=True)
                    nc.tensor.matmul(ps[h][:, T:TC3], upto[:, :], r[:, T:TC3], start=True, stop=True).then_inc(s_sp, 1)
                pe.wait_ge(s_ss, sm["w"])
                for h in range(SBH):
                    hd = slice(h * HD, (h + 1) * HD)
                    nc.tensor.matmul(ps[h][:, 0:P], sb_v[:, 0, hd], lb[:, h, 0:P], start=True, stop=True)
                    nc.tensor.matmul(ps[h][:, P:T], sb_v[:, 0, hd], lb[:, h, P:T], start=True, stop=False)
                    nc.tensor.matmul(ps[h][:, P:T], sb_v[:, 1, hd], lb[:, h, T:TC3], start=False, stop=True)\
                      .then_inc(s_so, 1)

        work = Places(pool, work_at)
        lg, pT = work.take(DLH, TC3), work.take(DLH, TC3)
        dist, dmask, dtmp = work.take(TC3), work.take(len(DILG), TC3), work.take(TC3)
        parts = [slice(0, P), slice(P, TC3)]
        dst_ = Places(small, 64 + TT * GR)
        dmax, dneg, dsum, dlse, dfac = [dst_.take(DLH, 2) for _ in range(5)]
        dm, dz = dst_.take(DHG, 2), dst_.take(DHG, 2)
        s_di, s_dp, s_ds, s_df, s_dt, s_do = (sem("dilated_distances"), sem("dilated_scores"), sem("dilated_step"),
                                              sem("dilated_functions"), sem("dilated_transposed"),
                                              sem("dilated_outputs"))
        slopes = [2.0 ** (-8.0 * (i + 1) / DLH) for i in range(DLH)]
        dk = {}
        with nc.Block() as block:
            @block.gpsimd
            def _(g):
                di = dist.bitcast(mybir.dt.int32)
                for c, d in enumerate(parts):
                    g.iota(di[:, d], pattern=[[-1, d.stop - d.start]], base=c * P, channel_multiplier=1).then_inc(s_di, 1)

            @block.vector
            def _(dve):
                v = nc.vector
                n = [0]

                def then(ins, mark=None):
                    ins.then_inc(s_ds, 1)
                    n[0] += 1
                    dk[mark] = n[0]
                    dve.wait_ge(s_ds, n[0])
                I32 = mybir.dt.int32
                dve.wait_ge(s_di, 2)
                for g, (window, dil) in enumerate(DILG):
                    dmi = dmask[:, g, :].bitcast(I32)
                    last = v.tensor_scalar(dmi, dist.bitcast(I32), dil - 1, None, ALU.bitwise_and)
                then(last)
                then(v.tensor_copy(dmask, dmask.bitcast(I32)))
                then(v.tensor_copy(dist, dist.bitcast(I32)))
                for g, (window, dil) in enumerate(DILG):
                    m_ = dmask[:, g, :]
                    then(v.tensor_scalar(m_, m_, 0.0, None, ALU.is_equal))
                    then(v.scalar_tensor_tensor(m_, dist, 0.0, m_, ALU.is_ge, ALU.mult))
                    then(v.scalar_tensor_tensor(m_, dist, float(window), m_, ALU.is_le, ALU.mult))
                    then(v.tensor_scalar(m_, m_, 1.0, -NEG, ALU.subtract, ALU.mult))
                for h in range(DLH):
                    then(v.scalar_tensor_tensor(dtmp, dist, -slopes[h], dmask[:, h // DHG, :], ALU.mult, ALU.add))
                    dve.wait_ge(s_dp, h + 1)
                    then(v.scalar_tensor_tensor(lg[:, h, :], ps[h][:, 0:TC3], HD ** -0.5, dtmp, ALU.mult, ALU.add))
                for c, d in enumerate(parts):
                    last = v.tensor_reduce(dmax[:, :, c], lg[:, :, d], AX, ALU.max)
                then(last)
                then(v.tensor_scalar(dneg, dmax, -1.0, None, ALU.mult), "max")
                dve.wait_ge(s_df, 2 * DLH + 1)
                then(v.tensor_tensor(dlse, dlse, dmax, ALU.add))
                g3 = (lambda x, g: x[:, g * DHG:(g + 1) * DHG, :])
                then(v.tensor_tensor(dm, g3(dlse, 0), g3(dlse, 1), ALU.max))
                then(v.tensor_tensor(dm, dm, g3(dlse, 2), ALU.max))
                for g in range(len(DILG)):
                    last = v.tensor_tensor(g3(dlse, g), g3(dlse, g), dm, ALU.subtract)
                then(last, "lse")
                dve.wait_ge(s_df, 2 * DLH + 2)
                then(v.tensor_tensor(dz, g3(dlse, 0), g3(dlse, 1), ALU.add))
                then(v.tensor_tensor(dz, dz, g3(dlse, 2), ALU.add))
                for g in range(len(DILG)):
                    last = v.tensor_tensor(g3(dfac, g), g3(dsum, g), dz, ALU.mult)
                then(last)
                then(v.reciprocal(dfac, dfac))
                then(v.tensor_tensor(dfac, dfac, dlse, ALU.mult))
                for c, d in enumerate(parts):
                    w = d.stop - d.start
                    last = v.tensor_tensor(lg[:, :, d], lg[:, :, d], dfac[:, :, c:c + 1].to_broadcast([P, DLH, w]),
                                           ALU.mult)
                then(last, "p")
                for h in range(DLH):
                    dve.wait_ge(s_dt, h + 1)
                    last = v.tensor_copy(pT[:, h, :], ps[h][:, 0:TC3])
                then(last, "pt")

            @block.scalar
            def _(act):
                act.wait_ge(s_ds, dk["max"])
                for h in range(DLH):
                    for c, d in enumerate(parts):
                        nc.scalar.activation(lg[:, h, d], lg[:, h, d], ACT.Exp, bias=dneg[:, h, c:c + 1],
                                             accum_out=dsum[:, h, c:c + 1]).then_inc(s_df, 1)
                act.wait_ge(s_df, 2 * DLH)
                nc.scalar.activation(dlse, dsum, ACT.Ln).then_inc(s_df, 1)
                act.wait_ge(s_ds, dk["lse"])
                nc.scalar.activation(dlse, dlse, ACT.Exp).then_inc(s_df, 1)
                for j in range(DHG):
                    act.wait_ge(s_do, j + 1)
                    nc.scalar.copy(oT[:, SBH + j, :], ps[6 + j][:, 0:T])

            @block.tensor
            def _(pe):
                for h in range(DLH):
                    k = DLH + h
                    nc.tensor.matmul(ps[h][:, 0:P], dilT[:, h, 0:P], dilT[:, k, 0:P], start=True, stop=True)
                    nc.tensor.matmul(ps[h][:, P:TC3], dilT[:, h, P:T], dilT[:, k, :], start=True, stop=True)\
                      .then_inc(s_dp, 1)
                pe.wait_ge(s_ds, dk["p"])
                for h in range(DLH):
                    for j in range(3):
                        last = nc.tensor.transpose(ps[h][:, j * P:(j + 1) * P], lg[:, h, j * P:(j + 1) * P], ident[:, :])
                    last.then_inc(s_dt, 1)
                pe.wait_ge(s_ds, dk["pt"])
                ng = len(DILG)
                for j in range(DHG):
                    for g in range(ng):
                        h = g * DHG + j
                        nc.tensor.matmul(ps[6 + j][:, 0:P], dil_v[:, 0, h * HD:(h + 1) * HD], pT[:, h, 0:P],
                                         start=g == 0, stop=g == ng - 1)
                    for g in range(ng):
                        h = g * DHG + j
                        nc.tensor.matmul(ps[6 + j][:, P:T], dil_v[:, 0, h * HD:(h + 1) * HD], pT[:, h, P:T],
                                         start=g == 0, stop=False)
                        last = nc.tensor.matmul(ps[6 + j][:, P:T], dil_v[:, 1, h * HD:(h + 1) * HD], pT[:, h, T:TC3],
                                                start=False, stop=g == ng - 1)
                    last.then_inc(s_do, 1)
        if stop <= 11:
            return halt(6)

        work = Places(pool, work_at)
        la, cum = work.take(TT, GK), work.take(GH, T)
        ee, qe, ke = work.take(GH, T), work.take(GH, T), work.take(GH, T)
        acc = work.take(TT, GH, P)
        off = work.take(GH, P)
        apart, lmask = work.take(P), work.take(P)
        mtmp = view(la.rearrange("p a b -> p (a b)"), [TT, GH, P])
        og_at = Places(pool, work_at + 2 * GH * T)
        og = og_at.take(TT, GV)
        ggain = T1.tensor[:, 0:GDV]
        LV = int(math.log2(T))
        gst = Places(small, 64 + TT * GR)
        gss = gst.take(TT * GH)
        s_gl_, s_gp, s_gs, s_gf, s_gT, s_gT2, s_gc = (sem("gla_landed"), sem("gla_products"), sem("gla_step"),
                                                      sem("gla_functions"), sem("gla_level_products"),
                                                      sem("gla_transposed"), sem("gla_copied"))
        s_gi = sem("gla_iota")
        gm = {}
        a_T = view(T1.tensor[:, GDV:GDV + T], [T])
        ga_w = view(T1.tensor[:, 2 * GDV:2 * GDV + GK], [GK])
        ga_b = view(T1.tensor[:, 2 * GDV + GK:2 * GDV + 2 * GK], [GK])
        with nc.Block() as block:
            @block.sync
            def _(sp):
                sp.dma_start(ga_w[0:GR, :], a["w_gla_a_2"][0]).then_inc(s_gl_, 16)
                sp.dma_start(ga_b, a["b_gla_a_2"][0].partition_broadcast(P)).then_inc(s_gl_, 16)
                sp.dma_start(ggain, a["gla_out_gain_2"][0].partition_broadcast(P)).then_inc(s_gl_, 16)

            @block.gpsimd
            def _(g):
                g.memset(upto[:, :], 1.0).then_inc(s_gi, 1)
                g.wait_ge(s_gi, 1)
                g.affine_select(out=upto[:, :], in_=upto[:, :], compare_op=ALU.is_ge, fill=0.0, base=0,
                                pattern=[[1, P]], channel_multiplier=-1).then_inc(s_gi, 1)
                I32 = mybir.dt.int32
                g.iota(apart.bitcast(I32), pattern=[[1, P]], base=0, channel_multiplier=0).then_inc(s_gi, 1)
                g.iota(lmask.bitcast(I32), pattern=[[0, P]], base=0, channel_multiplier=1).then_inc(s_gi, 1)

            @block.vector
            def _(dve):
                v = nc.vector
                n = [0]

                def then(ins, mark=None):
                    ins.then_inc(s_gs, 1)
                    n[0] += 1
                    gm[mark] = n[0]
                    dve.wait_ge(s_gs, n[0])
                I32 = mybir.dt.int32
                dve.wait_ge(s_gi, 4)
                then(v.tensor_tensor(apart.bitcast(I32), apart.bitcast(I32), lmask.bitcast(I32), ALU.bitwise_xor))
                then(v.tensor_copy(apart, apart.bitcast(I32)))
                then(v.scalar_tensor_tensor(apart, apart, 1.0, causal[:, :], ALU.add, ALU.mult))
                then(v.tensor_scalar(apart, apart, 1.0, None, ALU.subtract))
                dve.wait_ge(s_gp, 1)
                then(v.tensor_copy(a_T[0:GR, :], ps[0][0:GR, 0:T]), "aT")
                dve.wait_ge(s_gl_, 48)
                dve.wait_ge(s_gp, 2)
                for t in range(TT):
                    last = v.tensor_tensor(la[:, t, :], ps[1 + t][:, :], ga_b, ALU.add)
                then(last)
                e2 = view(ee.rearrange("p a b -> p (a b)"), [TT, GK])
                then(v.scalar_tensor_tensor(e2, la, -1.0, la, ALU.mult, ALU.max), "abs")
                dve.wait_ge(s_gf, 2)
                then(v.scalar_tensor_tensor(la, la, 0.0, e2, ALU.min, ALU.subtract))
                then(v.tensor_scalar(la, la, 1.0 / TAU, None, ALU.mult), "la")
                dve.wait_ge(s_gp, 3)
                for h in range(GH):
                    last = v.tensor_copy(cum[:, h, :], ps[3 + h // 2][:, (h % 2) * T:(h % 2 + 1) * T])
                then(last, "cum")
                for lv in range(LV + 1):
                    B = 1 << lv
                    if lv == 0:
                        dve.wait_ge(s_gT, 1)
                        for t in range(TT):
                            last = v.tensor_tensor(acc[:, t], view(ps[6 * 0 + t][:, :], [GH, P]),
                                                   bc(ident[:, :], 1, [P, GH, P]), ALU.mult)
                        then(last, "level0")
                        continue
                    cb = cum.rearrange("p h (n b) -> p (h n) b", b=B)
                    eb = ee.rearrange("p h (n b) -> p (h n) b", b=B)
                    then(v.tensor_tensor(eb, cb, cb[:, :, B // 2 - 1:B // 2].to_broadcast([P, GH * T // B, B]),
                                         ALU.subtract))
                    then(v.scalar_tensor_tensor(ee, ee, -1.0, ee, ALU.mult, ALU.min), f"diff{lv}")
                    dve.wait_ge(s_gf, 2 + lv)
                    v.tensor_tensor(qe, gqT, ee, ALU.mult)
                    then(v.tensor_tensor(ke, gkT, ee, ALU.mult), f"qk{lv}")
                    if lv < LV:
                        then(v.tensor_scalar(lmask, apart, float(B // 2), None, ALU.is_ge))
                        then(v.scalar_tensor_tensor(lmask, apart, float(B), lmask, ALU.is_lt, ALU.mult))
                        dve.wait_ge(s_gT, lv + 1)
                        for t in range(TT):
                            last = v.tensor_tensor(mtmp[:, t], view(ps[2 * (lv % 2) + t][:, :], [GH, P]),
                                                   bc(lmask, 1, [P, GH, P]), ALU.mult)
                        then(last)
                        then(v.tensor_tensor(acc, acc, mtmp, ALU.add), f"level{lv}")
                    else:
                        dve.wait_ge(s_gT, lv + 1)
                        then(v.tensor_copy(off, view(ps[2 * (lv % 2)][:, :], [GH, P])), "off")
                dve.wait_ge(s_gp, 4)
                for t in range(TT):
                    for j in range(2):
                        last = v.tensor_copy(og[:, t, j * NB:(j + 1) * NB], ps[4 + 2 * t + j][:, :])
                then(last, "og")
                ov = og.rearrange("p t (h e) -> p (t h) e", h=GH)
                sqv = view(cum.rearrange("p a b -> p (a b)"), [GH, GDV])
                for t in range(TT):
                    then(v.tensor_tensor(sqv, ov[:, t * GH:(t + 1) * GH, :], ov[:, t * GH:(t + 1) * GH, :], ALU.mult))
                    then(v.tensor_reduce(gss[:, t * GH:(t + 1) * GH], sqv, AX, ALU.add))
                then(v.tensor_scalar(gss, gss, 1.0 / GDV, EPS, ALU.mult, ALU.add), "ss")
                dve.wait_ge(s_gf, 2 + LV + 1)
                then(v.reciprocal(gss, gss))
                then(v.tensor_tensor(ov, ov, bc(gss, 2, [P, TT * GH, GDV]), ALU.mult))
                then(v.tensor_tensor(ov, ov, bc(ggain, 1, [P, TT * GH, GDV]), ALU.mult))
                dve.wait_ge(s_gf, 2 + LV + 2)
                then(v.tensor_tensor(og, og, gla_r, ALU.mult), "out")

            @block.scalar
            def _(act):
                e2 = ee
                act.wait_ge(s_gs, gm["abs"])
                nc.scalar.activation(e2, e2, ACT.Exp, scale=-1.0).then_inc(s_gf, 1)
                act.wait_ge(s_gf, 1)
                nc.scalar.activation(e2, e2, ACT.Ln, bias=1.0).then_inc(s_gf, 1)
                for lv in range(1, LV + 1):
                    act.wait_ge(s_gs, gm[f"diff{lv}"])
                    nc.scalar.activation(ee, ee, ACT.Exp).then_inc(s_gf, 1)
                act.wait_ge(s_gs, gm["ss"])
                nc.scalar.activation(gss, gss, ACT.Sqrt).then_inc(s_gf, 1)
                nc.scalar.activation(gla_r, gla_r, ACT.Silu).then_inc(s_gf, 1)
                for m in range(4):
                    act.wait_ge(s_gT2, m + 1)
                    k = SBH + DHG + 2 * m
                    nc.scalar.copy(oT[:, k:k + 2, :].rearrange("p k t -> p (k t)"), ps[m][:, :])

            @block.tensor
            def _(pe):
                for t in range(TT):
                    last = nc.tensor.transpose(ps[0][0:GR, t * P:(t + 1) * P], a_nat[:, t, :], ident[:, :])
                last.then_inc(s_gp, 1)
                pe.wait_ge(s_gs, gm["aT"])
                pe.wait_ge(s_gl_, 48)
                for t in range(TT):
                    last = nc.tensor.matmul(ps[1 + t][:, :], a_T[0:GR, t * P:(t + 1) * P], ga_w[0:GR, :],
                                            start=True, stop=True)
                last.then_inc(s_gp, 1)
                pe.wait_ge(s_gs, gm["la"])
                pe.wait_ge(s_gi, 2)
                for h in range(GH):
                    o, hs = ps[3 + h // 2], slice(h * P, (h + 1) * P)
                    c = (h % 2) * T
                    nc.tensor.matmul(o[:, c:c + P], la[:, 0, hs], upto[:, :], start=True, stop=True)
                    nc.tensor.matmul(o[:, c + P:c + T], la[:, 0, hs], ones[:, :], start=True, stop=False)
                    last = nc.tensor.matmul(o[:, c + P:c + T], la[:, 1, hs], upto[:, :], start=False, stop=True)
                last.then_inc(s_gp, 1)
                pe.wait_ge(s_gs, gm["cum"])
                for lv in range(LV + 1):
                    q, k = (gqT, gkT) if lv == 0 else (qe, ke)
                    if lv:
                        pe.wait_ge(s_gs, gm[f"qk{lv}"])
                    for t in range(TT if lv < LV else 1):
                        for h in range(GH):
                            js, is_ = slice(t * P, (t + 1) * P), slice(t * P, (t + 1) * P)
                            if lv == LV:
                                is_ = slice(P, T)
                            last = nc.tensor.matmul(ps[2 * (lv % 2) + t][:, h * P:(h + 1) * P], k[:, h, js], q[:, h, is_],
                                                    start=True, stop=True)
                    last.then_inc(s_gT, 1)
                pe.wait_ge(s_gs, gm["off"])
                for t in range(TT):
                    for h in range(GH):
                        o = ps[4 + 2 * t + h // 2][:, (h % 2) * GDV:(h % 2 + 1) * GDV]
                        last = nc.tensor.matmul(o, acc[:, t, h, :], gla_v[:, t, h * GDV:(h + 1) * GDV],
                                                start=True, stop=t == 0)
                        if t:
                            last = nc.tensor.matmul(o, off[:, h, :], gla_v[:, 0, h * GDV:(h + 1) * GDV],
                                                    start=False, stop=True)
                last.then_inc(s_gp, 1)
                pe.wait_ge(s_gs, gm["out"])
                for m in range(4):
                    for j in range(4):
                        k, t = 2 * m + j // 2, j % 2
                        last = nc.tensor.transpose(ps[m][:, j * P:(j + 1) * P], og[:, t, k * P:(k + 1) * P], ident[:, :])
                    last.then_inc(s_gT2, 1)
        if stop <= 12:
            return halt(6)

        y = nat
        work = Places(pool, work_at)
        sg = work.take(3, TT, NB)
        ytmp = work.take(TT, NB)
        g0 = first_slab[6]
        s_gd, s_ga = sem("gates_done"), sem("gated_steps")
        STEPS, USED = 5, (1, 2, 4)
        branch_bank = (4, 6, 4)
        with nc.Block() as block:
            @block.sync
            def _(sp):
                stream(sp, 6)

            @block.tensor
            def _(pe):
                for nb in range(OB):
                    for i in range(3):
                        m = 3 * nb + i
                        if m >= 2:
                            pe.wait_ge(s_gd, m - 1)
                        for j in range(4):
                            slab(pe, g0 + 16 * nb + 4 * i + j, [(ps[(m % 2) * TT + t][:, :], t) for t in range(TT)],
                                 left, 4 * j, j == 0, j == 3)
                    if nb:
                        pe.wait_ge(s_ga, STEPS * (nb - 1) + USED[2])
                    for j in range(4):
                        g = g0 + 16 * nb + 12 + j
                        pe.wait_ge(landed[g % SLOTS], reach[g])
                        for kk in range(KS):
                            i, k = br_chunks[KS * j + kk]
                            if i == 2 and k == 0:
                                pe.wait_ge(s_ga, STEPS * nb + USED[0])
                            for t in range(TT):
                                last = nc.tensor.matmul(ps[branch_bank[i] + t][:, :],
                                                        oT[:, KS * j + kk, t * P:(t + 1) * P],
                                                        ring[:, g % SLOTS, kk, :], start=k == 0,
                                                        stop=k == br_rows[i] - 1)
                        last.then_inc(slabs_used, 1)

            @block.scalar
            def _(act):
                for m in range(3 * OB):
                    nb, i = divmod(m, 3)
                    if nb:
                        act.wait_ge(s_ga, STEPS * (nb - 1) + USED[i])
                    act.wait_ge(slabs_used, g0 + 16 * nb + 4 * i + 4)
                    for t in range(TT):
                        last = nc.scalar.activation(sg[:, i, t, :], ps[(m % 2) * TT + t][:, :], ACT.Sigmoid)
                    last.then_inc(s_gd, 1)

            @block.vector
            def _(dve):
                v = nc.vector
                n = [0]

                def then(ins):
                    ins.then_inc(s_ga, 1)
                    n[0] += 1
                    dve.wait_ge(s_ga, n[0])
                for nb in range(OB):
                    dst = y[:, :, nb * NB:(nb + 1) * NB]
                    for i in range(3):
                        end = sum(br_rows[:i + 1]) - 1
                        dve.wait_ge(slabs_used, g0 + 16 * nb + 12 + end // KS + 1)
                        dve.wait_ge(s_gd, 3 * nb + i + 1)
                        for t in range(TT):
                            last = v.tensor_tensor((dst if i == 0 else ytmp)[:, t, :], ps[branch_bank[i] + t][:, :],
                                                   sg[:, i, t, :], ALU.mult)
                        then(last)
                        if i:
                            then(v.tensor_tensor(dst, dst, ytmp, ALU.add))
        if stop <= 13:
            return halt(7)

        def transposed(name, src):
            s_tr, s_ev = sem(name + "_transposed"), [sem(name + "_copied_act"), sem(name + "_copied_dve")]
            with nc.Block() as block:
                @block.tensor
                def _(pe):
                    for n in range(8):
                        if n >= 4:
                            pe.wait_ge(s_ev[n % 2], (n - 4) // 2 + 1)
                        for j in range(4):
                            k, t = 2 * n + j // 2, j % 2
                            last = nc.tensor.transpose(ps[n % 4][:, j * P:(j + 1) * P],
                                                       src[:, t, k * P:(k + 1) * P], ident[:, :])
                        last.then_inc(s_tr, 1)

                def evac(eng, copy, which):
                    for n in range(which, 8, 2):
                        eng.wait_ge(s_tr, n + 1)
                        copy(aT[:, 2 * n:2 * n + 2, :].rearrange("p k t -> p (k t)"), ps[n % 4][:, :])\
                            .then_inc(s_ev[which], 1)

                @block.scalar
                def _(act):
                    evac(act, nc.scalar.copy, 0)

                @block.vector
                def _(dve):
                    evac(dve, nc.vector.tensor_copy, 1)

        def gated_residual(name, sec, lhs, gate_row_src, at, store=False):
            place = Places(pool, at)
            gate_row, gtmp = place.take(D), place.take(2, TT, NB)
            s_row_, s_gr, s_gr2, s_st = (sem(name + "_gate_landed"), sem(name + "_gated"), sem(name + "_added"),
                                         sem(name + "_stored"))
            s, g0 = SECTIONS[sec], first_slab[sec]
            out_v = out[0].rearrange("(t p) d -> p t d", p=P)
            with nc.Block() as block:
                @block.sync
                def _(sp):
                    sp.dma_start(gate_row, gate_row_src.partition_broadcast(P)).then_inc(s_row_, 16)
                    stream(sp, sec)
                    if store:
                        for b in range(s.blocks):
                            sp.wait_ge(s_gr2, b + 1)
                            c = slice(b * NB, (b + 1) * NB)
                            sp.dma_start(out_v[:, :, c], res[:, :, c]).then_inc(s_st, 16)
                        sp.wait_ge(s_st, 16 * s.blocks)

                @block.tensor
                def _(pe):
                    for b in range(s.blocks):
                        if b >= 2:
                            pe.wait_ge(s_gr, b - 1)
                        for j in range(s.per):
                            slab(pe, g0 + s.per * b + j, [(ps[(b % 2) * TT + t][:, :], t) for t in range(TT)], lhs,
                                 KS * j, j == 0, j == s.per - 1)

                @block.vector
                def _(dve):
                    dve.wait_ge(s_row_, 16)
                    for b in range(s.blocks):
                        c = slice(b * NB, (b + 1) * NB)
                        dve.wait_ge(slabs_used, g0 + s.per * (b + 1))
                        for t in range(TT):
                            last = nc.vector.tensor_tensor(gtmp[:, b % 2, t, :], ps[(b % 2) * TT + t][:, :],
                                                           gate_row[:, c], ALU.mult)
                        last.then_inc(s_gr, 1)
                        dve.wait_ge(s_gr, b + 1)
                        nc.vector.tensor_tensor(res[:, :, c], res[:, :, c], gtmp[:, b % 2], ALU.add).then_inc(s_gr2, 1)

        transposed("y", nat)
        gated_residual("mixer", 7, left, mods[2], 0)
        if stop <= 14:
            return halt(8)
        norm_phase("norm2b", a["norm2_gain_2"][0], mods[4], mods[3])

        FC = FF // P
        place = Places(pool)
        hT = place.take(FC, T)
        silu_g, prod_ = place.take(TT, NB), place.take(TT, NB)
        g0 = first_slab[8]
        pairs = SECTIONS[8].blocks // 2
        s_fa, s_fu, s_fT, s_fc = sem("ffn_gates"), sem("ffn_products"), sem("ffn_transposed"), sem("ffn_copied")
        with nc.Block() as block:
            @block.sync
            def _(sp):
                with sp.Fori(1, pairs) as i:
                    for j in range(SLOTS):
                        sp.wait_ge(slabs_used, i * 8 + (g0 + j - SLOTS + 1))
                        src = a["w_ffn_in_2"][0][(j % 4) * KS * P:(j % 4 + 1) * KS * P,
                                                 bass.ds(i * NB + (j // 4) * FF, NB)]
                        slot = (g0 + j) % SLOTS
                        sp.dma_start(ring[:, slot, :, :], src.rearrange("(k p) n -> p k n", p=P))\
                          .then_inc(landed[slot], 16)
                for m in range(SLOTS):
                    issue(sp, 9, m, first_slab[9] + m)

            @block.tensor
            def _(pe):
                def transposes(i):
                    pe.wait_ge(s_fu, i * 1)
                    for k in range(4):
                        for t in range(TT):
                            last = nc.tensor.transpose(ps[4 + k // 2][:, (k % 2) * T + t * P:(k % 2) * T + (t + 1) * P],
                                                       prod_[:, t, k * P:(k + 1) * P], ident[:, :])
                    last.then_inc(s_fT, 1)

                def pair(i, first, second=False):
                    for p in range(2):
                        if not first:
                            if p == 0:
                                pe.wait_ge(s_fa, i * 1)
                            else:
                                if not second:
                                    pe.wait_ge(s_fc, i * 1 - 1)
                                transposes(i)
                        for j in range(4):
                            m = 4 * p + j
                            slot = (g0 + m) % SLOTS
                            pe.wait_ge(landed[slot], i * 16 + reach[g0 + m])
                            for k in range(KS):
                                for t in range(TT):
                                    last = nc.tensor.matmul(ps[2 * p + t][:, :], left(4 * j + k, t),
                                                            ring[:, slot, k, :], start=j + k == 0,
                                                            stop=j == 3 and k == KS - 1)
                            last.then_inc(slabs_used, 1)
                pair(0, True)
                pair(1, False, True)
                with pe.Fori(2, pairs) as i:
                    pair(i, False)
                pe.wait_ge(s_fc, pairs - 1)
                transposes(pairs)

            @block.scalar
            def _(act):
                def copies(i):
                    act.wait_ge(s_fT, i + 1)
                    for k in range(2):
                        last = nc.scalar.copy(hT[:, bass.ds(i * 4 + 2 * k, 2), :], view(ps[4 + k][:, :], [2, T]))
                    last.then_inc(s_fc, 1)

                def silu(i, first):
                    if not first:
                        act.wait_ge(s_fu, i * 1)
                    act.wait_ge(slabs_used, i * 8 + (g0 + 4))
                    for t in range(TT):
                        last = nc.scalar.activation(silu_g[:, t, :], ps[t][:, :], ACT.Silu)
                    last.then_inc(s_fa, 1)
                silu(0, True)
                with act.Fori(1, pairs) as i:
                    silu(i, False)
                    copies(i - 1)
                copies(pairs - 1)

            @block.vector
            def _(dve):
                def product(i, first):
                    dve.wait_ge(s_fa, i + 1)
                    dve.wait_ge(slabs_used, i * 8 + (g0 + 8))
                    if not first:
                        dve.wait_ge(s_fT, i * 1)
                    for t in range(TT):
                        last = nc.vector.tensor_tensor(prod_[:, t, :], silu_g[:, t, :], ps[2 + t][:, :], ALU.mult)
                    last.then_inc(s_fu, 1)
                product(0, True)
                with dve.Fori(1, pairs) as i:
                    product(i, False)
        if stop <= 15:
            return halt(9)
        gated_residual("ffn", 9, lambda k, t: hT[:, k, t * P:(t + 1) * P], mods[5], FC * T, store=True)


_INS = ["x", "norm1_g", "w_in", "b_gates", "conv_qk_w", "mlstm_norm_g", "s5_lambda_re", "s5_lambda_im", "s5_log_dt",
        "s5_b_re", "s5_b_im", "s5_c_re", "s5_c_im", "s5_d", "s5_glu_w", "w_out", "norm2_g", "peer_wq", "peer_subkeys",
        "peer_u", "peer_v", "final_g", "c_2", "w_ada_2", "b_ada_2", "norm1_gain_2", "norm2_gain_2", "w_in_2",
        "sb_q_gain_2", "sb_k_gain_2", "dil_q_gain_2", "dil_k_gain_2", "w_gla_a_2", "b_gla_a_2", "gla_out_gain_2",
        "w_br_sb_2", "w_br_dil_2", "w_br_gla_2", "w_out_2", "w_ffn_in_2", "w_ffn_out_2"]


def kernel(**inputs):
    import numpy as _np
    import concourse.bacc as _bacc
    from concourse import mybir as _mybir
    from concourse.bass_utils import run_bass_kernel_spmd as _run

    nc = _bacc.Bacc("TRN2", target_bir_lowering=False, num_devices=1)
    arrays, args = {}, {}
    for name in _INS:
        v = _np.ascontiguousarray(inputs[name])
        arrays[f"in_{name}"] = v
        args[name] = nc.dram_tensor(f"in_{name}", v.shape, _mybir.dt.from_np(v.dtype), kind="ExternalInput").ap()
    x = inputs["x"]
    out = nc.dram_tensor("out", x.shape, _mybir.dt.float32, kind="ExternalOutput").ap()
    build(nc, args, out)
    r = _run(nc, [arrays], core_ids=[0])
    return r.results[0]["out"]
```

```python
import math
from contextlib import ExitStack

import numpy as np

import concourse.bass as bass
from concourse import mybir
from concourse.alu_op_type import AluOpType as ALU

F32 = mybir.dt.float32
F32R = mybir.dt.float32r
U32 = mybir.dt.uint32
ACT = mybir.ActivationFunctionType
AX = mybir.AxisListType.X

P = 128
NB = 512
KS = 4
SLOTS = 4
PARTS = 2
NEG = -1.0e30
MAGIC = 1.5 * 2.0 ** 23


def bc(ap, axis, shape):
    return ap.unsqueeze(axis).to_broadcast(shape)


def build(nc, a, out, stop=99):
    T, D = a["x"].shape[1:]
    TT = T // P
    KD = D // P
    EPS = 1e-6
    W = a["mlstm_norm_g"].shape[1]
    H = a["b_gates"].shape[1] // 2
    DH = W // H
    DC = DH // P
    G, PS, HG = a["s5_b_re"].shape[1:]
    SC = G * HG // P
    GP = P // HG
    TILES = G * PS // P
    TC = TILES // SC
    CW = a["conv_qk_w"].shape[1]
    QC = 2 * W // P
    KEYS, HALF = a["peer_subkeys"].shape[2:]
    PH = a["peer_wq"].shape[2] // (2 * HALF)
    TOPK = 16
    HK = PH * TOPK
    HD = a["sb_q_gain_2"].shape[1]
    SBW = a["w_br_sb_2"].shape[1]
    SBH = SBW // HD
    DILG = ((128, 1), (512, 4), (2048, 16))
    DHG = a["w_br_dil_2"].shape[1] // HD
    DLH = DHG * len(DILG)
    DLW = DLH * HD
    GV = a["w_br_gla_2"].shape[1]
    GK = a["w_gla_a_2"].shape[2]
    GR = a["w_gla_a_2"].shape[1]
    GH = GK // P
    GDV = GV // GH
    TAU = 16.0
    FF = a["w_ffn_out_2"].shape[1]
    NMOD = 6
    assert TT == 2 and HD == P and TC * SC == TILES and PS * 2 == P

    ctx = ExitStack()
    with ctx:
        def sb(name, shape, dt=F32):
            return ctx.enter_context(nc.sbuf_tensor(name, shape, dt))

        phase_sems = []

        def sem(name):
            phase_sems.append(nc.alloc_semaphore(name=name))
            return phase_sems[-1]

        def recycle():
            nc.clear_and_free_semaphores(phase_sems)
            nc.all_engine_barrier()
            phase_sems.clear()

        ps = [ctx.enter_context(nc.psum_tensor(f"bank{i}", [P, NB], F32)) for i in range(8)]
        ARENA = (nc.sbuf_usable_end - nc.sbuf_base) // 128 * 32
        base = (nc.sbuf_base + 127) // 128 * 128
        if base + 4 * ARENA > nc.sbuf_usable_end:
            ARENA -= 32
        taken_at = [0]

        def place_at(name, words, dt=F32, at=None):
            if at is None:
                at = taken_at[0]
                taken_at[0] += words
            assert at + words <= ARENA, (name, at + words - ARENA)
            return nc.alloc_sbuf_tensor_at(name, [P, words], dt, offset=base + 4 * at), at

        SLAB = KS * NB
        ring_, _ = place_at("ring", SLOTS * SLAB)
        high_, parts_at = place_at("slab_high", PARTS * SLAB, F32R)
        low_, _ = place_at("slab_low", PARTS * SLAB, F32R)
        parts_, _ = place_at("parts_scratch", 2 * PARTS * SLAB, F32, parts_at)
        res_, _ = place_at("res", TT * D)
        aTh_, aT_at = place_at("left_high", KD * T, F32R)
        aTl_, _ = place_at("left_low", KD * T, F32R)
        aTs, _ = place_at("left_scratch", 2 * KD * T, F32, aT_at)
        ident, _ = place_at("ident", P)
        ones, _ = place_at("ones", P)
        upto, _ = place_at("upto", P)
        causal, _ = place_at("causal", P)
        small, _ = place_at("small", 256)
        POOL = ARENA - taken_at[0] - TT * D
        pool, pool_at = place_at("pool", POOL)
        nat_, _ = place_at("nat", TT * D)

        def view(ap, shape):
            names = "abcd"[:len(shape)]
            return ap.rearrange(f"p ({' '.join(names)}) -> p {' '.join(names)}", **dict(zip(names, shape)))

        ring = ring_[:, :].rearrange("p (s k n) -> p s k n", s=SLOTS, k=KS)
        high = high_[:, :].rearrange("p (s k n) -> p s k n", s=PARTS, k=KS)
        low = low_[:, :].rearrange("p (s k n) -> p s k n", s=PARTS, k=KS)
        res, nat = view(res_[:, :], [TT, D]), view(nat_[:, :], [TT, D])
        aTh, aTl = view(aTh_[:, :], [KD, T]), view(aTl_[:, :], [KD, T])

        class Places:

            def __init__(self, tensor, at=0):
                self.tensor, self.at = tensor, at

            def take(self, *shape):
                n = int(np.prod(shape))
                ap = self.tensor[:, self.at:self.at + n]
                self.at += n
                assert self.at <= self.tensor.shape[1], self.at
                return view(ap, shape) if len(shape) > 1 else ap

        landed = [ctx.enter_context(nc.semaphore(f"slab_landed{i}")) for i in range(SLOTS)]
        slabs_used = ctx.enter_context(nc.semaphore("slabs_used"))
        high_done = ctx.enter_context(nc.semaphore("slab_high_parts"))
        low_done = ctx.enter_context(nc.semaphore("slab_low_parts"))

        def cols(w, k0, c0, n=NB, ks=KS):
            return w[k0 * P:(k0 + ks) * P, c0:c0 + n].rearrange("(k p) n -> p k n", p=P) if isinstance(c0, int) \
                else w[k0 * P:(k0 + ks) * P, bass.ds(c0, n)].rearrange("(k p) n -> p k n", p=P)

        class Section:

            def __init__(self, blocks, per, source):
                self.blocks, self.per, self.source = blocks, per, source
                self.n = blocks * per

        w_in, w_in2 = a["w_in"][0], a["w_in_2"][0]
        C_GATES, C_U = 4 * W, 4 * W + 2 * H
        C_A = 3 * SBW + 3 * DLW + 2 * GK + 2 * GV
        C_G = C_A + GR
        OB = D // NB

        def plain(w, c0=0):
            return lambda b, s: [(0, KS, cols(w, KS * s, c0 + b * NB))]

        br = [a["w_br_sb_2"][0], a["w_br_dil_2"][0], a["w_br_gla_2"][0]]
        br_rows = [w.shape[0] // P for w in br]
        br_chunks = [(i, k) for i in range(3) for k in range(br_rows[i])]

        def gated(b, s):
            n, part = divmod(b, 4)
            if part < 3:
                return [(0, KS, cols(w_in2, KS * s, C_G + part * D + n * NB))]
            parts, todo = [], br_chunks[KS * s:KS * s + KS]
            for i in range(3):
                ks = [k for j, k in todo if j == i]
                if ks:
                    parts.append((todo.index((i, ks[0])), len(ks), cols(br[i], ks[0], n * NB, ks=len(ks))))
            return parts

        def ffn_pairs(b, s):
            i, odd = (b // 2, b % 2) if isinstance(b, int) else b
            return [(0, KS, cols(a["w_ffn_in_2"][0], KS * s, i * NB + odd * FF))]

        MODA = 2 * OB
        (U_, QKVO, W_OUT, PEER_Q, ADA_A, MIX, ADA_B, GATES, W_OUT2, FFN_IN, FFN_OUT) = range(11)
        SECTIONS = [
            Section(2, 4, plain(w_in, C_U)),
            Section(4 * W // NB, 4, plain(w_in)),
            Section(OB, 4, plain(a["w_out"][0])),
            Section(PH * 2 * HALF // NB, 4, plain(a["peer_wq"][0])),
            Section(MODA, 4, plain(a["w_ada_2"][0])),
            Section(C_A // NB, 4, plain(w_in2)),
            Section(NMOD * OB - MODA, 4, plain(a["w_ada_2"][0], MODA * NB)),
            Section(4 * OB, 4, gated),
            Section(OB, 4, plain(a["w_out_2"][0])),
            Section(2 * FF // NB, 4, ffn_pairs),
            Section(OB, FF // P // KS, plain(a["w_ffn_out_2"][0])),
        ]
        first_slab = [0]
        for s in SECTIONS:
            first_slab.append(first_slab[-1] + s.n)

        WHOLE = (ADA_A, ADA_B)

        def is_whole(g):
            return any(first_slab[sec] <= g < first_slab[sec + 1] for sec in WHOLE)

        def split_index(g):
            return g - sum(min(max(g - first_slab[sec], 0), SECTIONS[sec].n) for sec in WHOLE)

        def slot_free(sp, g):
            old = g - SLOTS
            if old >= 0:
                if is_whole(old):
                    sp.wait_ge(slabs_used, old + 1)
                else:
                    sp.wait_ge(low_done, split_index(old) + 1)

        def issue(sp, sec, n, g):
            s = SECTIONS[sec]
            slot_free(sp, g)
            for k0, ks, src in s.source(n // s.per, n % s.per):
                sp.dma_start(ring[:, g % SLOTS, k0:k0 + ks, :], src).then_inc(landed[g % SLOTS], 16)

        transfers, reach = [0] * SLOTS, []
        for s in SECTIONS:
            for n in range(s.n):
                g = len(reach)
                count = len(gated(n // 4, n % 4)) if s.source is gated else 1
                transfers[g % SLOTS] += 16 * count
                reach.append(transfers[g % SLOTS])

        def stream(sp, sec):
            s, g0 = SECTIONS[sec], first_slab[sec]
            n = SLOTS
            if s.source is not gated and s.per == 4 and s.n // 8 > 1:
                for m in range(SLOTS, 8):
                    issue(sp, sec, m, g0 + m)
                free, off = (slabs_used, 0) if sec in WHOLE else (low_done, g0 - split_index(g0))
                with sp.Fori(1, s.n // 8) as i:
                    for j in range(8):
                        sp.wait_ge(free, i * 8 + (g0 + j - SLOTS + 1 - off))
                        (k0, ks, src), = s.source((i, j // 4) if s.source is ffn_pairs else i * 2 + j // 4, j % 4)
                        slot = (g0 + j) % SLOTS
                        sp.dma_start(ring[:, slot, :, :], src).then_inc(landed[slot], 16)
                n = s.n // 8 * 8
            for m in range(n, s.n):
                issue(sp, sec, m, g0 + m)
            if sec + 1 < len(SECTIONS):
                for m in range(min(SLOTS, SECTIONS[sec + 1].n)):
                    issue(sp, sec + 1, m, first_slab[sec + 1] + m)

        def stream_on(sp, g, end):
            for m in range(g + SLOTS, end + SLOTS):
                sec = max(i for i in range(len(SECTIONS)) if first_slab[i] <= m)
                issue(sp, sec, m - first_slab[sec], m)

        def slab(pe, g, outs, lhs, k0, start, stop):
            pe.wait_ge(low_done, split_index(g) + 1)
            last = slab_products(split_index(g) % PARTS, outs, lhs, k0, start, stop)
            last.then_inc(slabs_used, 1)

        def slab_products(part, outs, lhs, k0, start, stop, ks=range(KS)):
            for k in ks:
                for o, t in outs:
                    lh, ll = lhs(k0 + k, t)
                    first, final = start and k == 0, stop and k == KS - 1
                    nc.tensor.matmul(o, lh, high[:, part, k, :], start=first, stop=False)
                    nc.tensor.matmul(o, lh, low[:, part, k, :], start=False, stop=False)
                    last = nc.tensor.matmul(o, ll, high[:, part, k, :], start=False, stop=final)
            return last

        def left(k, t):
            return aTh[:, k, t * P:(t + 1) * P], aTl[:, k, t * P:(t + 1) * P]

        def high_part(act, g, i=None):
            n, up = split_index(g), 0 if i is None else i * 8
            act.wait_ge(landed[g % SLOTS], reach[g] if i is None else i * 32 + reach[g])
            if g >= PARTS or i is not None:
                act.wait_ge(slabs_used, up + (g - PARTS + 1))
            nc.scalar.copy(high[:, n % PARTS], ring[:, g % SLOTS]).then_inc(high_done, 1)

        def low_part(eng, g, i=None):
            n, up = split_index(g), 0 if i is None else i * 8
            eng.wait_ge(high_done, up + (n + 1))
            eng.tensor_tensor(low[:, n % PARTS], ring[:, g % SLOTS], high[:, n % PARTS].bitcast(F32), ALU.subtract)\
               .then_inc(low_done, 1)

        def high_blocks(act, sec, evac):
            s, g0 = SECTIONS[sec], first_slab[sec]
            for m in range(s.n):
                if m % s.per == 2 and m >= s.per:
                    evac(m // s.per - 1)
                high_part(act, g0 + m)
            evac(s.blocks - 1)

        def low_blocks(eng, sec, evac):
            s, g0 = SECTIONS[sec], first_slab[sec]
            for m in range(s.n):
                if m % s.per == 2 and m >= s.per:
                    evac(m // s.per - 1)
                low_part(eng, g0 + m)
            evac(s.blocks - 1)

        def linear(pe, sec, taken, lhs=left):
            s, g0 = SECTIONS[sec], first_slab[sec]
            n0 = split_index(g0)

            def pair(i, first):
                for p in range(2):
                    if not first:
                        for t in taken:
                            each = TT // len(taken)
                            pe.wait_ge(t, i * 2 * each + (p - 1) * each)
                    for j in range(KD // KS):
                        m = p * (KD // KS) + j
                        pe.wait_ge(low_done, i * 8 + (n0 + m + 1))
                        last = slab_products((n0 + m) % PARTS, [(ps[p * TT + t][:, :], t) for t in range(TT)], lhs,
                                             j * KS, j == 0, j == KD // KS - 1)
                        last.then_inc(slabs_used, 1)
            pair(0, True)
            if s.blocks // 2 > 1:
                with pe.Fori(1, s.blocks // 2) as i:
                    pair(i, False)

        def whole_linear(pe, sec, taken, lhs):
            s, g0 = SECTIONS[sec], first_slab[sec]

            def pair(i, first):
                for p in range(2):
                    if not first:
                        pe.wait_ge(taken, i * 2 + (p - 1))
                    for j in range(KD // KS):
                        m = p * (KD // KS) + j
                        slot = (g0 + m) % SLOTS
                        pe.wait_ge(landed[slot], i * 32 + reach[g0 + m])
                        for k in range(KS):
                            last = nc.tensor.matmul(ps[p][0:1, :], lhs(j * KS + k), ring[:, slot, k, :],
                                                    start=j + k == 0, stop=j * KS + k == KD - 1)
                        last.then_inc(slabs_used, 1)
            pair(0, True)
            with pe.Fori(1, s.blocks // 2) as i:
                pair(i, False)

        def high_left(n, b):
            return nc.scalar.copy(aTh[:, 2 * n:2 * n + 2, :].rearrange("p k t -> p (k t)"), ps[b][:, :])

        def low_left(n, b):
            c = slice(2 * n, 2 * n + 2)
            return nc.vector.tensor_tensor(aTl[:, c, :].rearrange("p k t -> p (k t)"), ps[b][:, :],
                                           aTh[:, c, :].rearrange("p k t -> p (k t)").bitcast(F32), ALU.subtract)

        def halt(sec, used=0):
            last = first_slab[sec] + used + SLOTS
            with nc.Block() as block:
                @block.sync
                def _(sp):
                    for g in range(max(0, last - SLOTS), last):
                        sp.wait_ge(landed[g % SLOTS], reach[g])

        maskG = small[:, 0:GP]
        maskB = view(small[:, 8:8 + TC * GP], [TC, GP])
        gate_b = small[:, 40:40 + 2 * H]
        mlstm = Places(small, 64)
        stat = small[:, 48:64]

        s_const = sem("constants")
        s_x = sem("x_landed")
        with nc.Block() as block:
            @block.gpsimd
            def _(g):
                n = [0]

                def then(ins):
                    ins.then_inc(s_const, 1)
                    n[0] += 1
                    g.wait_ge(s_const, n[0])
                g.memset(ident[:, :], 0.0)
                g.memset(ones[:, :], 1.0)
                g.memset(upto[:, :], 1.0)
                g.memset(maskG, 1.0)
                g.memset(maskB, 1.0)
                then(g.memset(causal[:, :], 0.0))
                g.affine_select(out=ident[:, :], in_=ident[:, :], compare_op=ALU.not_equal, fill=1.0, base=0,
                                pattern=[[-1, P]], channel_multiplier=1)
                g.affine_select(out=upto[:, :], in_=upto[:, :], compare_op=ALU.is_ge, fill=0.0, base=0,
                                pattern=[[1, P]], channel_multiplier=-1)
                g.affine_select(out=causal[:, :], in_=causal[:, :], compare_op=ALU.is_ge, fill=NEG, base=0,
                                pattern=[[-1, P]], channel_multiplier=1)
                then(g.affine_select(out=maskG, in_=maskG, compare_op=ALU.is_ge, fill=0.0, base=0,
                                     pattern=[[-HG, GP]], channel_multiplier=1))
                then(g.affine_select(out=maskG, in_=maskG, compare_op=ALU.is_ge, fill=0.0, base=HG - 1,
                                     pattern=[[HG, GP]], channel_multiplier=-1))
                for h in range(2):
                    m = maskB[h * PS:(h + 1) * PS]
                    then(g.affine_select(out=m, in_=m, compare_op=ALU.is_equal, fill=0.0, base=-h,
                                         pattern=[[-2, TC], [1, GP]], channel_multiplier=0))

            @block.sync
            def _(sp):
                sp.dma_start(res[:, :, :], a["x"][0].rearrange("(t p) d -> p t d", p=P)).then_inc(s_x, 16)
                for m in range(SLOTS):
                    issue(sp, U_, m, m)
                sp.wait_ge(s_x, 16)

        def norm_phase(name, gain, scale=None, shift=None, dst=None, transposed=True):
            if stop < 0:
                return
            dst = nat if dst is None else dst
            rows = Places(pool)
            gain_row, scale_row, shift_row = rows.take(D), rows.take(D), rows.take(D)
            s_rows, s_sq, s_rt = sem(name + "_rows"), sem(name + "_squares"), sem(name + "_root")
            s_step, s_nat, s_tr = sem(name + "_vector_step"), sem(name + "_normed"), sem(name + "_transposed")
            s_hi, s_lo = sem(name + "_high"), sem(name + "_low")
            with nc.Block() as block:
                @block.sync
                def _(sp):
                    for row, src in ((gain_row, gain), (scale_row, scale), (shift_row, shift)):
                        if src is not None:
                            sp.dma_start(row, src.partition_broadcast(P)).then_inc(s_rows, 16)

                @block.scalar
                def _(act):
                    for t in range(TT):
                        nc.scalar.activation(aTs[:, t * D:(t + 1) * D], res[:, t, :],
                                             ACT.Square, accum_out=stat[:, t:t + 1]).then_inc(s_sq, 1)
                    act.wait_ge(s_step, 1)
                    nc.scalar.activation(stat[:, 4:4 + TT], stat[:, 2:2 + TT], ACT.Sqrt).then_inc(s_rt, 1)
                    if transposed:
                        act.wait_ge(s_sq, TT)
                        for n in range(8):
                            act.wait_ge(s_tr, n + 1)
                            high_left(n, n).then_inc(s_hi, 1)

                @block.vector
                def _(dve):
                    c = [0]

                    def then(ins):
                        ins.then_inc(s_step, 1)
                        c[0] += 1
                        dve.wait_ge(s_step, c[0])
                    dve.wait_ge(s_sq, TT)
                    then(nc.vector.tensor_scalar(stat[:, 2:2 + TT], stat[:, 0:TT], 1.0 / D, EPS, ALU.mult, ALU.add))
                    dve.wait_ge(s_rt, 1)
                    then(nc.vector.reciprocal(stat[:, 6:6 + TT], stat[:, 4:4 + TT]))
                    dve.wait_ge(s_rows, 16 * (1 + (scale is not None) + (shift is not None)))
                    if scale is not None:
                        then(nc.vector.tensor_scalar(scale_row, scale_row, 1.0, None, ALU.add))
                        then(nc.vector.tensor_tensor(gain_row, gain_row, scale_row, ALU.mult))
                    for t in range(TT):
                        ins = nc.vector.scalar_tensor_tensor(dst[:, t, :], res[:, t, :], stat[:, 6 + t:7 + t], gain_row,
                                                             ALU.mult, ALU.mult)
                        if shift is not None:
                            then(ins)
                            ins = nc.vector.tensor_tensor(dst[:, t, :], dst[:, t, :], shift_row, ALU.add)
                        ins.then_inc(s_nat, 1)
                    if transposed:
                        for n in range(8):
                            dve.wait_ge(s_hi, n + 1)
                            low_left(n, n).then_inc(s_lo, 1)

                if transposed:
                    @block.tensor
                    def _(pe):
                        pe.wait_ge(s_nat, TT)
                        pe.wait_ge(s_sq, TT)
                        for n in range(8):
                            for j in range(4):
                                k, t = 2 * n + j // 2, j % 2
                                last = nc.tensor.transpose(ps[n][:, j * P:(j + 1) * P],
                                                           dst[:, t, k * P:(k + 1) * P], ident[:, :])
                            last.then_inc(s_tr, 1)

        norm_phase("norm1", a["norm1_g"][0])
        if stop <= 1:
            return halt(U_)

        place = Places(pool)
        uT = place.take(SC, T)
        v_aug = place.take(TT, H, DH + 1)
        o_nat = place.take(TT, W)
        zg = place.take(TT, 2 * H)
        bb = [place.take(TILES, HG) for _ in range(2)]
        c_nat = [place.take(SC, PS) for _ in range(2)]
        glu_nat = place.take(SC, 2 * HG)
        d_col = place.take(SC)
        prm = place.take(5, TILES)
        NPOW = int(math.log2(T))
        powc, pows = place.take(NPOW, TILES), place.take(NPOW, TILES)
        s5_at = place.at
        blk_b = [place.take(TC, P) for _ in range(2)]
        blk_c = [place.take(TC, P) for _ in range(2)]
        BT = [place.take(TC, P) for _ in range(2)]
        CT = [place.take(TC, P) for _ in range(2)]
        tab_c, tab_s = place.take(TC, T), place.take(TC, T)
        w_re, w_im = place.take(TC, T), place.take(TC, T)
        over_x = Places(res_)
        r_re, r_im = over_x.take(TC, T), over_x.take(TC, T)
        tmp = over_x.take(TC, T)
        scratch = Places(pool, s5_at)
        u_nat = scratch.take(TT, SC * P)
        b_raw = [scratch.take(TILES, HG) for _ in range(2)]
        wg = scratch.take(KD, 2 * H)
        row = scratch.take(24, P)
        prod = [scratch.take(TILES, HG) for _ in range(2)]

        s_par, s_wg = sem("s5_parameters"), sem("gate_columns_landed")
        s_ua, s_ud, s_upe = sem("u_taken"), sem("u_transposed_copied"), sem("u_transposed")
        s_gpe = sem("gate_products")
        s_lin = sem("s5_row_step")
        s_act = sem("s5_row_functions")
        s_prt, s_prc = sem("s5_rows_transposed"), sem("s5_columns_copied")
        g0 = first_slab[U_]
        with nc.Block() as block:
            @block.sync
            def _(sp):
                R = row[0:TILES]
                sp.dma_start(R[:, 0, :], a["s5_lambda_re"][0].rearrange("(j g) p -> j (g p)", g=2)).then_inc(s_par, 16)
                sp.dma_start(R[:, 1, :], a["s5_lambda_im"][0].rearrange("(j g) p -> j (g p)", g=2)).then_inc(s_par, 16)
                sp.dma_start(R[:, 23, 0:2], a["s5_log_dt"][0].rearrange("(j g) -> j g", g=2)).then_inc(s_par, 16)
                for i, n in enumerate(("s5_b_re", "s5_b_im")):
                    src = a[n][0].rearrange("(j g) p h -> (g p) j h", g=2)
                    sp.dma_start(b_raw[i], src).then_inc(s_par, 16)
                for i, n in enumerate(("s5_c_re", "s5_c_im")):
                    sp.dma_start(c_nat[i], a[n][0].rearrange("g h p -> (g h) p").rearrange("(c q) p -> q c p", q=P))\
                      .then_inc(s_par, 16)
                sp.dma_start(glu_nat, a["s5_glu_w"][0].rearrange("g h k -> (g h) k").rearrange("(c q) k -> q c k", q=P))\
                  .then_inc(s_par, 16)
                sp.dma_start(d_col, a["s5_d"][0].rearrange("g h -> (g h)").rearrange("(c q) -> q c", q=P),
                             allow_slow_non_contiguous=True).then_inc(s_par, 16)
                sp.dma_start(gate_b, a["b_gates"][0].partition_broadcast(P)).then_inc(s_par, 16)
                sp.dma_start(wg, w_in[:, C_GATES:C_U].rearrange("(k p) n -> p k n", p=P)).then_inc(s_wg, 16)
                stream(sp, U_)

            @block.tensor
            def _(pe):
                for b in range(2):
                    for j in range(4):
                        slab(pe, g0 + 4 * b + j, [(ps[2 * b + t][:, :], t) for t in range(TT)], left, 4 * j,
                             j == 0, j == 3)
                pe.wait_ge(s_wg, 16)
                for t in range(TT):
                    for k in range(KD):
                        for h in range(2):
                            last = nc.tensor.matmul(ps[4][:, t * 8:t * 8 + 2 * H], left(k, t)[h].bitcast(F32),
                                                    wg[:, k, :], start=k + h == 0, stop=k + h == KD)
                last.then_inc(s_gpe, 1)
                pe.wait_ge(s_ua, 4)
                for n in range(4):
                    for j in range(4):
                        c, t = 2 * n + j // 2, j % 2
                        last = nc.tensor.transpose(ps[n][:, j * P:(j + 1) * P], u_nat[:, t, c * P:(c + 1) * P],
                                                   ident[:, :])
                    last.then_inc(s_upe, 1)
                pe.wait_ge(s_act, 4)
                for j in range(5):
                    last = nc.tensor.transpose(ps[5][:, j * TILES:(j + 1) * TILES], row[0:TILES, 16 + j, :],
                                               ident[0:TILES, 0:TILES])
                last.then_inc(s_prt, 1)

            @block.gpsimd
            def _(g):
                for m in range(8):
                    low_part(g, g0 + m)

            @block.scalar
            def _(act):
                R = row[0:TILES]
                act.wait_ge(s_par, 160)
                nc.scalar.activation(R[:, 23, 2:4], R[:, 23, 0:2], ACT.Exp).then_inc(s_act, 1)
                act.wait_ge(s_lin, 2)
                nc.scalar.activation(R[:, 18, :], R[:, 3, :], ACT.Exp).then_inc(s_act, 1)
                act.wait_ge(s_lin, 10)
                nc.scalar.activation(R[:, 20, :], R[:, 5, :], ACT.Sin)
                nc.scalar.activation(R[:, 19, :], R[:, 6, :], ACT.Sin).then_inc(s_act, 1)
                for m in range(8):
                    high_part(act, g0 + m)
                for b in range(2):
                    act.wait_ge(slabs_used, g0 + 4 * b + 4)
                    for t in range(TT):
                        nc.scalar.copy(u_nat[:, t, b * NB:(b + 1) * NB], ps[2 * b + t][:, :]).then_inc(s_ua, 1)

            @block.vector
            def _(dve):
                R = row[0:TILES]
                v = nc.vector
                c = [0]

                def then(ins):
                    ins.then_inc(s_lin, 1)
                    c[0] += 1
                    dve.wait_ge(s_lin, c[0])
                dve.wait_ge(s_par, 160)
                dve.wait_ge(s_act, 1)
                dt = bc(R[:, 23, 2:4], 2, [TILES, 2, PS])
                for i in range(2):
                    then(v.tensor_tensor(R[:, 3 + i, :].rearrange("j (g p) -> j g p", g=2),
                                         R[:, i, :].rearrange("j (g p) -> j g p", g=2), dt, ALU.mult))
                two_pi = 2 * math.pi
                h1 = 6.28125
                h2 = float(np.float32(np.round((two_pi - h1) * 2 ** 21) / 2 ** 21))
                h3 = two_pi - h1 - h2
                then(v.tensor_scalar(R[:, 7, :], R[:, 4, :], 1.0 / two_pi, MAGIC, ALU.mult, ALU.add))
                then(v.tensor_scalar(R[:, 7, :], R[:, 7, :], MAGIC, None, ALU.subtract))
                then(v.scalar_tensor_tensor(R[:, 5, :], R[:, 7, :], -h1, R[:, 4, :], ALU.mult, ALU.add))
                then(v.scalar_tensor_tensor(R[:, 5, :], R[:, 7, :], -h2, R[:, 5, :], ALU.mult, ALU.add))
                then(v.scalar_tensor_tensor(R[:, 5, :], R[:, 7, :], -h3, R[:, 5, :], ALU.mult, ALU.add))
                then(v.tensor_scalar(R[:, 5, :], R[:, 5, :], math.pi - 1e-6, -(math.pi - 1e-6), ALU.min, ALU.max))
                then(v.scalar_tensor_tensor(R[:, 6, :], R[:, 5, :], -1.0, R[:, 5, :], ALU.mult, ALU.max))
                then(v.tensor_scalar(R[:, 6, :], R[:, 6, :], -1.0, math.pi / 2, ALU.mult, ALU.add))
                dve.wait_ge(s_act, 3)
                re, im = R[:, 0, :], R[:, 1, :]
                then(v.tensor_tensor(R[:, 8, :], R[:, 18, :], R[:, 19, :], ALU.mult))
                then(v.tensor_tensor(R[:, 9, :], R[:, 18, :], R[:, 20, :], ALU.mult))
                then(v.tensor_scalar(R[:, 8, :], R[:, 8, :], 1.0, None, ALU.subtract))
                then(v.tensor_tensor(R[:, 10, :], re, re, ALU.mult))
                then(v.tensor_tensor(R[:, 11, :], im, im, ALU.mult))
                then(v.tensor_tensor(R[:, 10, :], R[:, 10, :], R[:, 11, :], ALU.add))
                then(v.reciprocal(R[:, 10, :], R[:, 10, :]))
                for dst, (x0, y0, x1, y1, op) in ((16, (8, re, 9, im, ALU.add)), (17, (9, re, 8, im, ALU.subtract))):
                    then(v.tensor_tensor(R[:, 12, :], R[:, x0, :], y0, ALU.mult))
                    then(v.tensor_tensor(R[:, 13, :], R[:, x1, :], y1, ALU.mult))
                    then(v.tensor_tensor(R[:, 12, :], R[:, 12, :], R[:, 13, :], op))
                    ins = v.tensor_tensor(R[:, dst, :], R[:, 12, :], R[:, 10, :], ALU.mult)
                    if dst == 16:
                        then(ins)
                    else:
                        ins.then_inc(s_act, 1)
                dve.wait_ge(s_prt, 1)
                then(v.tensor_copy(prm, view(ps[5][:, 0:5 * TILES], [5, TILES])))
                f = [bc(prm[:, i, :], 2, [P, TILES, HG]) for i in range(2)]
                for i, op in ((0, ALU.subtract), (1, ALU.add)):
                    then(v.tensor_tensor(prod[0], b_raw[i], f[0], ALU.mult))
                    then(v.tensor_tensor(prod[1], b_raw[1 - i], f[1], ALU.mult))
                    then(v.tensor_tensor(bb[i], prod[0], prod[1], op))
                then(v.tensor_copy(powc[:, 0, :], prm[:, 3, :]))
                then(v.tensor_copy(pows[:, 0, :], prm[:, 4, :]))
                q0, q1 = prod[0][:, 0:2, :].rearrange("p a b -> p (a b)"), prod[1][:, 0:2, :].rearrange("p a b -> p (a b)")
                for n in range(1, NPOW):
                    then(v.tensor_tensor(q0, powc[:, n - 1, :], powc[:, n - 1, :], ALU.mult))
                    then(v.tensor_tensor(q1, pows[:, n - 1, :], pows[:, n - 1, :], ALU.mult))
                    then(v.tensor_tensor(powc[:, n, :], q0, q1, ALU.subtract))
                    then(v.scalar_tensor_tensor(pows[:, n, :], powc[:, n - 1, :], 2.0, pows[:, n - 1, :],
                                                ALU.mult, ALU.mult))
                dve.wait_ge(s_gpe, 1)
                for t in range(TT):
                    v.tensor_tensor(zg[:, t, :], ps[4][:, t * 8:t * 8 + 2 * H], gate_b, ALU.add)
                for n in range(4):
                    dve.wait_ge(s_upe, n + 1)
                    v.tensor_copy(uT[:, 2 * n:2 * n + 2, :].rearrange("p k t -> p (k t)"), ps[n][:, :])
        if stop <= 2:
            return halt(QKVO)

        s_blk, s_bT, s_bTc = sem("s5_blocks"), sem("s5_b_transposed"), sem("s5_b_copied")
        s_blkc = sem("s5_c_blocks")
        s_cT, s_cTc = sem("s5_c_transposed"), sem("s5_c_copied")
        s_xp, s_rot, s_st, s_yp, s_yd = (sem("s5_inputs"), sem("s5_rotated"), sem("s5_states"), sem("s5_outputs"),
                                         sem("s5_outputs_taken"))
        s_proj, s_v5 = sem("qkvo_taken"), sem("s5_vector_step")
        g0 = first_slab[QKVO]
        with nc.Block() as block:
            @block.sync
            def _(sp):
                stream(sp, QKVO)

            @block.gpsimd
            def _(g):
                for m in range(SECTIONS[QKVO].n):
                    low_part(g, g0 + m)

            @block.tensor
            def _(pe):
                def b_transposes(c):
                    pe.wait_ge(s_blk, c + 1)
                    if c:
                        pe.wait_ge(s_bTc, 2 * c)
                    for i in range(2):
                        for b in range(TC):
                            last = nc.tensor.transpose(ps[4 + i][:, b * P:(b + 1) * P], blk_b[i][:, b, :], ident[:, :])
                    last.then_inc(s_bT, 1)

                b_transposes(0)
                for c in range(SC):
                    pe.wait_ge(s_bTc, 2 * c + 2)
                    if c:
                        pe.wait_ge(s_yd, c)
                        pe.wait_ge(s_cTc, 2 * c)
                    for i in range(2):
                        for b in range(TC):
                            last = nc.tensor.matmul(ps[2 * i + b // 2][:, (b % 2) * T:(b % 2 + 1) * T],
                                                    BT[i][:, b, :], uT[:, c, :], start=True, stop=True)
                    last.then_inc(s_xp, 1)
                    if c + 1 < SC:
                        b_transposes(c + 1)
                    if c:
                        pe.wait_ge(s_proj, 2 * c)
                    for j in range(4):
                        slab(pe, g0 + 4 * c + j, [(ps[6 + t][:, :], t) for t in range(TT)], left, 4 * j,
                             j == 0, j == 3)
                    pe.wait_ge(s_rot, c + 1)
                    pe.wait_ge(s_blkc, c + 1)
                    for i in range(2):
                        for b in range(TC):
                            last = nc.tensor.transpose(ps[1 + i][:, b * P:(b + 1) * P], blk_c[i][:, b, :], ident[:, :])
                    last.then_inc(s_cT, 1)
                    pe.wait_ge(s_cTc, 2 * c + 2)
                    pe.wait_ge(s_st, c + 1)
                    n = 0
                    for i, s in enumerate((w_re, w_im)):
                        for b in range(TC):
                            last = nc.tensor.matmul(ps[0][:, 0:T], CT[i][:, b, :], s[:, b, :],
                                                    start=n == 0, stop=n == 2 * TC - 1)
                            n += 1
                    last.then_inc(s_yp, 1)

            @block.scalar
            def _(act):
                def copy_b(c):
                    act.wait_ge(s_bT, c + 1)
                    if c:
                        act.wait_ge(s_xp, c)
                    for i in range(2):
                        nc.scalar.copy(BT[i].rearrange("p b q -> p (b q)"), ps[4 + i][:, :]).then_inc(s_bTc, 1)

                copy_b(0)
                for c in range(SC):
                    if c + 1 < SC:
                        copy_b(c + 1)
                    for j in range(4 * c + (2 if c else 0), min(4 * c + 6, 4 * SC)):
                        high_part(act, g0 + j)
                    act.wait_ge(slabs_used, g0 + 4 * c + 4)
                    for t in range(TT):
                        if c < 4:
                            dst = nat[:, t, c * NB:(c + 1) * NB]
                        elif c < 6:
                            hs = NB // DH
                            dst = v_aug[:, t, (c - 4) * hs:(c - 3) * hs, 0:DH]
                        else:
                            dst = o_nat[:, t, (c - 6) * NB:(c - 5) * NB]
                        src = ps[6 + t][:, :]
                        if 4 <= c < 6:
                            src = view(src, [NB // DH, DH])
                        nc.scalar.copy(dst, src).then_inc(s_proj, 1)
                    act.wait_ge(s_cT, c + 1)
                    if c:
                        act.wait_ge(s_yp, c)
                    for i in range(2):
                        nc.scalar.copy(CT[i].rearrange("p b q -> p (b q)"), ps[1 + i][:, :]).then_inc(s_cTc, 1)

            @block.vector
            def _(dve):
                v = nc.vector
                n = [0]

                def then(ins):
                    ins.then_inc(s_v5, 1)
                    n[0] += 1
                    dve.wait_ge(s_v5, n[0])

                def blocks_b(c):
                    if c:
                        dve.wait_ge(s_bT, c)
                    for i in range(2):
                        dst = blk_b[i].rearrange("p b (g h) -> p b g h", g=GP)
                        last = v.tensor_tensor(dst, bc(bb[i][:, TC * c:TC * c + TC, :], 2, [P, TC, GP, HG]),
                                               bc(maskB, 3, [P, TC, GP, HG]), ALU.mult)
                    last.then_inc(s_blk, 1)

                def blocks_c(c):
                    if c:
                        dve.wait_ge(s_cT, c)
                    for i in range(2):
                        dst = blk_c[i].rearrange("p b (g q) -> p (b g) q", g=2)
                        last = v.scalar_tensor_tensor(dst, bc(c_nat[i][:, c, :], 1, [P, GP, PS]), 1.0 - 2.0 * i,
                                                      bc(maskG, 2, [P, GP, PS]), ALU.mult, ALU.mult)
                    last.then_inc(s_blkc, 1)

                def tables(c):
                    v.memset(tab_c[:, :, 0:1], 1.0)
                    then(v.memset(tab_s[:, :, 0:1], 0.0))
                    for m in range(NPOW):
                        k = 1 << m
                        cn = bc(powc[:, m, TC * c:TC * c + TC], 2, [P, TC, k])
                        sn = bc(pows[:, m, TC * c:TC * c + TC], 2, [P, TC, k])
                        lo, hi = (lambda x: x[:, :, 0:k]), (lambda x: x[:, :, k:2 * k])
                        v.tensor_tensor(hi(tab_c), lo(tab_c), cn, ALU.mult)
                        v.tensor_tensor(lo(tmp), lo(tab_s), sn, ALU.mult)
                        v.tensor_tensor(hi(tab_s), lo(tab_s), cn, ALU.mult)
                        then(v.tensor_tensor(hi(tmp), lo(tab_c), sn, ALU.mult))
                        v.tensor_tensor(hi(tab_c), hi(tab_c), lo(tmp), ALU.subtract)
                        then(v.tensor_tensor(hi(tab_s), hi(tab_s), hi(tmp), ALU.add))

                blocks_b(0)
                tables(0)
                then(v.memset(v_aug[:, :, :, DH:DH + 1], 1.0))
                for c in range(SC):
                    blocks_c(c)
                    if c + 1 < SC:
                        blocks_b(c + 1)
                    dve.wait_ge(s_xp, c + 1)
                    if c:
                        dve.wait_ge(s_yp, c)
                    x = [[view(ps[2 * i + q][:, :], [2, T]) for q in range(2)] for i in range(2)]
                    half = [slice(0, 2), slice(2, 4)]
                    for q in range(2):
                        v.tensor_tensor(w_re[:, half[q], :], x[0][q], tab_c[:, half[q], :], ALU.mult)
                        v.tensor_tensor(r_re[:, half[q], :], x[1][q], tab_s[:, half[q], :], ALU.mult)
                        v.tensor_tensor(w_im[:, half[q], :], x[1][q], tab_c[:, half[q], :], ALU.mult)
                        last = v.tensor_tensor(r_im[:, half[q], :], x[0][q], tab_s[:, half[q], :], ALU.mult)
                    then(last)
                    v.tensor_tensor(w_re, w_re, r_re, ALU.add).then_inc(s_rot, 1)
                    then(v.tensor_tensor(w_im, w_im, r_im, ALU.subtract))
                    for b in range(TC):
                        mag = prm[:, 2, TC * c + b:TC * c + b + 1].to_broadcast([P, T])
                        v.tensor_tensor_scan(r_re[:, b, :], mag, w_re[:, b, :], 0.0, ALU.mult, ALU.add)
                        last = v.tensor_tensor_scan(r_im[:, b, :], mag, w_im[:, b, :], 0.0, ALU.mult, ALU.add)
                    then(last)
                    v.tensor_tensor(w_re, r_re, tab_c, ALU.mult)
                    then(v.tensor_tensor(tmp, r_im, tab_s, ALU.mult))
                    then(v.tensor_tensor(w_re, w_re, tmp, ALU.subtract))
                    v.tensor_tensor(w_im, r_re, tab_s, ALU.mult)
                    then(v.tensor_tensor(tmp, r_im, tab_c, ALU.mult))
                    v.tensor_tensor(w_im, w_im, tmp, ALU.add).then_inc(s_st, 1)
                    if c + 1 < SC:
                        dve.wait_ge(s_st, c + 1)
                        tables(c + 1)
                    dve.wait_ge(s_yp, c + 1)
                    v.scalar_tensor_tensor(uT[:, c, :], uT[:, c, :], d_col[:, c:c + 1], ps[0][:, 0:T],
                                           ALU.mult, ALU.add).then_inc(s_yd, 1)
        if stop <= 3:
            return halt(W_OUT)

        scratch = Places(pool, s5_at)
        qkT = scratch.take(QC, T)
        raw = scratch.take(QC, CW - 1 + T)
        glu_blk = view(aTs[:, SC * T:2 * SC * T], [2, SC, P])
        cw_row = scratch.take(P)
        cw = scratch.take(CW, QC)
        gated_b = view(aTs[:, 0:SC * T], [SC, T])
        s_cwl, s_gelu, s_glub = sem("conv_weights_landed"), sem("s5_gelu"), sem("glu_blocks")
        s_glu, s_sig, s_ys = sem("glu_products"), sem("glu_sigmoid"), sem("s5_done")
        s_cwT, s_cwc, s_halo = sem("conv_weights_transposed"), sem("conv_weights_copied"), sem("conv_halo")
        s_qkT, s_qkc, s_cstep, s_silu = sem("qk_transposed"), sem("qk_copied"), sem("conv_step"), sem("qk_done")
        s_og = sem("o_gate")
        with nc.Block() as block:
            @block.sync
            def _(sp):
                sp.dma_start(cw_row[0:CW * QC, :], a["conv_qk_w"][0].rearrange("i (c p) -> (i c) p", p=P))\
                  .then_inc(s_cwl, 16)

            @block.tensor
            def _(pe):
                pe.wait_ge(s_cwl, 16)
                nc.tensor.transpose(ps[6][:, 0:CW * QC], cw_row[0:CW * QC, :], ident[0:CW * QC, 0:CW * QC])\
                  .then_inc(s_cwT, 1)
                for n in range(8):
                    if n >= 4:
                        pe.wait_ge(s_qkc, n - 3)
                    for j in range(4):
                        c, t = 2 * n + j // 2, j % 2
                        last = nc.tensor.transpose(ps[n % 4][:, j * P:(j + 1) * P], nat[:, t, c * P:(c + 1) * P],
                                                   ident[:, :])
                    last.then_inc(s_qkT, 1)
                pe.wait_ge(s_gelu, 1)
                pe.wait_ge(s_glub, 1)
                for c in range(SC):
                    if c >= 2:
                        pe.wait_ge(s_ys, c - 1)
                    for i in range(2):
                        last = nc.tensor.matmul(ps[4 + c % 2][:, i * T:(i + 1) * T], glu_blk[:, i, c, :], uT[:, c, :],
                                                start=True, stop=True)
                    last.then_inc(s_glu, 1)

            @block.scalar
            def _(act):
                nc.scalar.activation(uT, uT, ACT.Gelu).then_inc(s_gelu, 1)
                for n in range(8):
                    act.wait_ge(s_qkT, n + 1)
                    nc.scalar.copy(raw[:, 2 * n:2 * n + 2, CW - 1:], view(ps[n % 4][:, :], [2, T])).then_inc(s_qkc, 1)
                for c in range(SC):
                    act.wait_ge(s_glu, c + 1)
                    nc.scalar.activation(gated_b[:, c, :], ps[4 + c % 2][:, T:2 * T], ACT.Sigmoid).then_inc(s_sig, 1)
                nc.scalar.activation(o_nat, o_nat, ACT.Sigmoid).then_inc(s_og, 1)
                for n in range(4):
                    act.wait_ge(s_cstep, 64 // 4 * (n + 1))
                    nc.scalar.activation(qkT[:, 4 * n:4 * n + 4, :], qkT[:, 4 * n:4 * n + 4, :], ACT.Silu)\
                      .then_inc(s_silu, 1)

            @block.vector
            def _(dve):
                v = nc.vector
                for i in range(2):
                    for c in range(SC):
                        last = v.tensor_tensor(view(glu_blk[:, i, c, :], [GP, HG]),
                                               bc(glu_nat[:, c, i * HG:(i + 1) * HG], 1, [P, GP, HG]),
                                               bc(maskG, 2, [P, GP, HG]), ALU.mult)
                last.then_inc(s_glub, 1)
                v.memset(raw[:, :, 0:CW - 1], 0.0).then_inc(s_halo, 1)
                dve.wait_ge(s_cwT, 1)
                v.tensor_copy(cw, view(ps[6][:, 0:CW * QC], [CW, QC])).then_inc(s_cwc, 1)
                dve.wait_ge(s_halo, 1)
                dve.wait_ge(s_cwc, 1)
                for n in range(QC // 4):
                    dve.wait_ge(s_qkc, 2 * n + 2)
                    for i in range(CW):
                        if n or i:
                            dve.wait_ge(s_cstep, 16 * n + 4 * i)
                        for c in range(4 * n, 4 * n + 4):
                            if i == 0:
                                ins = v.tensor_scalar(qkT[:, c, :], raw[:, c, 0:T], cw[:, 0, c:c + 1], None, ALU.mult)
                            else:
                                ins = v.scalar_tensor_tensor(qkT[:, c, :], raw[:, c, i:i + T], cw[:, i, c:c + 1],
                                                             qkT[:, c, :], ALU.mult, ALU.add)
                            ins.then_inc(s_cstep, 1)
                for c in range(SC):
                    dve.wait_ge(s_sig, c + 1)
                    v.tensor_tensor(uT[:, c, :], ps[4 + c % 2][:, 0:T], gated_b[:, c, :], ALU.mult).then_inc(s_ys, 1)
        if stop <= 4:
            return halt(W_OUT)

        R2 = TT * H
        kit = Places(aTs)
        bm = kit.take(R2, P)
        dg = kit.take(R2, P)
        kw = kit.take(H, DH)
        c0_at = Places(nat_)
        c0 = c0_at.take(H, DC, DH + 1)
        ng_row = c0_at.take(W)
        rawp = Places(pool, s5_at + QC * T)
        nd = rawp.take(R2, DH + 1)
        hm = rawp.take(TT, H, DH)
        cols_ = Places(small, 64)
        (lf, acum, atot, bcol, bmax, mt, minter, shift_, sint, eneg, t0, t1, ss, rr) = [cols_.take(R2) for _ in range(14)]
        bmax0, mloc, m0, wcol, snew = [cols_.take(H) for _ in range(5)]
        s_m, s_mf = sem("mlstm_vector_step"), sem("mlstm_functions")
        s_mp, s_mc, s_ngl = sem("mlstm_products"), sem("mlstm_copies"), sem("mlstm_gain_landed")
        s_nd, s_ndt, s_hmt = sem("mlstm_heads"), sem("mlstm_heads_taken"), sem("mlstm_transposed")
        with nc.Block() as block:
            @block.sync
            def _(sp):
                sp.dma_start(ng_row, a["mlstm_norm_g"][0].partition_broadcast(P)).then_inc(s_ngl, 16)
                sp.dma_start(res, a["x"][0].rearrange("(t p) d -> p t d", p=P)).then_inc(s_x, 16)
                sp.wait_ge(s_x, 32)

            m = {}

            @block.vector
            def _(dve):
                v = nc.vector
                n = [0]

                def then(ins, mark=None):
                    ins.then_inc(s_m, 1)
                    n[0] += 1
                    m[mark] = n[0]
                    dve.wait_ge(s_m, n[0])
                gi = zg[:, :, 0:H]
                gf = zg[:, :, H:2 * H]
                by = (lambda x: view(x, [TT, H]))
                then(v.scalar_tensor_tensor(by(t0), gf, -1.0, gf, ALU.mult, ALU.max), "abs")
                dve.wait_ge(s_mf, 2)
                then(v.scalar_tensor_tensor(by(lf), gf, 0.0, by(t1), ALU.min, ALU.subtract), "lf")
                dve.wait_ge(s_mp, 1)
                v.tensor_copy(acum, ps[6][:, 0:R2])
                then(v.tensor_copy(atot, ps[6][:, R2:2 * R2]))
                then(v.tensor_tensor(by(bcol), gi, by(acum), ALU.subtract))
                then(v.tensor_tensor(dg, bc(ident[:, :], 1, [P, R2, P]), bc(bcol, 2, [P, R2, P]), ALU.mult), "dg")
                dve.wait_ge(s_mp, 3)
                for c in range(TT):
                    v.tensor_tensor(bm[:, c * H:(c + 1) * H, :], view(ps[c][:, :], [H, P]),
                                    bc(causal[:, :], 1, [P, H, P]), ALU.add)
                then(v.tensor_reduce(bmax0, view(ps[0][:, :], [H, P]), AX, ALU.max))
                then(v.tensor_reduce(bmax, bm, AX, ALU.max))
                then(v.tensor_tensor(mloc, atot[:, 0:H], bmax0, ALU.add))
                then(v.tensor_tensor(m0, atot[:, 0:H], mloc, ALU.max))
                v.tensor_tensor(snew, mloc, m0, ALU.subtract)
                v.tensor_tensor(wcol, bcol[:, 0:H], bmax0, ALU.subtract)
                v.tensor_copy(minter[:, 0:H], acum[:, 0:H])
                v.tensor_tensor(minter[:, H:], acum[:, H:], m0, ALU.add)
                then(v.tensor_tensor(mt, acum, bmax, ALU.add))
                then(v.tensor_tensor(mt, mt, minter, ALU.max))
                v.tensor_tensor(sint, minter, mt, ALU.subtract)
                then(v.tensor_tensor(shift_, acum, mt, ALU.subtract))
                then(v.tensor_tensor(bm, bm, bc(shift_, 2, [P, R2, P]), ALU.add), "w")
                dve.wait_ge(s_mf, 3)
                then(v.tensor_tensor(wcol, wcol, snew, ALU.mult))
                for j in range(2):
                    src = view(ps[4 + j][:, :], [H // 2, DH])
                    last = v.tensor_tensor(kw[:, j * H // 2:(j + 1) * H // 2, :], src,
                                           bc(wcol[:, j * H // 2:(j + 1) * H // 2], 2, [P, H // 2, DH]), ALU.mult)
                then(last, "kw")
                dve.wait_ge(s_mf, 4)
                for c in range(TT):
                    last = v.scalar_tensor_tensor(bm[:, c * H:(c + 1) * H, :], view(ps[2 + c][:, :], [H, P]),
                                                  DH ** -0.5, bm[:, c * H:(c + 1) * H, :], ALU.mult, ALU.mult)
                then(last, "p")
                for k in range(H * DC):
                    dve.wait_ge(s_nd, k + 1)
                    v.tensor_copy(c0[:, k // DC, k % DC, :], ps[(6, 7, 4, 5)[k % 4]][:, 0:DH + 1]).then_inc(s_ndt, 1)
                dve.wait_ge(s_mp, 4)
                for c in range(TT):
                    last = v.tensor_copy(dg[:, c * H:(c + 1) * H, :], view(ps[c][:, :], [H, P]))
                then(last, "pt")
                v.tensor_scalar(sint, sint, DH ** -0.5, None, ALU.mult)
                for r in range(R2):
                    dve.wait_ge(s_nd, H * DC + r + 1)
                    last = v.tensor_copy(nd[:, r, :], ps[(2, 3)[r % 2]][:, 0:DH + 1])
                    last.then_inc(s_ndt, 1)
                dve.wait_ge(s_ndt, H * DC + R2)
                for h in range(H):
                    dve.wait_ge(s_nd, H * DC + R2 + h + 1)
                    last = v.scalar_tensor_tensor(nd[:, H + h, :], ps[4 + h][:, 0:DH + 1], sint[:, H + h:H + h + 1],
                                                  nd[:, H + h, :], ALU.mult, ALU.add)
                then(last)
                den = nd[:, :, DH:DH + 1].rearrange("p r o -> p (r o)")
                then(v.scalar_tensor_tensor(t0, den, -1.0, den, ALU.mult, ALU.max))
                then(v.tensor_tensor(t0, t0, eneg, ALU.max))
                then(v.reciprocal(t0, t0))
                hr = hm.rearrange("p c h d -> p (c h) d")
                then(v.tensor_tensor(hr, nd[:, :, 0:DH], bc(t0, 2, [P, R2, DH]), ALU.mult))
                sq = nd[:, :, 0:DH]
                then(v.tensor_tensor(sq, hr, hr, ALU.mult))
                then(v.tensor_reduce(ss, sq, AX, ALU.add))
                then(v.tensor_scalar(ss, ss, 1.0 / DH, EPS, ALU.mult, ALU.add), "sq")
                dve.wait_ge(s_mf, 5)
                then(v.reciprocal(rr, ss))
                then(v.tensor_tensor(hr, hr, bc(rr, 2, [P, R2, DH]), ALU.mult))
                dve.wait_ge(s_ngl, 16)
                hf = hm.rearrange("p c h d -> p c (h d)")
                then(v.tensor_tensor(hf, hf, bc(ng_row, 1, [P, TT, W]), ALU.mult))
                then(v.tensor_tensor(hf, hf, o_nat, ALU.mult), "h")
                dve.wait_ge(s_mc, 1)
                v.tensor_tensor(aTl[:, KD - SC:KD, :], uT, aTh[:, KD - SC:KD, :].bitcast(F32), ALU.subtract)
                for k in range(4):
                    dve.wait_ge(s_mc, k + 2)
                    low_left(k, k)

            @block.scalar
            def _(act):
                act.wait_ge(s_m, 1)
                nc.scalar.activation(t1, t0, ACT.Exp, scale=-1.0).then_inc(s_mf, 1)
                act.wait_ge(s_mf, 1)
                nc.scalar.activation(t1, t1, ACT.Ln, bias=1.0).then_inc(s_mf, 1)
                act.wait_ge(s_m, m["w"])
                nc.scalar.activation(wcol, wcol, ACT.Exp)
                nc.scalar.activation(snew, snew, ACT.Exp)
                nc.scalar.activation(sint, sint, ACT.Exp)
                nc.scalar.activation(eneg, mt, ACT.Exp, scale=-1.0).then_inc(s_mf, 1)
                nc.scalar.activation(bm, bm, ACT.Exp).then_inc(s_mf, 1)
                act.wait_ge(s_m, m["sq"])
                nc.scalar.activation(ss, ss, ACT.Sqrt).then_inc(s_mf, 1)
                act.wait_ge(s_m, m["h"])
                nc.scalar.copy(aTh[:, KD - SC:KD, :], uT).then_inc(s_mc, 1)
                for n in range(4):
                    act.wait_ge(s_hmt, n + 1)
                    high_left(n, n).then_inc(s_mc, 1)

            @block.tensor
            def _(pe):
                pe.wait_ge(s_m, m["lf"])
                nc.tensor.matmul(ps[6][:, 0:R2], upto[:, :], lf, start=True, stop=True)
                nc.tensor.matmul(ps[6][:, R2:2 * R2], ones[:, :], lf, start=True, stop=True).then_inc(s_mp, 1)
                for c in range(TT):
                    for h in range(H):
                        for d in range(DC):
                            tok = slice(c * P, (c + 1) * P)
                            last = nc.tensor.matmul(ps[2 + c][:, h * P:(h + 1) * P], qkT[:, h * DC + d, tok],
                                                    qkT[:, QC // 2 + h * DC + d, tok], start=d == 0, stop=d == DC - 1)
                for j in range(QC // 2):
                    last = nc.tensor.transpose(ps[4 + j // 4][:, (j % 4) * P:(j % 4 + 1) * P],
                                               qkT[:, QC // 2 + j, 0:P], ident[:, :])
                last.then_inc(s_mp, 1)
                pe.wait_ge(s_m, m["dg"])
                for c in range(TT):
                    last = nc.tensor.matmul(ps[c][:, :], ones[:, :],
                                            dg[:, c * H:(c + 1) * H, :].rearrange("p a b -> p (a b)"),
                                            start=True, stop=True)
                last.then_inc(s_mp, 1)
                pe.wait_ge(s_m, m["kw"])
                for h in range(H):
                    for d in range(DC):
                        n = h * DC + d
                        b = (6, 7, 4, 5)[n % 4]
                        if n >= 4:
                            pe.wait_ge(s_ndt, n - 3)
                        nc.tensor.matmul(ps[b][:, 0:DH + 1], kw[:, h, d * P:(d + 1) * P], v_aug[:, 0, h, :],
                                         start=True, stop=True).then_inc(s_nd, 1)
                pe.wait_ge(s_m, m["p"])
                for c in range(TT):
                    for h in range(H):
                        last = nc.tensor.transpose(ps[c][:, h * P:(h + 1) * P], bm[:, c * H + h, :], ident[:, :])
                last.then_inc(s_mp, 1)
                pe.wait_ge(s_m, m["pt"])
                for r in range(R2):
                    b = (2, 3)[r % 2]
                    if r >= 2:
                        pe.wait_ge(s_ndt, 8 + r - 1)
                    nc.tensor.matmul(ps[b][:, 0:DH + 1], dg[:, r, :], v_aug[:, r // H, r % H, :],
                                     start=True, stop=True).then_inc(s_nd, 1)
                for h in range(H):
                    b = 4 + h
                    for d in range(DC):
                        last = nc.tensor.matmul(ps[b][:, 0:DH + 1], qkT[:, h * DC + d, P:2 * P], c0[:, h, d, :],
                                                start=d == 0, stop=d == DC - 1)
                    last.then_inc(s_nd, 1)
                pe.wait_ge(s_m, m["h"])
                for n in range(4):
                    for j in range(4):
                        k, t = 2 * n + j // 2, j % 2
                        last = nc.tensor.transpose(ps[n][:, j * P:(j + 1) * P],
                                                   hm[:, t, :, :].rearrange("p h d -> p (h d)")[:, k * P:(k + 1) * P],
                                                   ident[:, :])
                    last.then_inc(s_hmt, 1)
        if stop <= 5:
            return halt(W_OUT)

        def into_residual(name, sec):
            taken = sem(name + "_taken")
            s, g0 = SECTIONS[sec], first_slab[sec]
            with nc.Block() as block:
                @block.sync
                def _(sp):
                    stream(sp, sec)

                @block.tensor
                def _(pe):
                    linear(pe, sec, [taken])

                @block.scalar
                def _(act):
                    high_blocks(act, sec, lambda b: None)

                @block.vector
                def _(dve):
                    def add(b):
                        dve.wait_ge(slabs_used, g0 + 4 * (b + 1))
                        for t in range(TT):
                            dst = res[:, t, b * NB:(b + 1) * NB]
                            nc.vector.tensor_tensor(dst, ps[(b % 2) * TT + t][:, :], dst, ALU.add).then_inc(taken, 1)
                    low_blocks(dve, sec, add)

        into_residual("w_out", W_OUT)
        if stop <= 6:
            return halt(PEER_Q)

        norm_phase("norm2", a["norm2_g"][0])

        place = Places(pool)
        GB = 8
        rows_ = [place.take(D) for _ in range(GB)]
        place_q = Places(pool)
        q_nat = place_q.take(TT, PH * 2 * HALF)
        upper = Places(aTs, KD * T)
        cand = upper.take(PH, TOPK * TOPK)
        hot = upper.take(HK, TOPK)
        idx = place.take(TT, HK).bitcast(U32)
        gate = place.take(TT, HK)
        actv = place.take(TT, HK)
        top = place.take(2 * PH, TOPK)
        topi = place.take(2 * PH, TOPK)
        pos = place.take(2, HK)
        stage = small[:, 0:2 * GB].bitcast(U32)
        iota16 = small[:, 16:16 + TOPK]
        dots = small[:, 32:32 + GB]
        ccol = small[:, 40:40 + KD]
        skT = place.take(2, KEYS)
        modrow = view(aTs[0:1, 0:2 * NB], [2, NB])
        scores = view(aTs[:, 0:KD * T], [TT, 2 * PH, KEYS])
        qT = view(aTs[:, 0:KD * T], [KD, T])
        sk_nat = view(rows_[4][:, 0:2 * KEYS], [2, HALF])

        def project_rows(name, sec, dst, more_sp=None):
            taken = [sem(name + "_taken_act"), sem(name + "_taken_dve")]
            s, g0 = SECTIONS[sec], first_slab[sec]
            with nc.Block() as block:
                @block.sync
                def _(sp):
                    if more_sp:
                        more_sp(sp)
                    stream(sp, sec)

                @block.tensor
                def _(pe):
                    linear(pe, sec, taken)

                def evac(eng, copy, t):
                    def one(b):
                        eng.wait_ge(slabs_used, g0 + 4 * (b + 1))
                        copy(dst(t, b), ps[(b % 2) * TT + t][:, :]).then_inc(taken[t], 1)
                    return one

                @block.scalar
                def _(act):
                    high_blocks(act, sec, evac(act, nc.scalar.copy, 0))

                @block.vector
                def _(dve):
                    low_blocks(dve, sec, evac(dve, nc.vector.tensor_copy, 1))

        s_cl, s_sk = sem("condition_landed"), sem("subkeys_landed")

        def peer_small(sp):
            sp.dma_start(ccol, a["c_2"][0].rearrange("(k p) -> p k", p=P), allow_slow_non_contiguous=True)\
              .then_inc(s_cl, 16)
            sp.dma_start(sk_nat, a["peer_subkeys"][0].rearrange("h k d -> k h d")).then_inc(s_sk, 16)
        project_rows("peer_q", PEER_Q, lambda t, b: q_nat[:, t, b * NB:(b + 1) * NB], peer_small)

        s_qT, s_qTc, s_sc = sem("peer_q_transposed"), sem("peer_q_copied"), sem("peer_scores")
        s_skT, s_skc, s_cs, s_io = sem("subkeys_transposed"), sem("subkeys_copied"), sem("condition_silu"), sem("iota_done")
        with nc.Block() as block:
            @block.gpsimd
            def _(g):
                g.iota(iota16, pattern=[[1, TOPK]], base=0, channel_multiplier=0,
                       allow_small_or_imprecise_dtypes=True).then_inc(s_io, 1)

            @block.tensor
            def _(pe):
                pe.wait_ge(s_sk, 16)
                for i in range(2):
                    last = nc.tensor.transpose(ps[7][:, i * P:(i + 1) * P], sk_nat[:, i, :], ident[:, :])
                last.then_inc(s_skT, 1)
                for n in range(8):
                    if n >= 4:
                        pe.wait_ge(s_qTc, n - 3)
                    for j in range(4):
                        k, t = 2 * n + j // 2, j % 2
                        last = nc.tensor.transpose(ps[n % 4][:, j * P:(j + 1) * P], q_nat[:, t, k * P:(k + 1) * P],
                                                   ident[:, :])
                    last.then_inc(s_qT, 1)
                pe.wait_ge(s_qTc, 8)
                pe.wait_ge(s_skc, 1)
                for t in range(TT):
                    for g in range(2 * PH):
                        last = nc.tensor.matmul(ps[4 * t + g // 4][:, (g % 4) * KEYS:(g % 4 + 1) * KEYS],
                                                qT[:, g, t * P:(t + 1) * P], skT[:, g % 2, :], start=True, stop=True)
                last.then_inc(s_sc, 1)

            @block.scalar
            def _(act):
                act.wait_ge(s_cl, 16)
                nc.scalar.activation(ccol, ccol, ACT.Silu).then_inc(s_cs, 1)
                for n in range(8):
                    act.wait_ge(s_qT, n + 1)
                    nc.scalar.copy(qT[:, 2 * n:2 * n + 2, :].rearrange("p k t -> p (k t)"), ps[n % 4][:, :])\
                      .then_inc(s_qTc, 1)
                act.wait_ge(s_sc, 1)
                for b in range(4, 8):
                    nc.scalar.copy(aTs[:, b * NB:(b + 1) * NB], ps[b][:, :])

            @block.vector
            def _(dve):
                dve.wait_ge(s_skT, 1)
                nc.vector.tensor_copy(skT, view(ps[7][:, 0:2 * P], [2, P])).then_inc(s_skc, 1)
                dve.wait_ge(s_sc, 1)
                for b in range(4):
                    nc.vector.tensor_copy(aTs[:, b * NB:(b + 1) * NB], ps[b][:, :])
        if stop <= 7:
            return halt(ADA_A)

        gsum = small[:, 64:64 + PH]
        mod = nc.dram_tensor("modulation", (NMOD * D,), F32, kind="Internal").ap()
        s_r, s_idx, s_e, s_g = sem("route_step"), sem("experts_known"), sem("gate_exponentials"), sem("activations")
        s_stage, s_free, s_turn = sem("indices_staged"), sem("rows_used"), sem("gathers_let_go")
        s_row = [sem(f"row_gathered{i}") for i in range(GB)]
        s_dv, s_gl, s_w = sem("dots_step"), sem("gelu_done"), sem("expert_weights")
        s_mtk, s_mout = sem("modulation_taken"), [sem(f"modulation_written{i}") for i in range(2)]
        s_mb, s_mba = sem("modulation_read_back"), sem("modulation_biased")
        g0 = first_slab[ADA_A]
        HB = HK // GB
        fsr = place.take(PH, TOPK)
        mod_sum = place.take(2, P)
        MR = MODA * NB // P
        with nc.Block() as block:
            DV = {}

            @block.vector
            def _(dve):
                v = nc.vector
                n = [0]

                def then(ins):
                    ins.then_inc(s_r, 1)
                    n[0] += 1
                    dve.wait_ge(s_r, n[0])
                dve.wait_ge(s_io, 1)
                for t in range(TT):
                    for half in range(2):
                        o = slice(8 * half, 8 * half + 8)
                        for g in range(2 * PH):
                            last = v.max(top[:, g, o], scores[:, t, g, :])
                        then(last)
                        for g in range(2 * PH):
                            last = v.max_index(topi[:, g, o].bitcast(U32), top[:, g, o], scores[:, t, g, :])
                        then(last)
                        if half == 0:
                            for g in range(2 * PH):
                                last = v.match_replace(scores[:, t, g, :], top[:, g, o], scores[:, t, g, :], -3.0e38)
                            then(last)
                    pair_ = top.rearrange("p (h q) i -> p h q i", q=2)
                    then(v.tensor_tensor(cand.rearrange("p h (i j) -> p h i j", i=TOPK),
                                         bc(pair_[:, :, 0, :], 3, [P, PH, TOPK, TOPK]),
                                         bc(pair_[:, :, 1, :], 2, [P, PH, TOPK, TOPK]), ALU.add))
                    pu = pos.bitcast(U32)
                    for half in range(2):
                        for h in range(PH):
                            last = v.max(fsr[:, h, 8 * half:8 * half + 8], cand[:, h, :])
                        then(last)
                        for h in range(PH):
                            last = v.max_index(pu[:, 0, h * TOPK + 8 * half:h * TOPK + 8 * half + 8],
                                               fsr[:, h, 8 * half:8 * half + 8], cand[:, h, :])
                        then(last)
                        if half == 0:
                            for h in range(PH):
                                last = v.match_replace(cand[:, h, :], fsr[:, h, 0:8], cand[:, h, :], -3.0e38)
                            then(last)
                    gt = view(gate[:, t, :], [PH, TOPK])
                    v.tensor_tensor(gt, fsr, fsr[:, :, 0:1].to_broadcast([P, PH, TOPK]), ALU.subtract).then_inc(s_g, 1)
                    v.tensor_scalar(pu[:, 1, :], pu[:, 0, :], 15, None, ALU.bitwise_and)
                    then(v.tensor_scalar(pu[:, 0, :], pu[:, 0, :], 4, None, ALU.logical_shift_right))
                    v.tensor_copy(pos, pu)
                    then(v.tensor_copy(topi, topi.bitcast(U32)))
                    ti = topi.rearrange("p (h q) i -> p h q i", q=2)
                    for q in range(2):
                        then(v.tensor_tensor(hot, bc(pos[:, q, :], 2, [P, HK, TOPK]), bc(iota16, 1, [P, HK, TOPK]),
                                             ALU.is_equal))
                        hk = hot.rearrange("p (h k) i -> p h k i", h=PH)
                        then(v.tensor_tensor(hk, hk, bc(ti[:, :, q, :], 2, [P, PH, TOPK, TOPK]), ALU.mult))
                        then(v.tensor_reduce(pos[:, q, :], hot, AX, ALU.add))
                    v.scalar_tensor_tensor(idx[:, t, :], pos[:, 0, :], float(KEYS), pos[:, 1, :], ALU.mult, ALU.add)\
                     .then_inc(s_idx, 1)
                    dve.wait_ge(s_idx, t + 1)
                    dve.wait_ge(s_e, t + 1)
                    then(v.tensor_reduce(gsum, gt, AX, ALU.add))
                    then(v.reciprocal(gsum, gsum))
                    then(v.tensor_tensor(gt, gt, bc(gsum, 2, [P, PH, TOPK]), ALU.mult))
                for q in range(4):
                    t = q % 2
                    if q == 2:
                        dve.wait_ge(s_gl, TT)
                        then(v.tensor_tensor(actv, actv, gate, ALU.mult))
                    with dve.Fori(0, HB) as i:
                        at = bass.ds(i * GB, GB)
                        if q < 2:
                            for r in range(GB):
                                dve.wait_ge(s_row[r], i * 16 + 16 * (q * HB + 1))
                                v.tensor_tensor_reduce(out=rows_[r], in0=rows_[r], in1=nat[:, t, :], scale=1.0,
                                                       scalar=0.0, op0=ALU.mult, op1=ALU.add,
                                                       accum_out=dots[:, r:r + 1]).then_inc(s_free, 1)
                            dve.wait_ge(s_free, i * GB + (q * HK + GB))
                            v.tensor_copy(actv[:, t, at], dots).then_inc(s_dv, 1)
                            dve.wait_ge(s_dv, i + (q * HB + 1))
                        else:
                            for r in range(GB):
                                dve.wait_ge(s_row[r], i * 16 + 16 * (q * HB + 1))
                                dve.wait_ge(s_free, i * GB + (q * HK + r))
                                v.scalar_tensor_tensor(res[:, t, :], rows_[r], actv[:, t, bass.ds(i * GB + r, 1)], res[:, t, :],
                                                       ALU.mult, ALU.add).then_inc(s_free, 1)
                    DV[q] = (q + 1) * HB
                dve.wait_ge(s_mb, 32)
                v.tensor_tensor(mod_sum[0:MR, 0, :], mod_sum[0:MR, 0, :], mod_sum[0:MR, 1, :],
                                ALU.add).then_inc(s_mba, 1)

            @block.gpsimd
            def _(g):
                def half(q, i, p, first):
                    t = q % 2
                    src = (a["peer_u"] if q < 2 else a["peer_v"])[0]
                    st = stage[:, p * GB:(p + 1) * GB]
                    g.tensor_copy(st, idx[:, t, bass.ds(i * (2 * GB) + p * GB, GB)]).then_inc(s_stage, 1)
                    for r in range(GB):
                        if r == 0:
                            g.wait_ge(s_stage, i * 2 + (q * HB + p + 1))
                        if not first:
                            g.wait_ge(s_free, i * (2 * GB) + (q * HK + p * GB + r + 1 - GB))
                        g.sem_inc(s_turn, 1)
                        g.indirect_dma_start(rows_[r], None, src, bass.IndirectOffsetOnAxis(st[:, r:r + 1], 0))\
                         .then_inc(s_row[r], 16)

                g.wait_ge(s_idx, TT)
                for q in range(4):
                    if q == 0:
                        half(0, 0, 0, True)
                        half(0, 0, 1, False)
                    with g.Fori(int(q == 0), HB // 2) as i:
                        half(q, i, 0, False)
                        half(q, i, 1, False)

            @block.sync
            def _(sp):
                stream(sp, ADA_A)
                for p in range(2):
                    sp.wait_ge(s_mout[p], 16 * MODA // 2)
                mod_rows, bias_rows = [x[0:MODA * NB].rearrange("(r c) -> r c", c=P) for x in (mod, a["b_ada_2"][0])]
                sp.dma_start(mod_sum[0:MR, 0, :], mod_rows).then_inc(s_mb, 16)
                sp.dma_start(mod_sum[0:MR, 1, :], bias_rows).then_inc(s_mb, 16)
                sp.wait_ge(s_mba, 1)
                sp.dma_start(mod_rows, mod_sum[0:MR, 0, :]).then_inc(s_mb, 16)
                sp.wait_ge(s_mb, 48)

            @block.tensor
            def _(pe):
                whole_linear(pe, ADA_A, s_mtk, lambda k: ccol[:, k:k + 1])

            @block.scalar
            def _(act):
                for t in range(TT):
                    act.wait_ge(s_g, t + 1)
                    nc.scalar.activation(gate[:, t, :], gate[:, t, :], ACT.Exp).then_inc(s_e, 1)
                act.wait_ge(s_idx, TT)

                def pair(i, first):
                    for p in range(2):
                        act.wait_ge(slabs_used, i * 8 + (g0 + 4 * p + 4))
                        if not first:
                            act.wait_ge(s_mout[p], i * 16)
                        nc.scalar.copy(modrow[:, p, :], ps[p][0:1, :]).then_inc(s_mtk, 1)
                        act.wait_ge(s_mtk, i * 2 + (p + 1))
                        act.dma_start(mod[bass.ds(i * (2 * NB) + p * NB, NB)].rearrange("(o n) -> o n", o=1),
                                      modrow[:, p, :]).then_inc(s_mout[p], 16)
                pair(0, True)
                with act.Fori(1, MODA // 2) as i:
                    pair(i, False)
                for t in range(TT):
                    act.wait_ge(s_dv, DV[t])
                    nc.scalar.activation(actv[:, t, :], actv[:, t, :], ACT.Gelu).then_inc(s_gl, 1)
        if stop <= 8:
            return halt(MIX)

        recycle()
        norm_phase("final1", a["final_g"], dst=res, transposed=False)
        mods = [mod[i * D:(i + 1) * D] for i in range(NMOD)]
        norm_phase("norm1b", a["norm1_gain_2"][0], mods[1], mods[0])
        if stop <= 9:
            return halt(MIX)

        DKH = 2 * SBH + 2 * DLH
        place = Places(pool)
        sb_v, dil_v = place.take(TT, SBW), place.take(TT, DLW)
        gla_v, gla_r = place.take(TT, GV), place.take(TT, GV)
        oT_at = place.at
        sb_qk, dil_qk, gla_qk = place.take(TT, 2 * SBW), place.take(TT, 2 * DLW), place.take(TT, 2 * GK)
        oTh = view(place_at("mixed_high", KD * T, F32R, pool_at + oT_at)[0][:, :], [KD, T])
        oTl = view(place_at("mixed_low", KD * T, F32R, pool_at + oT_at + KD * T)[0][:, :], [KD, T])
        assert place.at <= oT_at + 2 * KD * T <= POOL - KD * T
        T2_at = POOL - KD * T
        T2 = Places(pool, T2_at)
        T1 = Places(nat_)
        sbT, gkT = T1.take(2 * SBH, T), T1.take(GH, T)
        dilT, gqT = T2.take(2 * DLH, T), T2.take(GH, T)
        keep = Places(small, 64)
        a_nat = keep.take(TT, GR)
        qk_ss = keep.take(TT, DKH)
        gains = keep.take(4)
        segments = [(sb_qk, 2 * SBW), (sb_v, SBW), (dil_qk, 2 * DLW), (dil_v, DLW), (gla_qk, 2 * GK), (gla_v, GV),
                    (gla_r, GV)]

        def pieces(b, t):
            at, out_, lo, hi = 0, [], b * NB, (b + 1) * NB
            for seg, w in segments:
                x, y = max(lo, at), min(hi, at + w)
                if x < y:
                    out_.append((seg[:, t, x - at:y - at], x - lo, y - x))
                at += w
            return out_

        s5_, g0 = SECTIONS[MIX], first_slab[MIX]
        wa = view(nat_[:, 0:KD * GR], [KD, GR])
        s_wa, s_ap, s_ac = sem("rank_columns_landed"), sem("rank_products"), sem("rank_copied")
        s_pt = [sem("mix_taken_act"), sem("mix_taken_dve")]
        with nc.Block() as block:
            @block.sync
            def _(sp):
                sp.dma_start(wa, w_in2[:, C_A:C_G].rearrange("(k p) n -> p k n", p=P)).then_inc(s_wa, 16)
                for i, nme in enumerate(("sb_q_gain_2", "sb_k_gain_2", "dil_q_gain_2", "dil_k_gain_2")):
                    sp.dma_start(gains[:, i:i + 1], a[nme][0].rearrange("(p o) -> p o", o=1)).then_inc(s_wa, 16)
                stream(sp, MIX)
                sp.wait_ge(s_wa, 80)

            @block.tensor
            def _(pe):
                linear(pe, MIX, s_pt)
                b = s5_.blocks - 1
                for t in range(TT):
                    pe.wait_ge(s_pt[t], b - 1)
                for j in range(4):
                    slab(pe, g0 + 4 * b + j, [(ps[t][:, :], t) for t in range(TT)], left, 4 * j, j == 0, j == 3)
                pe.wait_ge(s_wa, 80)
                for t in range(TT):
                    for k in range(KD):
                        for h in range(2):
                            last = nc.tensor.matmul(ps[4][:, t * GR:(t + 1) * GR], left(k, t)[h].bitcast(F32),
                                                    wa[:, k, :], start=k + h == 0, stop=k + h == KD)
                last.then_inc(s_ap, 1)

            def evac(eng, copy, t):
                def one(b):
                    eng.wait_ge(slabs_used, g0 + 4 * (b + 1))
                    for dst, c0_, w in pieces(b, t):
                        last = copy(dst, ps[(b % 2) * TT + t][:, c0_:c0_ + w])
                    last.then_inc(s_pt[t], 1)
                return one

            @block.scalar
            def _(act):
                high_blocks(act, MIX, evac(act, nc.scalar.copy, 0))

            @block.vector
            def _(dve):
                low_blocks(dve, MIX, evac(dve, nc.vector.tensor_copy, 1))
                dve.wait_ge(s_ap, 1)
                nc.vector.tensor_copy(a_nat, view(ps[4][:, 0:TT * GR], [TT, GR]))

        MODB = SECTIONS[ADA_B].blocks
        scratch = Places(parts_, 2 * PARTS * SLAB - KD * 2 * MODB)
        spread = scratch.take(KD, 2 * MODB)
        ccol_again = stat[:, 0:KD]
        mod_b = Places(parts_, 2 * PARTS * SLAB - KD * 2 * MODB - NB).take(NB)
        s_sz, s_cl2, s_cs2, s_mbl, s_mbs = (sem("spread_zeroed"), sem("condition_landed_again"), sem("condition_spread"),
                                            sem("modulation_bias_landed"), sem("modulation_rest"))
        g0_b, modulated = first_slab[ADA_B], [0]

        def modulate(pe, n):
            for m in range(modulated[0], modulated[0] + n):
                slot = (g0_b + m) % SLOTS
                if m == 0:
                    pe.wait_ge(s_cs2, 1)
                pe.wait_ge(landed[slot], reach[g0_b + m])
                j = m // 4
                for k in range(KS):
                    last = nc.tensor.matmul(ps[7][0:MODB, :], spread[:, m % 4 * KS + k, MODB - 1 - j:2 * MODB - 1 - j],
                                            ring[:, slot, k, :], start=m + k == 0,
                                            stop=(m + 1, k + 1) == (4 * MODB, KS))
                last.then_inc(slabs_used, 1)
            modulated[0] += n

        BESIDE = {"heads": (3, 1), "stick": (5, 3, 0), "dilated": (5, 2, 0), "gla": (5, 5, 3, 4, 3, 4, 3, 4, 3, 5, 6)}
        assert sum(sum(x) for x in BESIDE.values()) == 4 * MODB
        beside_at, at = {}, g0_b
        for stage_ in BESIDE:
            beside_at[stage_] = (at, at + sum(BESIDE[stage_]))
            at += sum(BESIDE[stage_])

        s_hs, s_hr, s_hn = sem("head_step"), sem("head_root"), sem("heads_normed")
        s_hT, s_hc = sem("heads_transposed"), [sem("heads_copied_act"), sem("heads_copied_dve")]
        sq = view(parts_[:, 0:2 * SBW], [2 * SBH, HD])
        hmarks = {}
        heads = [(sb_qk, h, sbT, h, h // SBH) for h in range(2 * SBH)]
        heads += [(dil_qk, h, dilT, h, 2 + h // DLH) for h in range(2 * DLH)]
        heads += [(gla_qk, h, gqT if h < GH else gkT, h % GH, None) for h in range(2 * GH)]
        with nc.Block() as block:
            @block.sync
            def _(sp):
                sp.dma_start(ccol_again, a["c_2"][0].rearrange("(k p) -> p k", p=P), allow_slow_non_contiguous=True)\
                  .then_inc(s_cl2, 16)
                stream_on(sp, *beside_at["heads"])

            @block.gpsimd
            def _(g):
                g.memset(spread, 0.0).then_inc(s_sz, 1)

            @block.vector
            def _(dve):
                v = nc.vector
                n = [0]

                def then(ins, mark=None):
                    ins.then_inc(s_hs, 1)
                    n[0] += 1
                    hmarks[mark] = n[0]
                    dve.wait_ge(s_hs, n[0])
                for t in range(TT):
                    for i, qk in enumerate((sb_qk, dil_qk)):
                        hv = view(qk[:, t, :], [2 * SBH, HD])
                        then(v.tensor_tensor(sq, hv, hv, ALU.mult))
                        then(v.tensor_reduce(qk_ss[:, t, i * 2 * SBH:(i + 1) * 2 * SBH], sq, AX, ALU.add))
                then(v.tensor_scalar(qk_ss, qk_ss, 1.0 / HD, EPS, ALU.mult, ALU.add), "ss")
                dve.wait_ge(s_hr, 1)
                then(v.reciprocal(qk_ss, qk_ss))
                for i, qk in enumerate((sb_qk, dil_qk)):
                    for t in range(TT):
                        hv = view(qk[:, t, :], [2 * SBH, HD])
                        last = v.tensor_tensor(hv, hv, bc(qk_ss[:, t, i * 2 * SBH:(i + 1) * 2 * SBH], 2,
                                                          [P, 2 * SBH, HD]), ALU.mult)
                    last.then_inc(s_hn, 1)
                for m in range(1, len(heads) // 2, 2):
                    dve.wait_ge(s_hT, m + 1)
                    for j in range(2):
                        _, _, dst, hh, gcol = heads[2 * m + j]
                        src = ps[m % 4][:, j * T:(j + 1) * T]
                        if gcol is None:
                            last = v.tensor_scalar(dst[:, hh, :], src, P ** -0.5 if dst is gqT else 1.0, None, ALU.mult)
                        else:
                            last = v.tensor_scalar(dst[:, hh, :], src, gains[:, gcol:gcol + 1], None, ALU.mult)
                    last.then_inc(s_hc[1], 1)

            @block.scalar
            def _(act):
                act.wait_ge(s_sz, 1)
                act.wait_ge(s_cl2, 16)
                nc.scalar.activation(spread[:, :, MODB - 1], ccol_again, ACT.Silu).then_inc(s_cs2, 1)
                act.wait_ge(s_hs, hmarks["ss"])
                nc.scalar.activation(qk_ss, qk_ss, ACT.Sqrt).then_inc(s_hr, 1)
                for m in range(0, len(heads) // 2, 2):
                    act.wait_ge(s_hT, m + 1)
                    for j in range(2):
                        _, _, dst, hh, gcol = heads[2 * m + j]
                        src = ps[m % 4][:, j * T:(j + 1) * T]
                        if gcol is None:
                            last = nc.scalar.mul(dst[:, hh, :], src, P ** -0.5 if dst is gqT else 1.0)
                        else:
                            last = nc.scalar.mul(dst[:, hh, :], src, gains[:, gcol:gcol + 1])
                    last.then_inc(s_hc[0], 1)

            @block.tensor
            def _(pe):
                modulate(pe, BESIDE["heads"][0])
                for m in range(len(heads) // 2):
                    src = heads[2 * m][0]
                    pe.wait_ge(s_hn, 1 if src is sb_qk else 2)
                    if m >= 4:
                        pe.wait_ge(s_hc[m % 2], (m - 4) // 2 + 1)
                    for j in range(4):
                        src, h, *_ = heads[2 * m + j // 2]
                        t = j % 2
                        last = nc.tensor.transpose(ps[m % 4][:, j * P:(j + 1) * P], src[:, t, h * P:(h + 1) * P],
                                                   ident[:, :])
                    last.then_inc(s_hT, 1)
                modulate(pe, BESIDE["heads"][1])
        if stop <= 10:
            return halt(ADA_B, modulated[0])

        TC3 = 3 * P
        diag = [slice(0, P), slice(2 * P, TC3)]
        work = Places(parts_)
        z, lb, lr = work.take(SBH, TC3), work.take(SBH, TC3), work.take(SBH, TC3)
        s_mk, s_sp, s_ss, s_sf, s_so, s_oc = (sem("stick_masks"), sem("stick_products"), sem("stick_step"),
                                              sem("stick_functions"), sem("stick_outputs"), sem("stick_copied"))
        sm = {}
        with nc.Block() as block:
            @block.sync
            def _(sp):
                stream_on(sp, *beside_at["stick"])

            @block.gpsimd
            def _(g):
                g.memset(causal[:, :], 1.0).then_inc(s_mk, 1)
                g.memset(upto[:, :], 1.0).then_inc(s_mk, 1)
                g.wait_ge(s_mk, 2)
                g.affine_select(out=causal[:, :], in_=causal[:, :], compare_op=ALU.is_gt, fill=0.0, base=0,
                                pattern=[[1, P]], channel_multiplier=-1).then_inc(s_mk, 1)
                g.affine_select(out=upto[:, :], in_=upto[:, :], compare_op=ALU.is_gt, fill=0.0, base=0,
                                pattern=[[-1, P]], channel_multiplier=1).then_inc(s_mk, 1)

            @block.vector
            def _(dve):
                v = nc.vector
                n = [0]

                def then(ins, mark=None):
                    ins.then_inc(s_ss, 1)
                    n[0] += 1
                    sm[mark] = n[0]
                    dve.wait_ge(s_ss, n[0])
                dve.wait_ge(s_mk, 4)
                for h in range(SBH):
                    dve.wait_ge(s_sp, h + 1)
                    last = v.tensor_scalar(z[:, h, :], ps[h][:, 0:TC3], HD ** -0.5, None, ALU.mult)
                then(last)
                then(v.scalar_tensor_tensor(lr, z, -1.0, z, ALU.mult, ALU.max), "abs")
                dve.wait_ge(s_sf, 2)
                then(v.scalar_tensor_tensor(lb, z, 0.0, lr, ALU.min, ALU.subtract))
                then(v.tensor_scalar(z, z, -1.0, 0.0, ALU.mult, ALU.min))
                then(v.tensor_tensor(lr, z, lr, ALU.subtract))
                for d in diag:
                    last = v.tensor_tensor(lr[:, :, d], lr[:, :, d], bc(causal[:, :], 1, [P, SBH, P]), ALU.mult)
                then(last, "rest")
                for h in range(SBH):
                    dve.wait_ge(s_sp, SBH + h + 1)
                    last = v.tensor_tensor(lb[:, h, :], ps[h][:, 0:TC3], lb[:, h, :], ALU.add)
                then(last, "logw")
                dve.wait_ge(s_sf, 3)
                for d in diag:
                    last = v.tensor_tensor(lb[:, :, d], lb[:, :, d], bc(causal[:, :], 1, [P, SBH, P]), ALU.mult)
                then(last, "w")
                for h in range(SBH):
                    dve.wait_ge(s_oc, h + 1)
                    v.tensor_tensor(oTl[:, h, :], ps[h][:, 0:T], oTh[:, h, :].bitcast(F32), ALU.subtract)

            @block.scalar
            def _(act):
                act.wait_ge(s_ss, sm["abs"])
                nc.scalar.activation(lr, lr, ACT.Exp, scale=-1.0).then_inc(s_sf, 1)
                act.wait_ge(s_sf, 1)
                nc.scalar.activation(lr, lr, ACT.Ln, bias=1.0).then_inc(s_sf, 1)
                act.wait_ge(s_ss, sm["logw"])
                nc.scalar.activation(lb, lb, ACT.Exp).then_inc(s_sf, 1)
                for h in range(SBH):
                    act.wait_ge(s_so, h + 1)
                    nc.scalar.copy(oTh[:, h, :], ps[h][:, 0:T]).then_inc(s_oc, 1)

            @block.tensor
            def _(pe):
                for h in range(SBH):
                    k = SBH + h
                    nc.tensor.matmul(ps[h][:, 0:T], sbT[:, k, 0:P], sbT[:, h, :], start=True, stop=True)
                    nc.tensor.matmul(ps[h][:, T:TC3], sbT[:, k, P:T], sbT[:, h, P:T], start=True, stop=True)\
                      .then_inc(s_sp, 1)
                modulate(pe, BESIDE["stick"][0])
                pe.wait_ge(s_ss, sm["rest"])
                for h in range(SBH):
                    r = lr[:, h, :]
                    nc.tensor.matmul(ps[h][:, 0:P], upto[:, :], r[:, 0:P], start=True, stop=True)
                    nc.tensor.matmul(ps[h][:, P:T], upto[:, :], r[:, P:T], start=True, stop=False)
                    nc.tensor.matmul(ps[h][:, P:T], ones[:, :], r[:, T:TC3], start=False, stop=True)
                    nc.tensor.matmul(ps[h][:, T:TC3], upto[:, :], r[:, T:TC3], start=True, stop=True).then_inc(s_sp, 1)
                modulate(pe, BESIDE["stick"][1])
                pe.wait_ge(s_ss, sm["w"])
                for h in range(SBH):
                    hd = slice(h * HD, (h + 1) * HD)
                    nc.tensor.matmul(ps[h][:, 0:P], sb_v[:, 0, hd], lb[:, h, 0:P], start=True, stop=True)
                    nc.tensor.matmul(ps[h][:, P:T], sb_v[:, 0, hd], lb[:, h, P:T], start=True, stop=False)
                    nc.tensor.matmul(ps[h][:, P:T], sb_v[:, 1, hd], lb[:, h, T:TC3], start=False, stop=True)\
                      .then_inc(s_so, 1)
                modulate(pe, BESIDE["stick"][2])

        work = Places(parts_)
        lg, pT = work.take(DLH, TC3), work.take(DLH, TC3)
        dist, dmask, dtmp = work.take(TC3), work.take(len(DILG), TC3), work.take(TC3)
        parts = [slice(0, P), slice(P, TC3)]
        dst_ = Places(small, 64 + TT * GR)
        dmax, dneg, dsum, dlse, dfac = [dst_.take(DLH, 2) for _ in range(5)]
        dm, dz = dst_.take(DHG, 2), dst_.take(DHG, 2)
        s_di, s_dp, s_ds, s_df, s_dt, s_do = (sem("dilated_distances"), sem("dilated_scores"), sem("dilated_step"),
                                              sem("dilated_functions"), sem("dilated_transposed"),
                                              sem("dilated_outputs"))
        slopes = [2.0 ** (-8.0 * (i + 1) / DLH) for i in range(DLH)]
        obank = (6, 0)
        dk = {}
        with nc.Block() as block:
            @block.sync
            def _(sp):
                stream_on(sp, *beside_at["dilated"])

            @block.gpsimd
            def _(g):
                di = dist.bitcast(mybir.dt.int32)
                for c, d in enumerate(parts):
                    g.iota(di[:, d], pattern=[[-1, d.stop - d.start]], base=c * P, channel_multiplier=1).then_inc(s_di, 1)

            @block.vector
            def _(dve):
                v = nc.vector
                n = [0]

                def then(ins, mark=None):
                    ins.then_inc(s_ds, 1)
                    n[0] += 1
                    dk[mark] = n[0]
                    dve.wait_ge(s_ds, n[0])
                I32 = mybir.dt.int32
                dve.wait_ge(s_di, 2)
                for g, (window, dil) in enumerate(DILG):
                    dmi = dmask[:, g, :].bitcast(I32)
                    last = v.tensor_scalar(dmi, dist.bitcast(I32), dil - 1, None, ALU.bitwise_and)
                then(last)
                then(v.tensor_copy(dmask, dmask.bitcast(I32)))
                then(v.tensor_copy(dist, dist.bitcast(I32)))
                for g, (window, dil) in enumerate(DILG):
                    m_ = dmask[:, g, :]
                    then(v.tensor_scalar(m_, m_, 0.0, None, ALU.is_equal))
                    then(v.scalar_tensor_tensor(m_, dist, 0.0, m_, ALU.is_ge, ALU.mult))
                    then(v.scalar_tensor_tensor(m_, dist, float(window), m_, ALU.is_le, ALU.mult))
                    then(v.tensor_scalar(m_, m_, 1.0, -NEG, ALU.subtract, ALU.mult))
                for h in range(DLH):
                    then(v.scalar_tensor_tensor(dtmp, dist, -slopes[h], dmask[:, h // DHG, :], ALU.mult, ALU.add))
                    dve.wait_ge(s_dp, h + 1)
                    then(v.scalar_tensor_tensor(lg[:, h, :], ps[h][:, 0:TC3], HD ** -0.5, dtmp, ALU.mult, ALU.add))
                for c, d in enumerate(parts):
                    last = v.tensor_reduce(dmax[:, :, c], lg[:, :, d], AX, ALU.max)
                then(last)
                then(v.tensor_scalar(dneg, dmax, -1.0, None, ALU.mult), "max")
                dve.wait_ge(s_df, 2 * DLH + 1)
                then(v.tensor_tensor(dlse, dlse, dmax, ALU.add))
                g3 = (lambda x, g: x[:, g * DHG:(g + 1) * DHG, :])
                then(v.tensor_tensor(dm, g3(dlse, 0), g3(dlse, 1), ALU.max))
                then(v.tensor_tensor(dm, dm, g3(dlse, 2), ALU.max))
                for g in range(len(DILG)):
                    last = v.tensor_tensor(g3(dlse, g), g3(dlse, g), dm, ALU.subtract)
                then(last, "lse")
                dve.wait_ge(s_df, 2 * DLH + 2)
                then(v.tensor_tensor(dz, g3(dlse, 0), g3(dlse, 1), ALU.add))
                then(v.tensor_tensor(dz, dz, g3(dlse, 2), ALU.add))
                for g in range(len(DILG)):
                    last = v.tensor_tensor(g3(dfac, g), g3(dsum, g), dz, ALU.mult)
                then(last)
                then(v.reciprocal(dfac, dfac))
                then(v.tensor_tensor(dfac, dfac, dlse, ALU.mult))
                for c, d in enumerate(parts):
                    w = d.stop - d.start
                    last = v.tensor_tensor(lg[:, :, d], lg[:, :, d], dfac[:, :, c:c + 1].to_broadcast([P, DLH, w]),
                                           ALU.mult)
                then(last, "p")
                for h in range(DLH):
                    dve.wait_ge(s_dt, h + 1)
                    last = v.tensor_copy(pT[:, h, :], ps[h][:, 0:TC3])
                then(last, "pt")
                for j in range(DHG):
                    dve.wait_ge(s_df, 2 * DLH + 3 + j)
                    v.tensor_tensor(oTl[:, SBH + j, :], ps[obank[j]][:, 0:T], oTh[:, SBH + j, :].bitcast(F32),
                                    ALU.subtract)

            @block.scalar
            def _(act):
                act.wait_ge(s_ds, dk["max"])
                for h in range(DLH):
                    for c, d in enumerate(parts):
                        nc.scalar.activation(lg[:, h, d], lg[:, h, d], ACT.Exp, bias=dneg[:, h, c:c + 1],
                                             accum_out=dsum[:, h, c:c + 1]).then_inc(s_df, 1)
                act.wait_ge(s_df, 2 * DLH)
                nc.scalar.activation(dlse, dsum, ACT.Ln).then_inc(s_df, 1)
                act.wait_ge(s_ds, dk["lse"])
                nc.scalar.activation(dlse, dlse, ACT.Exp).then_inc(s_df, 1)
                for j in range(DHG):
                    act.wait_ge(s_do, j + 1)
                    nc.scalar.copy(oTh[:, SBH + j, :], ps[obank[j]][:, 0:T]).then_inc(s_df, 1)

            @block.tensor
            def _(pe):
                for h in range(DLH):
                    k = DLH + h
                    nc.tensor.matmul(ps[h][:, 0:P], dilT[:, h, 0:P], dilT[:, k, 0:P], start=True, stop=True)
                    nc.tensor.matmul(ps[h][:, P:TC3], dilT[:, h, P:T], dilT[:, k, :], start=True, stop=True)\
                      .then_inc(s_dp, 1)
                modulate(pe, BESIDE["dilated"][0])
                pe.wait_ge(s_ds, dk["p"])
                for h in range(DLH):
                    for j in range(3):
                        last = nc.tensor.transpose(ps[h][:, j * P:(j + 1) * P], lg[:, h, j * P:(j + 1) * P], ident[:, :])
                    last.then_inc(s_dt, 1)
                modulate(pe, BESIDE["dilated"][1])
                pe.wait_ge(s_ds, dk["pt"])
                ng = len(DILG)
                for j in range(DHG):
                    for g in range(ng):
                        h = g * DHG + j
                        nc.tensor.matmul(ps[obank[j]][:, 0:P], dil_v[:, 0, h * HD:(h + 1) * HD], pT[:, h, 0:P],
                                         start=g == 0, stop=g == ng - 1)
                    for g in range(ng):
                        h = g * DHG + j
                        nc.tensor.matmul(ps[obank[j]][:, P:T], dil_v[:, 0, h * HD:(h + 1) * HD], pT[:, h, P:T],
                                         start=g == 0, stop=False)
                        last = nc.tensor.matmul(ps[obank[j]][:, P:T], dil_v[:, 1, h * HD:(h + 1) * HD], pT[:, h, T:TC3],
                                                start=False, stop=g == ng - 1)
                    last.then_inc(s_do, 1)
                modulate(pe, BESIDE["dilated"][2])
        if stop <= 11:
            return halt(ADA_B, modulated[0])

        work = Places(parts_)
        la, cum = work.take(TT, GK), work.take(GH, T)
        ee, qe, ke = work.take(GH, T), work.take(GH, T), work.take(GH, T)
        acc = work.take(TT, GH, P)
        off = work.take(GH, P)
        apart, lmask = work.take(P), work.take(P)
        mtmp = view(la.rearrange("p a b -> p (a b)"), [TT, GH, P])
        og_at = Places(parts_, 2 * GH * T)
        og = og_at.take(TT, GV)
        ggain = nat_[:, 0:GDV]
        LV = int(math.log2(T))
        gst = Places(small, 64 + TT * GR)
        gss = gst.take(TT * GH)
        s_gl_, s_gp, s_gs, s_gf, s_gT, s_gT2, s_gc = (sem("gla_landed"), sem("gla_products"), sem("gla_step"),
                                                      sem("gla_functions"), sem("gla_level_products"),
                                                      sem("gla_transposed"), sem("gla_copied"))
        s_gi = sem("gla_iota")
        gm = {}
        a_T = view(nat_[:, GDV:GDV + T], [T])
        ga_w = view(nat_[:, 2 * GDV:2 * GDV + GK], [GK])
        ga_b = view(nat_[:, 2 * GDV + GK:2 * GDV + 2 * GK], [GK])
        with nc.Block() as block:
            @block.sync
            def _(sp):
                sp.dma_start(ga_w[0:GR, :], a["w_gla_a_2"][0]).then_inc(s_gl_, 16)
                sp.dma_start(ga_b, a["b_gla_a_2"][0].partition_broadcast(P)).then_inc(s_gl_, 16)
                sp.dma_start(ggain, a["gla_out_gain_2"][0].partition_broadcast(P)).then_inc(s_gl_, 16)
                bias_rows, mod_rows = [x[MODA * NB:NMOD * D].rearrange("(r c) -> r c", c=NB)
                                       for x in (a["b_ada_2"][0], mod)]
                sp.dma_start(mod_b[0:MODB, :], bias_rows).then_inc(s_mbl, 16)
                stream_on(sp, *beside_at["gla"])
                sp.wait_ge(s_mbs, 1)
                sp.dma_start(mod_rows, mod_b[0:MODB, :]).then_inc(s_mbl, 16)
                sp.wait_ge(s_mbl, 32)

            @block.gpsimd
            def _(g):
                g.memset(upto[:, :], 1.0).then_inc(s_gi, 1)
                g.wait_ge(s_gi, 1)
                g.affine_select(out=upto[:, :], in_=upto[:, :], compare_op=ALU.is_ge, fill=0.0, base=0,
                                pattern=[[1, P]], channel_multiplier=-1).then_inc(s_gi, 1)
                I32 = mybir.dt.int32
                g.iota(apart.bitcast(I32), pattern=[[1, P]], base=0, channel_multiplier=0).then_inc(s_gi, 1)
                g.iota(lmask.bitcast(I32), pattern=[[0, P]], base=0, channel_multiplier=1).then_inc(s_gi, 1)

            @block.vector
            def _(dve):
                v = nc.vector
                n = [0]

                def then(ins, mark=None):
                    ins.then_inc(s_gs, 1)
                    n[0] += 1
                    gm[mark] = n[0]
                    dve.wait_ge(s_gs, n[0])
                I32 = mybir.dt.int32
                dve.wait_ge(s_gi, 4)
                then(v.tensor_tensor(apart.bitcast(I32), apart.bitcast(I32), lmask.bitcast(I32), ALU.bitwise_xor))
                then(v.tensor_copy(apart, apart.bitcast(I32)))
                then(v.scalar_tensor_tensor(apart, apart, 1.0, causal[:, :], ALU.add, ALU.mult))
                then(v.tensor_scalar(apart, apart, 1.0, None, ALU.subtract))
                dve.wait_ge(s_gp, 1)
                then(v.tensor_copy(a_T[0:GR, :], ps[0][0:GR, 0:T]), "aT")
                dve.wait_ge(s_gl_, 48)
                dve.wait_ge(s_gp, 2)
                for t in range(TT):
                    last = v.tensor_tensor(la[:, t, :], ps[1 + t][:, :], ga_b, ALU.add)
                then(last)
                e2 = view(ee.rearrange("p a b -> p (a b)"), [TT, GK])
                then(v.scalar_tensor_tensor(e2, la, -1.0, la, ALU.mult, ALU.max), "abs")
                dve.wait_ge(s_gf, 2)
                then(v.scalar_tensor_tensor(la, la, 0.0, e2, ALU.min, ALU.subtract))
                then(v.tensor_scalar(la, la, 1.0 / TAU, None, ALU.mult), "la")
                dve.wait_ge(s_gp, 3)
                for h in range(GH):
                    last = v.tensor_copy(cum[:, h, :], ps[3 + h // 2][:, (h % 2) * T:(h % 2 + 1) * T])
                then(last, "cum")
                for lv in range(LV + 1):
                    B = 1 << lv
                    if lv == 0:
                        dve.wait_ge(s_gT, 1)
                        for t in range(TT):
                            last = v.tensor_tensor(acc[:, t], view(ps[6 * 0 + t][:, :], [GH, P]),
                                                   bc(ident[:, :], 1, [P, GH, P]), ALU.mult)
                        then(last, "level0")
                        continue
                    cb = cum.rearrange("p h (n b) -> p (h n) b", b=B)
                    eb = ee.rearrange("p h (n b) -> p (h n) b", b=B)
                    then(v.tensor_tensor(eb, cb, cb[:, :, B // 2 - 1:B // 2].to_broadcast([P, GH * T // B, B]),
                                         ALU.subtract))
                    then(v.scalar_tensor_tensor(ee, ee, -1.0, ee, ALU.mult, ALU.min), f"diff{lv}")
                    dve.wait_ge(s_gf, 2 + lv)
                    v.tensor_tensor(qe, gqT, ee, ALU.mult)
                    then(v.tensor_tensor(ke, gkT, ee, ALU.mult), f"qk{lv}")
                    if lv < LV:
                        then(v.tensor_scalar(lmask, apart, float(B // 2), None, ALU.is_ge))
                        then(v.scalar_tensor_tensor(lmask, apart, float(B), lmask, ALU.is_lt, ALU.mult))
                        dve.wait_ge(s_gT, lv + 1)
                        for t in range(TT):
                            last = v.tensor_tensor(mtmp[:, t], view(ps[2 * (lv % 2) + t][:, :], [GH, P]),
                                                   bc(lmask, 1, [P, GH, P]), ALU.mult)
                        then(last)
                        then(v.tensor_tensor(acc, acc, mtmp, ALU.add), f"level{lv}")
                    else:
                        dve.wait_ge(s_gT, lv + 1)
                        then(v.tensor_copy(off, view(ps[2 * (lv % 2)][:, :], [GH, P])), "off")
                dve.wait_ge(s_gp, 4)
                for t in range(TT):
                    for j in range(2):
                        last = v.tensor_copy(og[:, t, j * NB:(j + 1) * NB], ps[2 * t + j][:, :])
                then(last, "og")
                ov = og.rearrange("p t (h e) -> p (t h) e", h=GH)
                sqv = view(cum.rearrange("p a b -> p (a b)"), [GH, GDV])
                for t in range(TT):
                    then(v.tensor_tensor(sqv, ov[:, t * GH:(t + 1) * GH, :], ov[:, t * GH:(t + 1) * GH, :], ALU.mult))
                    then(v.tensor_reduce(gss[:, t * GH:(t + 1) * GH], sqv, AX, ALU.add))
                then(v.tensor_scalar(gss, gss, 1.0 / GDV, EPS, ALU.mult, ALU.add), "ss")
                dve.wait_ge(s_gf, 2 + LV + 1)
                then(v.reciprocal(gss, gss))
                then(v.tensor_tensor(ov, ov, bc(gss, 2, [P, TT * GH, GDV]), ALU.mult))
                then(v.tensor_tensor(ov, ov, bc(ggain, 1, [P, TT * GH, GDV]), ALU.mult))
                dve.wait_ge(s_gf, 2 + LV + 2)
                then(v.tensor_tensor(og, og, gla_r, ALU.mult), "out")
                dve.wait_ge(s_mbl, 16)
                dve.wait_ge(slabs_used, first_slab[ADA_B + 1])
                v.tensor_tensor(mod_b[0:MODB, :], mod_b[0:MODB, :], ps[7][0:MODB, :], ALU.add).then_inc(s_mbs, 1)
                for m in range(4):
                    dve.wait_ge(s_gc, m + 1)
                    c = slice(SBH + DHG + 2 * m, SBH + DHG + 2 * m + 2)
                    v.tensor_tensor(oTl[:, c, :].rearrange("p k t -> p (k t)"), ps[m][:, :],
                                    oTh[:, c, :].rearrange("p k t -> p (k t)").bitcast(F32), ALU.subtract)

            @block.scalar
            def _(act):
                e2 = ee
                act.wait_ge(s_gs, gm["abs"])
                nc.scalar.activation(e2, e2, ACT.Exp, scale=-1.0).then_inc(s_gf, 1)
                act.wait_ge(s_gf, 1)
                nc.scalar.activation(e2, e2, ACT.Ln, bias=1.0).then_inc(s_gf, 1)
                for lv in range(1, LV + 1):
                    act.wait_ge(s_gs, gm[f"diff{lv}"])
                    nc.scalar.activation(ee, ee, ACT.Exp).then_inc(s_gf, 1)
                act.wait_ge(s_gs, gm["ss"])
                nc.scalar.activation(gss, gss, ACT.Sqrt).then_inc(s_gf, 1)
                nc.scalar.activation(gla_r, gla_r, ACT.Silu).then_inc(s_gf, 1)
                for m in range(4):
                    act.wait_ge(s_gT2, m + 1)
                    k = SBH + DHG + 2 * m
                    nc.scalar.copy(oTh[:, k:k + 2, :].rearrange("p k t -> p (k t)"), ps[m][:, :]).then_inc(s_gc, 1)

            @block.tensor
            def _(pe):
                for t in range(TT):
                    last = nc.tensor.transpose(ps[0][0:GR, t * P:(t + 1) * P], a_nat[:, t, :], ident[:, :])
                last.then_inc(s_gp, 1)
                modulate(pe, BESIDE["gla"][0])
                pe.wait_ge(s_gs, gm["aT"])
                pe.wait_ge(s_gl_, 48)
                for t in range(TT):
                    last = nc.tensor.matmul(ps[1 + t][:, :], a_T[0:GR, t * P:(t + 1) * P], ga_w[0:GR, :],
                                            start=True, stop=True)
                last.then_inc(s_gp, 1)
                modulate(pe, BESIDE["gla"][1])
                pe.wait_ge(s_gs, gm["la"])
                pe.wait_ge(s_gi, 2)
                for h in range(GH):
                    o, hs = ps[3 + h // 2], slice(h * P, (h + 1) * P)
                    c = (h % 2) * T
                    nc.tensor.matmul(o[:, c:c + P], la[:, 0, hs], upto[:, :], start=True, stop=True)
                    nc.tensor.matmul(o[:, c + P:c + T], la[:, 0, hs], ones[:, :], start=True, stop=False)
                    last = nc.tensor.matmul(o[:, c + P:c + T], la[:, 1, hs], upto[:, :], start=False, stop=True)
                last.then_inc(s_gp, 1)
                pe.wait_ge(s_gs, gm["cum"])
                for lv in range(LV + 1):
                    q, k = (gqT, gkT) if lv == 0 else (qe, ke)
                    if lv:
                        modulate(pe, BESIDE["gla"][1 + lv])
                        pe.wait_ge(s_gs, gm[f"qk{lv}"])
                    for t in range(TT if lv < LV else 1):
                        for h in range(GH):
                            js, is_ = slice(t * P, (t + 1) * P), slice(t * P, (t + 1) * P)
                            if lv == LV:
                                is_ = slice(P, T)
                            last = nc.tensor.matmul(ps[2 * (lv % 2) + t][:, h * P:(h + 1) * P], k[:, h, js], q[:, h, is_],
                                                    start=True, stop=True)
                    last.then_inc(s_gT, 1)
                pe.wait_ge(s_gs, gm["off"])
                for t in range(TT):
                    for h in range(GH):
                        o = ps[2 * t + h // 2][:, (h % 2) * GDV:(h % 2 + 1) * GDV]
                        last = nc.tensor.matmul(o, acc[:, t, h, :], gla_v[:, t, h * GDV:(h + 1) * GDV],
                                                start=True, stop=t == 0)
                        if t:
                            last = nc.tensor.matmul(o, off[:, h, :], gla_v[:, 0, h * GDV:(h + 1) * GDV],
                                                    start=False, stop=True)
                last.then_inc(s_gp, 1)
                modulate(pe, BESIDE["gla"][LV + 2])
                pe.wait_ge(s_gs, gm["out"])
                for m in range(4):
                    for j in range(4):
                        k, t = 2 * m + j // 2, j % 2
                        last = nc.tensor.transpose(ps[m][:, j * P:(j + 1) * P], og[:, t, k * P:(k + 1) * P], ident[:, :])
                    last.then_inc(s_gT2, 1)
        if stop <= 12:
            return halt(GATES)

        y = nat
        work = Places(pool, T2_at)
        sg = work.take(3, TT, NB)
        ytmp = work.take(TT, NB)
        g0 = first_slab[GATES]
        s_gd, s_ga = sem("gates_done"), sem("gated_steps")
        STEPS, USED = 5, (1, 2, 4)
        branch_bank = (4, 6, 4)
        with nc.Block() as block:
            @block.sync
            def _(sp):
                stream(sp, GATES)

            @block.tensor
            def _(pe):
                for nb in range(OB):
                    for i in range(3):
                        m = 3 * nb + i
                        if m >= 2:
                            pe.wait_ge(s_gd, m - 1)
                        for j in range(4):
                            slab(pe, g0 + 16 * nb + 4 * i + j, [(ps[(m % 2) * TT + t][:, :], t) for t in range(TT)],
                                 left, 4 * j, j == 0, j == 3)
                    if nb:
                        pe.wait_ge(s_ga, STEPS * (nb - 1) + USED[2])
                    for j in range(4):
                        g = g0 + 16 * nb + 12 + j
                        pe.wait_ge(low_done, split_index(g) + 1)
                        part = split_index(g) % PARTS
                        for kk in range(KS):
                            i, k = br_chunks[KS * j + kk]
                            if i == 2 and k == 0:
                                pe.wait_ge(s_ga, STEPS * nb + USED[0])
                            for t in range(TT):
                                o, tok = ps[branch_bank[i] + t][:, :], slice(t * P, (t + 1) * P)
                                lh, ll = oTh[:, KS * j + kk, tok], oTl[:, KS * j + kk, tok]
                                nc.tensor.matmul(o, lh, high[:, part, kk, :], start=k == 0, stop=False)
                                nc.tensor.matmul(o, lh, low[:, part, kk, :], start=False, stop=False)
                                last = nc.tensor.matmul(o, ll, high[:, part, kk, :], start=False,
                                                        stop=k == br_rows[i] - 1)
                        last.then_inc(slabs_used, 1)

            @block.gpsimd
            def _(g):
                for m in range(SECTIONS[GATES].n):
                    low_part(g, g0 + m)

            @block.scalar
            def _(act):
                done = 0
                for m in range(3 * OB):
                    nb, i = divmod(m, 3)
                    upto_ = min(16 * nb + 4 * i + 6, SECTIONS[GATES].n)
                    for x in range(done, upto_):
                        high_part(act, g0 + x)
                    done = upto_
                    if nb:
                        act.wait_ge(s_ga, STEPS * (nb - 1) + USED[i])
                    act.wait_ge(slabs_used, g0 + 16 * nb + 4 * i + 4)
                    for t in range(TT):
                        last = nc.scalar.activation(sg[:, i, t, :], ps[(m % 2) * TT + t][:, :], ACT.Sigmoid)
                    last.then_inc(s_gd, 1)
                for x in range(done, SECTIONS[GATES].n):
                    high_part(act, g0 + x)

            @block.vector
            def _(dve):
                v = nc.vector
                n = [0]

                def then(ins):
                    ins.then_inc(s_ga, 1)
                    n[0] += 1
                    dve.wait_ge(s_ga, n[0])
                for nb in range(OB):
                    dst = y[:, :, nb * NB:(nb + 1) * NB]
                    for i in range(3):
                        end = sum(br_rows[:i + 1]) - 1
                        dve.wait_ge(slabs_used, g0 + 16 * nb + 12 + end // KS + 1)
                        dve.wait_ge(s_gd, 3 * nb + i + 1)
                        for t in range(TT):
                            last = v.tensor_tensor((dst if i == 0 else ytmp)[:, t, :], ps[branch_bank[i] + t][:, :],
                                                   sg[:, i, t, :], ALU.mult)
                        then(last)
                        if i:
                            then(v.tensor_tensor(dst, dst, ytmp, ALU.add))
        if stop <= 13:
            return halt(W_OUT2)

        def transposed(name, src):
            s_tr, s_hi = sem(name + "_transposed"), sem(name + "_high")
            with nc.Block() as block:
                @block.tensor
                def _(pe):
                    for n in range(8):
                        for j in range(4):
                            k, t = 2 * n + j // 2, j % 2
                            last = nc.tensor.transpose(ps[n][:, j * P:(j + 1) * P], src[:, t, k * P:(k + 1) * P],
                                                       ident[:, :])
                        last.then_inc(s_tr, 1)

                @block.scalar
                def _(act):
                    for n in range(8):
                        act.wait_ge(s_tr, n + 1)
                        high_left(n, n).then_inc(s_hi, 1)

                @block.vector
                def _(dve):
                    for n in range(8):
                        dve.wait_ge(s_hi, n + 1)
                        low_left(n, n)

        def gated_residual(name, sec, lhs, gate_row_src, place, store=False):
            gate_row, gtmp = place.take(D), place.take(2, TT, NB)
            s_row_, s_gr, s_gr2, s_st = (sem(name + "_gate_landed"), sem(name + "_gated"), sem(name + "_added"),
                                         sem(name + "_stored"))
            s, g0 = SECTIONS[sec], first_slab[sec]
            out_v = out[0].rearrange("(t p) d -> p t d", p=P)
            with nc.Block() as block:
                @block.sync
                def _(sp):
                    sp.dma_start(gate_row, gate_row_src.partition_broadcast(P)).then_inc(s_row_, 16)
                    stream(sp, sec)
                    if store:
                        for b in range(s.blocks):
                            sp.wait_ge(s_gr2, b + 1)
                            c = slice(b * NB, (b + 1) * NB)
                            sp.dma_start(out_v[:, :, c], res[:, :, c]).then_inc(s_st, 16)
                        sp.wait_ge(s_st, 16 * s.blocks)

                @block.tensor
                def _(pe):
                    for b in range(s.blocks):
                        if b >= 2:
                            pe.wait_ge(s_gr, b - 1)
                        for j in range(s.per):
                            slab(pe, g0 + s.per * b + j, [(ps[(b % 2) * TT + t][:, :], t) for t in range(TT)], lhs,
                                 KS * j, j == 0, j == s.per - 1)

                @block.scalar
                def _(act):
                    high_blocks(act, sec, lambda b: None)

                @block.vector
                def _(dve):
                    def add(b):
                        if b == 0:
                            dve.wait_ge(s_row_, 16)
                        c = slice(b * NB, (b + 1) * NB)
                        dve.wait_ge(slabs_used, g0 + s.per * (b + 1))
                        for t in range(TT):
                            last = nc.vector.tensor_tensor(gtmp[:, b % 2, t, :], ps[(b % 2) * TT + t][:, :],
                                                           gate_row[:, c], ALU.mult)
                        last.then_inc(s_gr, 1)
                        dve.wait_ge(s_gr, b + 1)
                        nc.vector.tensor_tensor(res[:, :, c], res[:, :, c], gtmp[:, b % 2], ALU.add).then_inc(s_gr2, 1)
                    low_blocks(dve, sec, add)

        transposed("y", nat)
        gated_residual("mixer", W_OUT2, left, mods[2], Places(pool))
        if stop <= 14:
            return halt(FFN_IN)
        norm_phase("norm2b", a["norm2_gain_2"][0], mods[4], mods[3])

        FC = FF // P
        hTh = view(place_at("hidden_high", FC * T, F32R, pool_at)[0][:, :], [FC, T])
        hTl = view(place_at("hidden_low", FC * T, F32R, pool_at + FC * T)[0][:, :], [FC, T])
        prod_ = view(place_at("hidden_rows", TT * NB, F32, pool_at + 2 * FC * T)[0][:, :], [TT, NB])
        g0 = first_slab[FFN_IN]
        n0 = split_index(g0)
        pairs = SECTIONS[FFN_IN].blocks // 2
        s_fa, s_fu, s_fT = sem("ffn_gates"), sem("ffn_products"), sem("ffn_transposed")
        s_fh, s_fl = sem("ffn_high"), sem("ffn_low")
        with nc.Block() as block:
            @block.sync
            def _(sp):
                stream(sp, FFN_IN)

            @block.tensor
            def _(pe):
                def transposes(i):
                    pe.wait_ge(s_fu, i * 1)
                    for k in range(4):
                        for t in range(TT):
                            last = nc.tensor.transpose(ps[4 + k // 2][:, (k % 2) * T + t * P:(k % 2) * T + (t + 1) * P],
                                                       prod_[:, t, k * P:(k + 1) * P], ident[:, :])
                    last.then_inc(s_fT, 1)

                def pair(i, first, second=False):
                    for p in range(2):
                        for j in range(4):
                            m = 4 * p + j
                            if not first and p == 0 and j == 0:
                                pe.wait_ge(s_fa, i * 1)
                            if not first and p == 0 and j == 2:
                                if not second:
                                    pe.wait_ge(s_fl, i * 1 - 1)
                                transposes(i)
                            pe.wait_ge(low_done, i * 8 + (n0 + m + 1))
                            last = slab_products((n0 + m) % PARTS, [(ps[2 * p + t][:, :], t) for t in range(TT)],
                                                 left, 4 * j, j == 0, j == 3)
                            last.then_inc(slabs_used, 1)
                pair(0, True)
                pair(1, False, True)
                with pe.Fori(2, pairs) as i:
                    pair(i, False)
                pe.wait_ge(s_fl, pairs - 1)
                transposes(pairs)

            @block.scalar
            def _(act):
                def silu(i):
                    act.wait_ge(slabs_used, i * 8 + (g0 + 4))
                    if not isinstance(i, int) or i:
                        act.wait_ge(s_fT, i * 1)
                    for t in range(TT):
                        last = nc.scalar.activation(prod_[:, t, :], ps[t][:, :], ACT.Silu)
                    last.then_inc(s_fa, 1)

                def highs(i):
                    act.wait_ge(s_fT, i + 1)
                    for k in range(2):
                        last = nc.scalar.copy(hTh[:, bass.ds(i * 4 + 2 * k, 2), :], view(ps[4 + k][:, :], [2, T]))
                    last.then_inc(s_fh, 1)

                def pair(i, first):
                    for m in range(8):
                        if m == 6:
                            silu(i)
                        if m == 4 and not first:
                            highs(i - 1)
                        high_part(act, g0 + m, None if isinstance(i, int) else i)
                pair(0, True)
                with act.Fori(1, pairs) as i:
                    pair(i, False)
                highs(pairs - 1)

            @block.vector
            def _(dve):
                def product(i):
                    dve.wait_ge(s_fa, i + 1)
                    dve.wait_ge(slabs_used, i * 8 + (g0 + 8))
                    for t in range(TT):
                        last = nc.vector.tensor_tensor(prod_[:, t, :], prod_[:, t, :], ps[2 + t][:, :], ALU.mult)
                    last.then_inc(s_fu, 1)

                def lows(i):
                    dve.wait_ge(s_fh, i + 1)
                    for k in range(2):
                        c = bass.ds(i * 4 + 2 * k, 2)
                        last = nc.vector.tensor_tensor(hTl[:, c, :], view(ps[4 + k][:, :], [2, T]),
                                                       hTh[:, c, :].bitcast(F32), ALU.subtract)
                    last.then_inc(s_fl, 1)

                def pair(i, first):
                    for m in range(8):
                        if not first and m == 2:
                            product(i - 1)
                        if not first and m == 4:
                            lows(i - 1)
                        low_part(dve, g0 + m, None if isinstance(i, int) else i)
                pair(0, True)
                with dve.Fori(1, pairs) as i:
                    pair(i, False)
                product(pairs - 1)
                lows(pairs - 1)
        if stop <= 15:
            return halt(FFN_OUT)
        gated_residual("ffn", FFN_OUT, lambda k, t: (hTh[:, k, t * P:(t + 1) * P], hTl[:, k, t * P:(t + 1) * P]), mods[5],
                       Places(aTs), store=True)


_INS = ["x", "norm1_g", "w_in", "b_gates", "conv_qk_w", "mlstm_norm_g", "s5_lambda_re", "s5_lambda_im", "s5_log_dt",
        "s5_b_re", "s5_b_im", "s5_c_re", "s5_c_im", "s5_d", "s5_glu_w", "w_out", "norm2_g", "peer_wq", "peer_subkeys",
        "peer_u", "peer_v", "final_g", "c_2", "w_ada_2", "b_ada_2", "norm1_gain_2", "norm2_gain_2", "w_in_2",
        "sb_q_gain_2", "sb_k_gain_2", "dil_q_gain_2", "dil_k_gain_2", "w_gla_a_2", "b_gla_a_2", "gla_out_gain_2",
        "w_br_sb_2", "w_br_dil_2", "w_br_gla_2", "w_out_2", "w_ffn_in_2", "w_ffn_out_2"]


def kernel(**inputs):
    import numpy as _np
    import concourse.bacc as _bacc
    from concourse import mybir as _mybir
    from concourse.bass_utils import run_bass_kernel_spmd as _run

    nc = _bacc.Bacc("TRN2", target_bir_lowering=False, num_devices=1)
    arrays, args = {}, {}
    for name in _INS:
        v = _np.ascontiguousarray(inputs[name])
        arrays[f"in_{name}"] = v
        args[name] = nc.dram_tensor(f"in_{name}", v.shape, _mybir.dt.from_np(v.dtype), kind="ExternalInput").ap()
    x = inputs["x"]
    out = nc.dram_tensor("out", x.shape, _mybir.dt.float32, kind="ExternalOutput").ap()
    build(nc, args, out)
    r = _run(nc, [arrays], core_ids=[0])
    return r.results[0]["out"]
```
